# Optimizing a Trainium2 kernel written in Bass

```python
import math, functools
import jax, jax.numpy as jnp
from jax import lax
import numpy as np

D_MODEL = 1024
BATCH = 1
SEQ = 128
DEPTH = 2
DEC_BATCH = 1
DEC_SEQ = 512
PAST_LEN = 128

GRID_W = 64
Q_BLOCK = 128
ROPE_BASE = 10000.0
NORM_EPS = 1e-6
HA = 4
DA = 64
HB = 4
NOPE = 64
ROPE_B = 32
VB = 128
Q_LORA = 192
KV_LORA = 128
HC = 8
NC = 64
W_LORA = 64
A_LORA = 64
G_LORA = 128
WKV_LN_EPS = 64e-5
WKV_DECAY_SCALE = 0.606531
HD = 8
PD = 64
G_SSM = 2
NS = 64
CHUNK = 128
D_INNER = HD * PD
CONV_CH = D_INNER + 2 * G_SSM * NS
F_FF = 2816
A_COLS = 3 * HA * 2 * DA
B_COLS = Q_LORA + KV_LORA + ROPE_B
C_COLS = 3 * HC * NC + 2 * W_LORA + 2 * A_LORA + G_LORA
D_COLS = D_INNER + CONV_CH + HD
MIX_WIDTH = HA * 2 * DA + HB * VB

kernel_name = 'hybrid_diffusion_trunk_step'

def rmsnorm(x, g, eps=NORM_EPS):
    xf = x.astype(jnp.float32)
    y = xf * lax.rsqrt(jnp.mean(xf * xf, axis=-1, keepdims=True) + eps)
    return (y * g).astype(x.dtype)

def head_layernorm(y, w, b, eps):
    yf = y.astype(jnp.float32)
    mu = jnp.mean(yf, axis=-1, keepdims=True)
    var = jnp.mean(jnp.square(yf - mu), axis=-1, keepdims=True)
    return ((yf - mu) * lax.rsqrt(var + eps) * w + b).astype(y.dtype)

def dwconv3(x, w, b):
    xp = jnp.pad(x, ((0, 0), (1, 1), (0, 0)))
    return xp[:, :-2] * w[0] + xp[:, 1:-1] * w[1] + xp[:, 2:] * w[2] + b

def centred_shift(x):
    xp = jnp.pad(x, ((0, 0), (1, 1), (0, 0)))
    return 0.5 * (xp[:, :-2] + xp[:, 2:])

def axial_rope_tables(length, dim):
    rows = length // GRID_W
    quarter = dim // 4
    inv = ROPE_BASE ** (-jnp.arange(quarter, dtype=jnp.float32) / quarter)
    pos = jnp.arange(rows * GRID_W)
    row = (pos // GRID_W).astype(jnp.float32)
    col = (pos % GRID_W).astype(jnp.float32)
    ang_r = row[:, None] * inv
    ang_c = col[:, None] * inv
    return jnp.cos(ang_r), jnp.sin(ang_r), jnp.cos(ang_c), jnp.sin(ang_c)

def rope_2d(x, tables):
    cr, sr, cc, sc = tables

    def rot(xh, c, s):
        x1, x2 = jnp.split(xh, 2, axis=-1)
        return jnp.concatenate([x1 * c - x2 * s, x1 * s + x2 * c], axis=-1)

    xr, xc = jnp.split(x, 2, axis=-1)
    return jnp.concatenate([rot(xr, cr, sr), rot(xc, cc, sc)], axis=-1).astype(x.dtype)

def attend(q, k, v, scale):
    b, h, lq, dq = q.shape
    nblk = lq // Q_BLOCK
    qb = q.reshape(b, h, nblk, Q_BLOCK, dq).transpose(2, 0, 1, 3, 4)

    def one(qblk):
        s = jnp.einsum('bhqd,bhkd->bhqk', qblk, k).astype(jnp.float32) * scale
        p = jax.nn.softmax(s, axis=-1).astype(v.dtype)
        return jnp.einsum('bhqk,bhkd->bhqd', p, v)

    o = lax.map(one, qb)
    return o.transpose(1, 2, 0, 3, 4).reshape(b, h, lq, v.shape[-1])

def wkv_scan(r, w, kk, a, k, v, S0, reverse):
    f32 = jnp.float32
    tm = lambda t: jnp.moveaxis(t.astype(f32), 1, 0)
    xs = (tm(r), tm(w), tm(-kk), tm(kk * a), tm(k), tm(v))

    def step(S, inp):
        r_t, w_t, a_t, b_t, k_t, v_t = inp
        sa = jnp.einsum('bhvk,bhk->bhv', S, a_t)
        S = S * w_t[:, :, None, :] + sa[..., None] * b_t[:, :, None, :] + v_t[..., None] * k_t[:, :, None, :]
        return S, jnp.einsum('bhvk,bhk->bhv', S, r_t)

    S, ys = lax.scan(step, S0.astype(f32), xs, reverse=reverse)
    return jnp.moveaxis(ys, 0, 1).astype(r.dtype), S

def ssd_scan(x, dt, A, Bm, Cm, S0):
    f32 = jnp.float32
    b, L, H, P = x.shape
    nc = L // CHUNK
    rep = H // Bm.shape[2]
    Bh = jnp.repeat(Bm.astype(f32), rep, axis=2).reshape(b, nc, CHUNK, H, -1)
    Ch = jnp.repeat(Cm.astype(f32), rep, axis=2).reshape(b, nc, CHUNK, H, -1)
    dtf = dt.astype(f32)
    xdt = (x.astype(f32) * dtf[..., None]).reshape(b, nc, CHUNK, H, P)
    acum = jnp.cumsum((dtf * A.astype(f32)).reshape(b, nc, CHUNK, H), axis=2)
    causal = jnp.tril(jnp.ones((CHUNK, CHUNK), dtype=bool))[None, None, :, :, None]
    seg = acum[:, :, :, None, :] - acum[:, :, None, :, :]
    decay_in = jnp.where(causal, jnp.exp(jnp.where(causal, seg, 0.0)), 0.0)
    scores = jnp.einsum('bcihn,bcjhn->bcijh', Ch, Bh) * decay_in
    y_intra = jnp.einsum('bcijh,bcjhp->bcihp', scores, xdt)
    decay_end = jnp.exp(acum[:, :, -1:, :] - acum)
    chunk_states = jnp.einsum('bcjhn,bcjhp->bchpn', Bh * decay_end[..., None], xdt)
    chunk_decay = jnp.exp(acum[:, :, -1, :])

    def step(S, inp):
        dec, st = inp
        return S * dec[:, :, None, None] + st, S

    S_fin, S_start = lax.scan(step, S0.astype(f32),
                              (jnp.moveaxis(chunk_decay, 1, 0), jnp.moveaxis(chunk_states, 1, 0)))
    S_start = jnp.moveaxis(S_start, 0, 1)
    y_inter = jnp.einsum('bcihn,bchpn->bcihp', Ch * jnp.exp(acum)[..., None], S_start)
    return (y_intra + y_inter).reshape(b, L, H, P).astype(x.dtype), S_fin

def even_mixer(hn, p, ctx, layer_idx):
    b, L, _ = hn.shape
    latent = ctx is not None
    proj = hn @ p['w_in']
    qa, ka, va, q_down, ckv, kpe = jnp.split(
        proj, [HA * 2 * DA, 2 * HA * 2 * DA, A_COLS, A_COLS + Q_LORA, A_COLS + Q_LORA + KV_LORA], axis=-1)
    heads = lambda t, n: t.reshape(t.shape[0], t.shape[1], n, -1).transpose(0, 2, 1, 3)
    qa, ka, va = heads(qa, HA), heads(ka, HA), heads(va, HA)
    q1, q2 = jnp.split(qa, 2, axis=-1)
    k1, k2 = jnp.split(ka, 2, axis=-1)
    qb = heads(rmsnorm(q_down, p['q_norm']) @ p['w_uq'], HB)
    q_nope, q_pe = jnp.split(qb, [NOPE], axis=-1)
    ckv = rmsnorm(ckv, p['kv_norm'])
    if latent:
        ta = axial_rope_tables(L, DA)
        tb = axial_rope_tables(L, ROPE_B)
        q1, q2, k1, k2 = rope_2d(q1, ta), rope_2d(q2, ta), rope_2d(k1, ta), rope_2d(k2, ta)
        q_pe, kpe = rope_2d(q_pe, tb), rope_2d(kpe, tb)
    own = (jnp.concatenate([k1, k2], axis=-1), va, ckv, kpe)
    if latent:
        k_all, v_all, ckv_all, kpe_all = (jnp.concatenate([cc.astype(oo.dtype), oo], axis=-2)
                                          for cc, oo in zip(ctx, own))
    else:
        k_all, v_all, ckv_all, kpe_all = own
    lambda_init = 0.8 - 0.6 * math.exp(-0.3 * layer_idx)
    f32 = jnp.float32
    lam = (jnp.exp(jnp.sum(p['lambda_q1'].astype(f32) * p['lambda_k1'].astype(f32)))
           - jnp.exp(jnp.sum(p['lambda_q2'].astype(f32) * p['lambda_k2'].astype(f32))) + lambda_init)
    k1a, k2a = jnp.split(k_all, 2, axis=-1)
    sa = DA ** -0.5
    oa = attend(q1, k1a, v_all, sa) - lam.astype(hn.dtype) * attend(q2, k2a, v_all, sa)
    oa = rmsnorm(oa, p['subln']) * (1.0 - lambda_init)
    Lk = ckv_all.shape[1]
    kv = (ckv_all @ p['w_ukv']).reshape(b, Lk, HB, NOPE + VB).transpose(0, 2, 1, 3)
    k_nope, vb = jnp.split(kv, [NOPE], axis=-1)
    kpe_h = jnp.broadcast_to(kpe_all[:, None], (b, HB, Lk, ROPE_B))
    ob = attend(jnp.concatenate([q_nope, q_pe], axis=-1), jnp.concatenate([k_nope, kpe_h], axis=-1),
                vb, (NOPE + ROPE_B) ** -0.5)
    merged = jnp.concatenate([oa.transpose(0, 2, 1, 3).reshape(b, L, -1),
                              ob.transpose(0, 2, 1, 3).reshape(b, L, -1)], axis=-1)
    return merged @ p['w_out'], own

def odd_mixer(hn, p, ctx):
    b, L, _ = hn.shape
    f32 = jnp.float32
    proj = hn @ p['w_in']
    zc, zd = jnp.split(proj, [C_COLS], axis=-1)
    zc = zc + p['mu'] * (centred_shift(zc) - zc)
    r, k, v, wd, ad, gd = jnp.split(
        zc, [HC * NC, 2 * HC * NC, 3 * HC * NC, 3 * HC * NC + 2 * W_LORA, 3 * HC * NC + 2 * W_LORA + 2 * A_LORA],
        axis=-1)
    hsplit = lambda t: t.reshape(b, L, HC, NC)
    r, k, v = hsplit(r), hsplit(k), hsplit(v)
    kkf = (k * p['k_k'].reshape(HC, NC)).astype(f32)
    kk = (kkf * lax.rsqrt(jnp.sum(kkf * kkf, axis=-1, keepdims=True) + 1e-12)).astype(k.dtype)
    g = jax.nn.sigmoid(gd) @ p['g2']
    wds = jnp.split(wd, 2, axis=-1)
    ads = jnp.split(ad, 2, axis=-1)
    k_a = p['k_a'].reshape(HC, NC)
    if ctx is None:
        wkv0 = (jnp.zeros((b, HC, NC, NC), f32), jnp.zeros((b, HC, NC, NC), f32))
        ssm0 = (jnp.zeros((b, HD, PD, NS), f32), jnp.zeros((b, HD, PD, NS), f32))
    else:
        wkv0 = (ctx[0], ctx[1])
        ssm0 = (ctx[2], ctx[3])

    def wkv_direction(i):
        logw = -WKV_DECAY_SCALE * jax.nn.sigmoid(p['w0'][i] + jnp.tanh(wds[i]) @ p['w2'][i])
        a = hsplit(jax.nn.sigmoid(p['a0'][i] + ads[i] @ p['a2'][i]))
        k_i = k * (1.0 + (a - 1.0) * k_a)
        return wkv_scan(r, jnp.exp(hsplit(logw)), kk, a, k_i, v, wkv0[i], reverse=(i == 1))

    y_f, S_f = wkv_direction(0)
    y_b, S_b = wkv_direction(1)
    y = head_layernorm(y_f + y_b, p['ln_w'].reshape(HC, NC), p['ln_b'].reshape(HC, NC), WKV_LN_EPS)
    y = y + jnp.sum(r * k * p['r_k'], axis=-1, keepdims=True) * v
    oc = y.reshape(b, L, HC * NC) * g
    zg, xbc, dt_raw = jnp.split(zd, [D_INNER, D_INNER + CONV_CH], axis=-1)
    xbc = jax.nn.silu(dwconv3(xbc, p['conv_w'], p['conv_b']))
    xs, Bs, Cs = jnp.split(xbc, [D_INNER, D_INNER + G_SSM * NS], axis=-1)
    xs = xs.reshape(b, L, HD, PD)
    Bs = Bs.reshape(b, L, G_SSM, NS)
    Cs = Cs.reshape(b, L, G_SSM, NS)

    def ssd_direction(i):
        dt = jax.nn.softplus(dt_raw + p['dt_bias'][i])
        A = -jnp.exp(p['A_log'][i].astype(f32))
        if i == 1:
            fl = lambda t: jnp.flip(t, axis=1)
            yy, S = ssd_scan(fl(xs), fl(dt), A, fl(Bs), fl(Cs), ssm0[i])
            yy = fl(yy)
        else:
            yy, S = ssd_scan(xs, dt, A, Bs, Cs, ssm0[i])
        return yy + p['D'][i][:, None] * xs, S

    yd_f, H_f = ssd_direction(0)
    yd_b, H_b = ssd_direction(1)
    od = rmsnorm((yd_f + yd_b).reshape(b, L, D_INNER) * jax.nn.silu(zg), p['gnorm'])
    merged = jnp.concatenate([oc, od], axis=-1)
    return merged @ p['w_out'], (S_f, S_b, H_f, H_b)

def conv_ffn(x, p):
    u = dwconv3(x @ p['ffn_up'], p['ffn_conv_w'], p['ffn_conv_b'])
    gate, val = jnp.split(u, 2, axis=-1)
    return (jax.nn.silu(gate) * val) @ p['ffn_down']

def trunk_layer(h, cond, p, mixer, ctx):
    sh1, sc1, g1, sh2, sc2, g2 = jnp.split(jax.nn.silu(cond) @ p['ada_w'] + p['ada_b'], 6, axis=-1)
    hn = rmsnorm(h, p['norm1']) * (1.0 + sc1) + sh1
    m, ctx_out = mixer(hn, p['mix'], ctx)
    h = h + g1 * m
    hn = rmsnorm(h, p['norm2']) * (1.0 + sc2) + sh2
    h = h + g2 * conv_ffn(hn, p)
    return h, ctx_out

def setup_inputs(seed: int = 0) -> dict:
    key = jax.random.key(seed)
    ks = iter(jax.random.split(key, 96))
    nrm = lambda shape, s=1.0: jax.random.normal(next(ks), shape, jnp.float32) * s
    gain = lambda n: 1.0 + 0.02 * jax.random.normal(next(ks), (n,), jnp.float32)
    inp = {}
    inp['x_prompt'] = nrm((BATCH, SEQ, D_MODEL))
    inp['x_sample'] = nrm((DEC_BATCH, DEC_SEQ, D_MODEL))
    inp['cache_l0_k'] = nrm((DEC_BATCH, HA, PAST_LEN, 2 * DA))
    inp['cache_l0_v'] = nrm((DEC_BATCH, HA, PAST_LEN, 2 * DA))
    inp['cache_l0_ckv'] = nrm((DEC_BATCH, PAST_LEN, KV_LORA))
    inp['cache_l0_kpe'] = nrm((DEC_BATCH, PAST_LEN, ROPE_B))
    inp['state_l1_wkv_fwd'] = nrm((DEC_BATCH, HC, NC, NC), 0.5)
    inp['state_l1_wkv_bwd'] = nrm((DEC_BATCH, HC, NC, NC), 0.5)
    inp['state_l1_ssm_fwd'] = nrm((DEC_BATCH, HD, PD, NS), 0.5)
    inp['state_l1_ssm_bwd'] = nrm((DEC_BATCH, HD, PD, NS), 0.5)
    inp['c'] = nrm((DEC_BATCH, D_MODEL))
    inp['c_ctx'] = nrm((D_MODEL,))

    def common(i):
        inp['ada_w_%d' % i] = nrm((D_MODEL, 6 * D_MODEL), D_MODEL ** -0.5)
        inp['ada_b_%d' % i] = nrm((6 * D_MODEL,), 0.02)
        inp['norm1_%d' % i] = gain(D_MODEL)
        inp['norm2_%d' % i] = gain(D_MODEL)
        inp['ffn_up_%d' % i] = nrm((D_MODEL, 2 * F_FF), D_MODEL ** -0.5)
        inp['ffn_conv_w_%d' % i] = nrm((3, 2 * F_FF), 3 ** -0.5)
        inp['ffn_conv_b_%d' % i] = nrm((2 * F_FF,), 0.02)
        inp['ffn_down_%d' % i] = nrm((F_FF, D_MODEL), F_FF ** -0.5)

    common(0)
    inp['l0_w_in'] = nrm((D_MODEL, A_COLS + B_COLS), D_MODEL ** -0.5)
    inp['l0_lambda_q1'] = nrm((DA,), 0.1)
    inp['l0_lambda_k1'] = nrm((DA,), 0.1)
    inp['l0_lambda_q2'] = nrm((DA,), 0.1)
    inp['l0_lambda_k2'] = nrm((DA,), 0.1)
    inp['l0_subln'] = gain(2 * DA)
    inp['l0_q_norm'] = gain(Q_LORA)
    inp['l0_w_uq'] = nrm((Q_LORA, HB * (NOPE + ROPE_B)), Q_LORA ** -0.5)
    inp['l0_kv_norm'] = gain(KV_LORA)
    inp['l0_w_ukv'] = nrm((KV_LORA, HB * (NOPE + VB)), KV_LORA ** -0.5)
    inp['l0_w_out'] = nrm((MIX_WIDTH, D_MODEL), MIX_WIDTH ** -0.5)
    common(1)
    inp['l1_w_in'] = nrm((D_MODEL, C_COLS + D_COLS), D_MODEL ** -0.5)
    inp['l1_mu'] = jax.random.uniform(next(ks), (C_COLS,), jnp.float32)
    inp['l1_w0'] = nrm((2, HC * NC), 0.5)
    inp['l1_w2'] = nrm((2, W_LORA, HC * NC), W_LORA ** -0.5)
    inp['l1_a0'] = nrm((2, HC * NC), 0.5)
    inp['l1_a2'] = nrm((2, A_LORA, HC * NC), A_LORA ** -0.5)
    inp['l1_g2'] = nrm((G_LORA, HC * NC), G_LORA ** -0.5)
    inp['l1_k_k'] = 0.85 + nrm((HC * NC,), 0.05)
    inp['l1_k_a'] = 1.0 + nrm((HC * NC,), 0.05)
    inp['l1_r_k'] = nrm((HC, NC), 0.1)
    inp['l1_ln_w'] = gain(HC * NC)
    inp['l1_ln_b'] = nrm((HC * NC,), 0.02)
    inp['l1_conv_w'] = nrm((3, CONV_CH), 3 ** -0.5)
    inp['l1_conv_b'] = nrm((CONV_CH,), 0.02)
    inp['l1_A_log'] = jnp.log(jax.random.uniform(next(ks), (2, HD), jnp.float32, 1.0, 16.0))
    dt0 = jnp.exp(jax.random.uniform(next(ks), (2, HD), jnp.float32, math.log(1e-3), math.log(1e-1)))
    inp['l1_dt_bias'] = dt0 + jnp.log(-jnp.expm1(-dt0))
    inp['l1_D'] = 1.0 + nrm((2, HD), 0.1)
    inp['l1_gnorm'] = gain(D_INNER)
    inp['l1_w_out'] = nrm((MIX_WIDTH, D_MODEL), MIX_WIDTH ** -0.5)
    inp['norm_f'] = gain(D_MODEL)
    return inp

def reference(x_prompt, x_sample, cache_l0_k, cache_l0_v, cache_l0_ckv, cache_l0_kpe,
              state_l1_wkv_fwd, state_l1_wkv_bwd, state_l1_ssm_fwd, state_l1_ssm_bwd,
              c, c_ctx,
              ada_w_0, ada_b_0, norm1_0, norm2_0, ffn_up_0, ffn_conv_w_0, ffn_conv_b_0, ffn_down_0,
              l0_w_in, l0_lambda_q1, l0_lambda_k1, l0_lambda_q2, l0_lambda_k2, l0_subln,
              l0_q_norm, l0_w_uq, l0_kv_norm, l0_w_ukv, l0_w_out,
              ada_w_1, ada_b_1, norm1_1, norm2_1, ffn_up_1, ffn_conv_w_1, ffn_conv_b_1, ffn_down_1,
              l1_w_in, l1_mu, l1_w0, l1_w2, l1_a0, l1_a2, l1_g2, l1_k_k, l1_k_a, l1_r_k,
              l1_ln_w, l1_ln_b, l1_conv_w, l1_conv_b, l1_A_log, l1_dt_bias, l1_D, l1_gnorm, l1_w_out,
              norm_f):
    layers = [
        dict(ada_w=ada_w_0, ada_b=ada_b_0, norm1=norm1_0, norm2=norm2_0, ffn_up=ffn_up_0,
             ffn_conv_w=ffn_conv_w_0, ffn_conv_b=ffn_conv_b_0, ffn_down=ffn_down_0,
             mix=dict(w_in=l0_w_in, lambda_q1=l0_lambda_q1, lambda_k1=l0_lambda_k1,
                      lambda_q2=l0_lambda_q2, lambda_k2=l0_lambda_k2, subln=l0_subln,
                      q_norm=l0_q_norm, w_uq=l0_w_uq, kv_norm=l0_kv_norm, w_ukv=l0_w_ukv, w_out=l0_w_out)),
        dict(ada_w=ada_w_1, ada_b=ada_b_1, norm1=norm1_1, norm2=norm2_1, ffn_up=ffn_up_1,
             ffn_conv_w=ffn_conv_w_1, ffn_conv_b=ffn_conv_b_1, ffn_down=ffn_down_1,
             mix=dict(w_in=l1_w_in, mu=l1_mu, w0=l1_w0, w2=l1_w2, a0=l1_a0, a2=l1_a2, g2=l1_g2,
                      k_k=l1_k_k, k_a=l1_k_a, r_k=l1_r_k, ln_w=l1_ln_w, ln_b=l1_ln_b,
                      conv_w=l1_conv_w, conv_b=l1_conv_b, A_log=l1_A_log, dt_bias=l1_dt_bias,
                      D=l1_D, gnorm=l1_gnorm, w_out=l1_w_out)),
    ]
    caches = [(cache_l0_k, cache_l0_v, cache_l0_ckv, cache_l0_kpe),
              (state_l1_wkv_fwd, state_l1_wkv_bwd, state_l1_ssm_fwd, state_l1_ssm_bwd)]
    cond_ctx = c_ctx[None, None, :]
    cond_lat = c[:, None, :]
    h_ctx, h_lat = x_prompt, x_sample
    new_state = []
    for i in range(DEPTH):
        p = layers[i]
        mixer = functools.partial(even_mixer, layer_idx=i) if i % 2 == 0 else odd_mixer
        h_ctx, ctx_tensors = trunk_layer(h_ctx, cond_ctx, p, mixer, None)
        h_lat, _ = trunk_layer(h_lat, cond_lat, p, mixer, caches[i])
        new_state.append(ctx_tensors)
    y_prompt = rmsnorm(h_ctx, norm_f)
    y_sample = rmsnorm(h_lat, norm_f)
    new_l0_k, new_l0_v, new_l0_ckv, new_l0_kpe = new_state[0]
    new_l1_wkv_fwd, new_l1_wkv_bwd, new_l1_ssm_fwd, new_l1_ssm_bwd = new_state[1]
    return (y_prompt, y_sample, new_l0_k, new_l0_v, new_l0_ckv, new_l0_kpe,
            new_l1_wkv_fwd, new_l1_wkv_bwd, new_l1_ssm_fwd, new_l1_ssm_bwd)


_drawn_inputs = setup_inputs


def setup_inputs(seed=0):
    import zlib

    import numpy as np

    out = dict(_drawn_inputs(seed))
    spreads = {}
    factors = {'cache_l0_ckv': 2.845,
     'cache_l0_kpe': 5.62,
     'state_l1_wkv_fwd': 8.0,
     'state_l1_wkv_bwd': 8.0,
     'norm1_0': 3.218,
     'norm2_0': 3.612,
     'ffn_conv_b_0': 3.679,
     'l0_lambda_q1': 7.173,
     'l0_lambda_k1': 8.0,
     'l0_subln': 5.881,
     'l0_q_norm': 8.0,
     'l0_kv_norm': 2.916,
     'norm2_1': 20.219,
     'ffn_conv_b_1': 22.259,
     'l1_ln_w': 200.0,
     'l1_ln_b': 200.0,
     'l1_D': 4.19,
     'l1_gnorm': 135.852,
     'norm_f': 22.865,
     'cache_l0_k': 8.0,
     'cache_l0_v': 8.0,
     'l1_r_k': 6.671}
    for name, (base, spread) in spreads.items():
        noise = np.random.default_rng([zlib.crc32(name.encode()), seed]).standard_normal(out[name].shape)
        drawn = base * np.exp(spread * noise) if base else spread * noise
        out[name] = __import__('jax').numpy.asarray(drawn.astype(out[name].dtype))
    for name, factor in factors.items():
        out[name] = (out[name] * factor).astype(out[name].dtype)
    return out
```

```python
import math
from contextlib import ExitStack

import numpy as np
import concourse.bass as bass
from concourse import mybir

F32 = mybir.dt.float32
ALU = mybir.AluOpType
ACT = mybir.ActivationFunctionType
AXX = mybir.AxisListType.X
P = 128

D = 1024
KT = D // P
NL, NP_, NPAST = 512, 128, 128
NT = NL + NP_
NK = NT + NPAST
FF = 2816
FT = FF // P
HA, DA = 4, 64
HB, NOPE, ROPE, VB = 4, 64, 32, 128
QL, KVL = 192, 128
QK = NOPE + ROPE
HC, NC_ = 8, 64
HD, PD, NS = 8, 64, 64
NCH = NT // P
DEC = 0.606531
EPS = 1e-6
RING = 2
SLOT = 4096
SEG = ((0, NL), (NL, NT))


def param_columns():
    at, n = {}, 0
    for name, w in ([("cond", 2 * KT)] +
                    [(f"{k}{i}", w) for i in range(2) for k, w in
                     (("ada_b", 48), ("norm1", KT), ("norm2", KT), ("ffn_b", 2 * FT), ("ffn_w", 3 * 2 * FT))] +
                    [("norm_f", KT), ("lam", 4), ("subln", 1), ("q_norm", 2), ("kv_norm", 1),
                     ("mu", 15), ("w0", 8), ("a0", 8), ("k_k", 4), ("k_a", 4), ("r_k", 4), ("ln_w", 4),
                     ("ln_b", 4), ("conv_w", 18), ("conv_b", 6), ("gnorm", 4), ("Dskip", 8),
                     ("dt_bias", 1), ("A_log", 1)]):
        at[name] = n
        n += w
    return at, n


def const_columns():
    at, n = {}, 0
    for name, w in (("ident", P), ("blk", P), ("rotA", P), ("rotB", P), ("cosA", NL), ("sinA", NL),
                    ("cosB", NL), ("sinB", NL), ("gmask", 2 * P), ("armask", 4 * P), ("lev", 7 * 2 * P),
                    ("reset", NT), ("selh", 8 * P), ("selr", 4 * P)):
        at[name] = (n, w)
        n += w
    return at, n


def build(nc, t_in, t_out):
    PC, NPAR = param_columns()
    CC, NCON = const_columns()
    ctx = ExitStack()
    with ctx:
        def sb(name, n, dt=F32):
            return ctx.enter_context(nc.sbuf_tensor(name, [P, n], dt))

        def sem(name):
            return ctx.enter_context(nc.semaphore(name))

        ps_all = ctx.enter_context(nc.psum_tensor("ps", [P, 8 * 512], F32))

        def bank(b, n=512, p0=0, p1=P):
            return ps_all[p0:p1, 512 * b:512 * b + n]

        ring = sb("ring", RING * SLOT)
        h_b = sb("h", KT * NT)
        merged_b = sb("merged", KT * NT)
        par = sb("par", NPAR)
        mods = sb("mods", 2 * 96)
        geff = sb("geff", 4 * 16)
        ones = sb("ones", P)
        ident = sb("ident", P)
        blk = sb("blk", P)
        stat = sb("stat", 2 * NT)
        sqb = sb("sqb", 2 * NT)
        small = sb("small", 160)
        WN = 30800
        work = sb("work", WN)

        def area(start):
            pos = [start]

            def take(n):
                a = work[:, pos[0]:pos[0] + n]
                pos[0] += n
                assert pos[0] <= WN, (pos[0], WN)
                return a
            return take

        take0 = area(0)
        hn_b = take0(KT * NT)
        W0 = KT * NT

        def tile(buf, t, a=0, b=NT, n=NT):
            return buf[:, t * n + a:t * n + b]

        h = lambda t, a=0, b=NT: tile(h_b, t, a, b)
        hn = lambda t, a=0, b=NT: tile(hn_b, t, a, b)
        merged = lambda t, a=0, b=NT: tile(merged_b, t, a, b)

        def pc(name, i=0, w=1, p0=0, p1=P):
            return par[p0:p1, PC[name] + i:PC[name] + i + w]

        blocks = []
        def kblock(src, c0, c1):
            return [(src[:, c0:c1].rearrange("(k p) c -> p k c", p=P), KT, 0, c1 - c0, c1 - c0)]

        def plan():
            for l in range(2):
                for b in range(12):
                    blocks.append(("ada", kblock(t_in[f"ada_w_{l}"], 512 * b, 512 * b + 512)))
                win = t_in[f"l{l}_w_in"]
                cuts = ((0, 512), (512, 1024), (1024, 1536), (1536, 1888)) if l == 0 else \
                    ((1920, 2432), (2432, 2944), (2944, 3208), (0, 512), (512, 1024), (1024, 1536), (1536, 1920))
                for a, b in cuts:
                    blocks.append(("win", kblock(win, a, b)))
                for b in range(2):
                    blocks.append(("wout", kblock(t_in[f"l{l}_w_out"], 512 * b, 512 * b + 512)))
                up, down = t_in[f"ffn_up_{l}"], t_in[f"ffn_down_{l}"]
                for b in range(FT // 2):
                    src = up.rearrange("(k p) c -> p k c", p=P)
                    blocks.append(("up", [(src[:, :, 256 * b:256 * b + 256], KT, 0, 256, 512),
                                          (src[:, :, FF + 256 * b:FF + 256 * b + 256], KT, 256, 256, 512)]))
                for b in range(KT):
                    blocks.append(("down", [(down[:, P * b:P * b + P].rearrange("(k p) c -> p k c", p=P), FT, 0, P, P)]))
        plan()
        full = [sem(f"block_loaded{i}") for i in range(RING)]
        parts_before = [[0] * (len(blocks) + 1) for _ in range(RING)]
        for n, (_, parts) in enumerate(blocks):
            for i in range(RING):
                parts_before[i][n + 1] = parts_before[i][n] + (len(parts) if n % RING == i else 0)
        released = []
        used = [0]

        def next_block(pe):
            n = used[0]
            used[0] += 1
            _, parts = blocks[n]
            pe.wait_ge(full[n % RING], 16 * parts_before[n % RING][n + 1])
            kt, width = parts[0][1], parts[0][4]
            return ring[:, (n % RING) * SLOT:(n % RING) * SLOT + kt * width].rearrange("p (k c) -> p k c", k=kt)

        S = {}

        def sg(name):
            if name not in S:
                S[name] = sem(name)
            return S[name]

        phase = sem("phase_left")
        phase_no = [0, 0, 0, 0]

        def leave_phase(eng, who):
            phase_no[who] += 1
            eng.drain().then_inc(phase, 1)
            eng.wait_ge(phase, 4 * phase_no[who])

        PE_, ACT_, DVE_, POOL_ = range(4)

        class Chain:
            def __init__(self, eng, name):
                self.eng, self.sem, self.n = eng, sg(name), 0

            def __call__(self, ins):
                self.n += 1
                ins.then_inc(self.sem, 1)
                self.eng.wait_ge(self.sem, self.n)

        def mm(pe, out, lhsT, rhs, first=True, last=True):
            return pe.matmul(out, lhsT, rhs, start=first, stop=last)

        def project(pe, pair, lhs, rhs, nk, p1=P, toks=SEG, p0=0):
            for k in range(nk):
                for a, b in toks:
                    ins = mm(pe, ps_all[p0:p1, 1024 * pair + a:1024 * pair + b], lhs(k), rhs(k, a, b),
                             k == 0, k == nk - 1)
            return ins

        def pair_ap(pair, a=0, b=NT, p0=0, p1=P):
            return ps_all[p0:p1, 1024 * pair + a:1024 * pair + b]

        def ada_pe(pe, l):
            pe.wait_ge(sg("cond_silu"), 1)
            for b in range(12):
                w = next_block(pe)
                for m in range(4):
                    for k in range(KT):
                        ins = mm(pe, bank(5)[:, 2 * (4 * b + m):2 * (4 * b + m) + 2], w[:, k, P * m:P * m + P],
                                 small[:, 2 * k:2 * k + 2], k == 0, k == KT - 1)
                ins.then_inc(sg("ada_block"), 1)
                released.append((sg("ada_block"), 12 * l + b + 1))

        def ada_dve(dve, l, ch):
            dve.wait_ge(sg("ada_block"), 12 * (l + 1))
            md = mods[:, 96 * l:96 * l + 96].rearrange("p (m c) -> p m c", c=2)
            ch(dve.tensor_tensor(md, bank(5, 96).rearrange("p (m c) -> p m c", c=2),
                                 pc(f"ada_b{l}", 0, 48).unsqueeze(2).to_broadcast([P, 48, 2]), ALU.add))
            for i in range(2):
                g = geff[:, 16 * (2 * l + i):16 * (2 * l + i) + 16].rearrange("p (m c) -> p m c", c=2)
                ch(dve.tensor_scalar(g, md[:, 24 * i + 8:24 * i + 16, :], 1.0, None, ALU.add))
                ins = dve.tensor_tensor(g, g, pc(f"norm{i + 1}{l}", 0, KT).unsqueeze(2).to_broadcast([P, KT, 2]),
                                        ALU.mult)
                if i == 0:
                    ch(ins)
                else:
                    ins.then_inc(sg("mods_ready"), 1)
            dve.wait_ge(sg("mods_ready"), l + 1)

        def mod(l, part, t, c):
            o = 96 * l + 2 * (8 * part + t) + c
            return mods[:, o:o + 1]

        def norm_act(act, n, shift, src=h, nt=KT, last=False):
            for t in range(nt):
                if t >= 2:
                    act.wait_ge(sg("norm_sum"), 8 * n + t - 1)
                if last:
                    pass
                act.activation(tile(sqb, t % 2), src(t), ACT.Square).then_inc(sg("norm_sq"), 1)
            act.wait_ge(sg("norm_sum"), 8 * n + 8)
            act.activation(stat[:, 0:NT], pair_ap(3), ACT.Sqrt, bias=small[:, 16:17], scale=1.0 / D)\
                .then_inc(sg("norm_root"), 1)
            if shift is not None:
                for t in range(nt):
                    act.wait_ge(sg("norm_scaled"), 8 * n + t + 1)
                    act.activation(hn(t, 0, NL), hn(t, 0, NL), ACT.Identity, bias=shift(t, 0)).then_inc(sg("hn_half"), 1)
                    act.activation(hn(t, NL, NT), hn(t, NL, NT), ACT.Identity, bias=shift(t, 1)).then_inc(sg("hn_ready"), 1)

        def norm_pe(pe, n):
            for t in range(KT):
                pe.wait_ge(sg("norm_sq"), 8 * n + t + 1)
                for a, b in SEG:
                    ins = mm(pe, pair_ap(3, a, b), ones[:, :], tile(sqb, t % 2, a, b), t == 0, t == KT - 1)
                ins.then_inc(sg("norm_sum"), 1)

        def norm_dve(dve, n, gain, ch, out=hn):
            dve.wait_ge(sg("norm_root"), n + 1)
            ch(dve.reciprocal(stat[:, NT:2 * NT], stat[:, 0:NT]))
            for t in range(KT):
                dve.scalar_tensor_tensor(out(t, 0, NL), h(t, 0, NL), gain(t, 0), stat[:, NT:NT + NL], ALU.mult, ALU.mult)
                dve.scalar_tensor_tensor(out(t, NL, NT), h(t, NL, NT), gain(t, 1), stat[:, NT + NL:2 * NT],
                                         ALU.mult, ALU.mult).then_inc(sg("norm_scaled"), 1)

        def g_eff(n):
            return lambda t, c: geff[:, 16 * n + 2 * t + c:16 * n + 2 * t + c + 1]

        res_no = [0]

        def residual_dve(dve, base, gate, ch):
            for m in range(KT):
                dve.wait_ge(sg("res_prod"), base + m + 1)
                dve.scalar_tensor_tensor(h(m, 0, NL), pair_ap(m % 2, 0, NL), gate(m, 0), h(m, 0, NL), ALU.mult, ALU.add)
                dve.scalar_tensor_tensor(h(m, NL, NT), pair_ap(m % 2, NL, NT), gate(m, 1), h(m, NL, NT),
                                         ALU.mult, ALU.add).then_inc(sg("res_done"), 1)
            dve.wait_ge(sg("res_done"), base + KT)

        def wout_pe(pe, base):
            for b in range(2):
                w = next_block(pe)
                for m in range(4):
                    n = 4 * b + m
                    if n >= 2:
                        pe.wait_ge(sg("res_done"), base + n - 1)
                    project(pe, n % 2, lambda k: w[:, k, P * m:P * m + P], merged, KT).then_inc(sg("res_prod"), 1)
                released.append((sg("res_prod"), base + 4 * b + 4))

        tk = area(W0)
        G_b = tk(FT * NT)
        G = lambda t, a=0, b=NT: tile(G_b, t, a, b)
        cacc = tk(4 * NT)

        def conv3_dve(dve, acc, psrc, w0, w2, ch, final=None):
            for i, (a, b) in enumerate(SEG):
                ch(dve.scalar_tensor_tensor(acc(a + 1, b), psrc(a, b - 1), w0, acc(a + 1, b), ALU.mult, ALU.add))
            for i, (a, b) in enumerate(SEG):
                ins = dve.scalar_tensor_tensor(acc(a, b - 1), psrc(a + 1, b), w2, acc(a, b - 1), ALU.mult, ALU.add)
                if i == 1 and final is not None:
                    ins.then_inc(final, 1)
                else:
                    ch(ins)

        def ffn_pe(pe, l):
            for b in range(FT // 2):
                w = next_block(pe)
                for i in range(2):
                    for half in range(2):
                        n = 2 * (2 * b + i) + half
                        if n >= 2:
                            pe.wait_ge(sg("conv_done"), 2 * FT * l + n - 1)
                        project(pe, n % 2, lambda k: w[:, k, 256 * half + P * i:256 * half + P * i + P], hn, KT)\
                            .then_inc(sg("up_prod"), 1)
                released.append((sg("up_prod"), 2 * FT * l + 4 * b + 4))
            base = KT * (2 * l + 1)
            pe.wait_ge(sg("gated"), FT * (l + 1))
            for m in range(KT):
                w = next_block(pe)
                if m >= 2:
                    pe.wait_ge(sg("res_done"), base + m - 1)
                project(pe, m % 2, lambda k: w[:, k, :], G, FT).then_inc(sg("res_prod"), 1)
                released.append((sg("res_prod"), base + m + 1))

        def cw(l, tap, t):
            return pc(f"ffn_w{l}", tap * 2 * FT + t)

        def ffn_act(act, l):
            for m in range(FT):
                for half in range(2):
                    n = 2 * m + half
                    act.wait_ge(sg("up_prod"), 2 * FT * l + n + 1)
                    if m >= 2:
                        act.wait_ge(sg("gated"), FT * l + m - 1)
                    act.activation(tile(cacc, 2 * (m % 2) + half), pair_ap(n % 2), ACT.Identity,
                                   bias=pc(f"ffn_b{l}", half * FT + m), scale=cw(l, 1, half * FT + m))\
                        .then_inc(sg("centre_tap"), 1)
                act.wait_ge(sg("conv_done"), 2 * FT * l + 2 * m + 1)
                a = tile(cacc, 2 * (m % 2))
                act.activation(a, a, ACT.Silu).then_inc(sg("gate_silu"), 1)

        def ffn_dve(dve, l, ch):
            for m in range(FT):
                for half in range(2):
                    n = 2 * m + half
                    dve.wait_ge(sg("centre_tap"), 2 * FT * l + n + 1)
                    conv3_dve(dve, lambda a, b: tile(cacc, 2 * (m % 2) + half, a, b),
                              lambda a, b: pair_ap(n % 2, a, b), cw(l, 0, half * FT + m), cw(l, 2, half * FT + m),
                              ch, sg("conv_done"))
                dve.wait_ge(sg("gate_silu"), FT * l + m + 1)
                dve.wait_ge(sg("conv_done"), 2 * FT * l + 2 * m + 2)
                dve.tensor_tensor(G(m), tile(cacc, 2 * (m % 2)), tile(cacc, 2 * (m % 2) + 1), ALU.mult)\
                    .then_inc(sg("gated"), 1)
            residual_dve(dve, KT * (2 * l + 1), lambda t, c: mod(l, 5, t, c), ch)

        stat_at = [0, 0]

        def plan_stats(items):
            i0, c0 = stat_at
            stat_at[0] += len(items)
            stat_at[1] += sum(len(it[0]) for it in items)
            return i0, c0, items

        def stats_act(act, planned):
            i, c, items = planned
            for srcs, mat, scale, eps, outs in items:
                for src, kk in srcs:
                    if c >= 2:
                        act.wait_ge(sg("st_sum"), c - 1)
                    act.activation(sqb[0:kk, (c % 2) * NT:(c % 2) * NT + NT], src, ACT.Square).then_inc(sg("st_sq"), 1)
                    c += 1
                act.wait_ge(sg("st_sum"), c)
                if i >= 2:
                    act.wait_ge(sg("st_used"), i - 1)
                act.activation(stat[:, (i % 2) * NT:(i % 2) * NT + NT], pair_ap(3), ACT.Sqrt,
                               bias=small[:, eps:eps + 1], scale=scale).then_inc(sg("st_root"), 1)
                i += 1

        def stats_pe(pe, planned):
            i, c, items = planned
            for srcs, mat, scale, eps, outs in items:
                if i >= 1:
                    pe.wait_ge(sg("st_root"), i)
                for j, (src, kk) in enumerate(srcs):
                    pe.wait_ge(sg("st_sq"), c + 1)
                    for a, b in SEG:
                        ins = mm(pe, pair_ap(3, a, b), mat[0:kk, :], sqb[0:kk, (c % 2) * NT + a:(c % 2) * NT + b],
                                 j == 0, j == len(srcs) - 1)
                    ins.then_inc(sg("st_sum"), 1)
                    c += 1
                i += 1

        def stats_dve(dve, planned, ch):
            i, c, items = planned
            for srcs, mat, scale, eps, outs in items:
                dve.wait_ge(sg("st_root"), i + 1)
                st = stat[:, (i % 2) * NT:(i % 2) * NT + NT]
                ch(dve.reciprocal(st, st))
                for j, (out, in_, gain, kk) in enumerate(outs):
                    ins = dve.scalar_tensor_tensor(out, in_, gain, st[0:kk, :], ALU.mult, ALU.mult)
                    if j == len(outs) - 1:
                        ins.then_inc(sg("st_used"), 1)
                    else:
                        ch(ins)
                i += 1
            dve.wait_ge(sg("st_used"), i)

        tk = area(W0)
        q_b, k_b, v_b = tk(4 * NT), tk(4 * NK), tk(6 * 512)
        pr_b, dT_b, dTp_b = tk(2 * 2 * NT), tk(2 * 5 * 512), tk(2 * P)
        qd_b, ckv_b, kpe_b = tk(2 * NT), tk(NK), tk(NK)
        wuq, wukv = tk(2 * 384), tk(768)
        cosA, sinA, cosB, sinB, rotA, rotB = tk(NL), tk(NL), tk(NL), tk(NL), tk(P), tk(P)
        rt_b = tk(NL)
        q = lambda t, a=0, b=NT: tile(q_b, t, a, b)
        kk_ = lambda t, a=0, b=NK: tile(k_b, t, a, b, NK)
        KP0 = NT
        NEGLAM, SUB8 = 24, 25

        def rope(dve, x, x_raw, psum, cos, sin, ch, p0=0, p1=P, done=None):
            ch(dve.tensor_tensor(rt_b[p0:p1, :], psum, sin[p0:p1, :], ALU.mult))
            ch(dve.tensor_tensor(x, x, cos[p0:p1, :], ALU.mult))
            ins = dve.tensor_tensor(x, x, rt_b[p0:p1, :], ALU.add)
            if done is not None:
                ins.then_inc(done, 1)
            else:
                ch(ins)

        def mix0_pe(pe):
            n = 0
            for part in range(2):
                w = next_block(pe)
                for m in range(4):
                    if n >= 3:
                        pe.wait_ge(sg("m0_copied"), n - 2)
                    project(pe, n % 3, lambda k: w[:, k, P * m:P * m + P], hn, KT).then_inc(sg("m0_prod"), 1)
                    n += 1
                released.append((sg("m0_prod"), n))
            w = next_block(pe)
            for tt in range(5):
                pe.wait_ge(sg("m0_copied"), n - 2)
                for k in range(KT):
                    ins = mm(pe, bank(2 * (n % 3)), hn(k, P * tt, P * tt + P), w[:, k, :], k == 0, k == KT - 1)
                ins.then_inc(sg("m0_prod"), 1)
                n += 1
            released.append((sg("m0_prod"), n))
            w = next_block(pe)
            for c0, c1 in ((0, 128), (128, 192), (192, 320), (256, 352)):
                pe.wait_ge(sg("m0_copied"), n - 2)
                project(pe, n % 3, lambda k: w[:, k, c0:c1], hn, KT, p1=c1 - c0).then_inc(sg("m0_prod"), 1)
                n += 1
            released.append((sg("m0_prod"), n))
            pe.wait_ge(sg("m0_loaded"), 16 * 14)
            for m in range(8):
                pe.wait_ge(sg("m0_copied"), 17)
                if m >= 2:
                    pe.wait_ge(sg("m0_roped"), m - 1)
                src = q(m, 0, NL) if m < 4 else kk_(m - 4, 0, NL)
                mm(pe, bank(m % 2), rotA[:, :], src).then_inc(sg("m0_rot"), 1)
            pe.wait_ge(sg("m0_roped"), 8)
            mm(pe, bank(0, 512, 0, QK), rotB[0:QK, 0:QK], kpe_b[0:QK, 0:NL]).then_inc(sg("m0_rot"), 1)
            stats_pe(pe, low_norms)
            pe.wait_ge(sg("m0_roped"), 9)
            pe.wait_ge(sg("lam_prod"), 1)
            mm(pe, bank(0, 2), ones[0:64, :], small[0:64, 26:28]).then_inc(sg("lam_sum"), 1)

        low_norms = plan_stats([
            ([(tile(qd_b, 0), P), (qd_b[0:64, NT:2 * NT], 64)], ones, 1.0 / QL, 16,
             [(tile(qd_b, 0), tile(qd_b, 0), pc("q_norm", 0), P),
              (qd_b[0:64, NT:2 * NT], qd_b[0:64, NT:2 * NT], pc("q_norm", 1, 1, 0, 64), 64)]),
            ([(sqb[:, 0:NT] if False else merged(0), P)], ones, 1.0 / KVL, 16,
             [(merged(0), merged(0), pc("kv_norm"), P)])])

        def mix0_act(act):
            n = 0
            for m in range(8):
                act.wait_ge(sg("m0_prod"), n + 1)
                if m < 4:
                    act.activation(q(m), pair_ap(n % 3), ACT.Copy, scale=DA ** -0.5).then_inc(sg("m0_copied"), 1)
                else:
                    act.activation(kk_(m - 4, 0, NL), pair_ap(n % 3, 0, NL), ACT.Copy)
                    act.activation(kk_(m - 4, KP0, NK), pair_ap(n % 3, NL, NT), ACT.Copy).then_inc(sg("m0_copied"), 1)
                n += 1
            for tt in range(5):
                act.wait_ge(sg("m0_prod"), n + 1)
                slot = tt if tt < 4 else 5
                act.activation(v_b[:, 512 * slot:512 * slot + 512], bank(2 * (n % 3)), ACT.Copy).then_inc(sg("m0_copied"), 1)
                n += 1
            for i in range(4):
                act.wait_ge(sg("m0_prod"), n + 1)
                pp = n % 3
                if i == 0:
                    act.activation(tile(qd_b, 0), pair_ap(pp), ACT.Copy).then_inc(sg("m0_copied"), 1)
                elif i == 1:
                    act.activation(qd_b[0:64, NT:2 * NT], pair_ap(pp, 0, NT, 0, 64), ACT.Copy).then_inc(sg("m0_copied"), 1)
                elif i == 2:
                    act.activation(merged(0), pair_ap(pp), ACT.Copy).then_inc(sg("m0_copied"), 1)
                else:
                    act.activation(kpe_b[0:QK, 0:NL], pair_ap(pp, 0, NL, 0, QK), ACT.Copy)
                    act.activation(kpe_b[64:QK, KP0:NK], pair_ap(pp, NL, NT, 64, QK), ACT.Copy).then_inc(sg("m0_copied"), 1)
                n += 1
            act.wait_ge(sg("m0_copied"), 17)
            stats_act(act, low_norms)
            act.wait_ge(sg("lam_sum"), 1)
            act.activation(small[:, 28:30], bank(0, 2), ACT.Exp).then_inc(sg("lam_exp"), 1)

        def mix0_dve(dve, ch):
            for m in range(9):
                dve.wait_ge(sg("m0_rot"), m + 1)
                if m < 8:
                    src = q(m, 0, NL) if m < 4 else kk_(m - 4, 0, NL)
                    rope(dve, src, src, bank(m % 2), cosA, sinA, ch, done=sg("m0_roped"))
                else:
                    x = kpe_b[64:QK, 0:NL]
                    rope(dve, x, x, bank(0, 512, 64, QK), cosB, sinB, ch, 64, QK, done=sg("m0_roped"))
                dve.wait_ge(sg("m0_roped"), m + 1)
            stats_dve(dve, low_norms, ch)
            ch(dve.tensor_copy(ckv_b[:, 0:NL], merged(0, 0, NL)))
            ch(dve.tensor_copy(ckv_b[:, KP0:NK], merged(0, NL, NT)))
            lp = par[0:64, PC["lam"]:PC["lam"] + 4].rearrange("p (a b) -> p a b", b=2)
            dve.tensor_tensor(small[0:64, 26:28], lp[:, :, 0], lp[:, :, 1], ALU.mult).then_inc(sg("lam_prod"), 1)
            lam_init = 0.8 - 0.6 * math.exp(0.0)
            dve.wait_ge(sg("lam_exp"), 1)
            ch(dve.tensor_tensor(small[:, NEGLAM:NEGLAM + 1], small[:, 29:30], small[:, 28:29], ALU.subtract))
            ch(dve.tensor_scalar(small[:, NEGLAM:NEGLAM + 1], small[:, NEGLAM:NEGLAM + 1], -lam_init, None, ALU.add))
            ch(dve.tensor_scalar(small[:, SUB8:SUB8 + 1], pc("subln"), 1.0 - lam_init, None, ALU.mult))

        def att_units():
            return [(hd, qt) for hd in range(4) for qt in range(5)]

        def att_pe(pe, g):
            maps = 2 - g
            units = att_units()
            x = f"att{g}_"

            def scores(u):
                hd, qt = units[u]
                for s in range(maps):
                    i = maps * u + s
                    if i >= 2:
                        pe.wait_ge(sg(x + "exp"), i - 1)
                    p0, p1 = (64 * s, 64 * s + 64) if g == 0 else (0, QK)
                    lhs = q_b[p0:p1, NT * hd + P * qt:NT * hd + P * qt + P]
                    key = lambda a, b: k_b[p0:p1, NK * hd + a:NK * hd + b]
                    if qt < 4:
                        mm(pe, pair_ap(i % 2, 0, 512), lhs, key(0, 512))
                        ins = mm(pe, pair_ap(i % 2, 512, 640), lhs, key(512, 640))
                    else:
                        ins = mm(pe, pair_ap(i % 2, 0, P), lhs, key(KP0, NK))
                    ins.then_inc(sg(x + "scores"), 1)

            def transposes(u):
                hd, qt = units[u]
                pe.wait_ge(sg(x + "probs"), u + 1)
                if u >= 1:
                    pe.wait_ge(sg(x + "turned_out"), u)
                pb = pr_b[:, (u % 2) * 2 * NT:(u % 2) * 2 * NT + NT]
                for kt in range(5 if qt < 4 else 1):
                    ins = pe.transpose(bank(4)[:, P * kt:P * kt + P] if kt < 4 else bank(5, P), pb[:, P * kt:P * kt + P],
                                       ident[:, :])
                ins.then_inc(sg(x + "turned"), 1)

            def values(hd):
                pe.wait_ge(sg(x + "turned_out"), 5 * hd + 5)
                if hd >= 1:
                    pe.wait_ge(sg(x + "out"), hd)
                for kt in range(5):
                    mm(pe, bank(6), v_b[:, 512 * kt + P * hd:512 * kt + P * hd + P],
                       dT_b[:, (hd % 2) * 2560 + 512 * kt:(hd % 2) * 2560 + 512 * kt + 512], kt == 0, kt == 4)
                mm(pe, bank(7, P), v_b[:, 512 * 5 + P * hd:512 * 5 + P * hd + P],
                   dTp_b[:, (hd % 2) * P:(hd % 2) * P + P]).then_inc(sg(x + "values"), 1)

            for u in range(len(units) + 2):
                if u < len(units):
                    scores(u)
                if 1 <= u <= len(units):
                    transposes(u - 1)
                if u >= 2 and units[u - 2][1] == 4:
                    values(units[u - 2][0])

        def att_act(act, g):
            maps = 2 - g
            units = att_units()
            x = f"att{g}_"
            for u in range(len(units) + 2):
                if u < len(units):
                    hd, qt = units[u]
                    w = NT if qt < 4 else P
                    for s in range(maps):
                        i = maps * u + s
                        act.wait_ge(sg(x + "max"), i + 1)
                        if u >= 2:
                            act.wait_ge(sg(x + "turned"), u - 1)
                        pb = pr_b[:, (u % 2) * 2 * NT + s * NT:(u % 2) * 2 * NT + s * NT + w]
                        c = 32 + (i % 4)
                        act.activation(pb, pair_ap(i % 2, 0, w), ACT.Exp, bias=small[:, c:c + 1],
                                       accum_out=small[:, c + 4:c + 5]).then_inc(sg(x + "exp"), 1)
                if 1 <= u <= len(units):
                    hd, qt = units[u - 1]
                    act.wait_ge(sg(x + "turned"), u)
                    if hd >= 2:
                        act.wait_ge(sg(x + "values"), hd - 1)
                    o = (hd % 2) * 2560
                    if qt < 4:
                        dst = dT_b[:, o:o + 2560].rearrange("p (k q) -> p k q", k=5)
                        act.activation(dst[:, 0:4, P * qt:P * qt + P], bank(4).rearrange("p (k q) -> p k q", k=4), ACT.Copy)
                        act.activation(dst[:, 4, P * qt:P * qt + P], bank(5, P), ACT.Copy).then_inc(sg(x + "turned_out"), 1)
                    else:
                        act.activation(dTp_b[:, (hd % 2) * P:(hd % 2) * P + P], bank(4, P), ACT.Copy)\
                            .then_inc(sg(x + "turned_out"), 1)
                if u >= 2 and units[u - 2][1] == 4:
                    hd = units[u - 2][0]
                    act.wait_ge(sg(x + "values"), hd + 1)
                    act.activation(merged(4 * g + hd, 0, NL), bank(6), ACT.Copy)
                    act.activation(merged(4 * g + hd, NL, NT), bank(7, P), ACT.Copy).then_inc(sg(x + "out"), 1)

        def att_dve(dve, g, ch):
            maps = 2 - g
            units = att_units()
            x = f"att{g}_"
            for u in range(len(units) + 1):
                if u < len(units):
                    w = NT if units[u][1] < 4 else P
                    for s in range(maps):
                        i = maps * u + s
                        dve.wait_ge(sg(x + "scores"), i + 1)
                        c = 32 + (i % 4)
                        dve.tensor_reduce(small[:, c:c + 1], pair_ap(i % 2, 0, w), AXX, ALU.max, negate=True)\
                            .then_inc(sg(x + "max"), 1)
                if u >= 1:
                    v = u - 1
                    w = NT if units[v][1] < 4 else P
                    dve.wait_ge(sg(x + "exp"), maps * v + maps)
                    pb = pr_b[:, (v % 2) * 2 * NT:(v % 2) * 2 * NT + w]
                    c = 36 + (maps * v) % 4
                    ch(dve.reciprocal(small[:, c + 4:c + 4 + maps], small[:, c:c + maps]))
                    if g == 0:
                        pb2 = pr_b[:, (v % 2) * 2 * NT + NT:(v % 2) * 2 * NT + NT + w]
                        ch(dve.tensor_tensor(small[:, c + 5:c + 6], small[:, c + 5:c + 6], small[:, NEGLAM:NEGLAM + 1], ALU.mult))
                        ch(dve.tensor_scalar(pb, pb, small[:, c + 4:c + 5], None, ALU.mult))
                        dve.scalar_tensor_tensor(pb, pb2, small[:, c + 5:c + 6], pb, ALU.mult, ALU.add)\
                            .then_inc(sg(x + "probs"), 1)
                    else:
                        dve.tensor_scalar(pb, pb, small[:, c + 4:c + 5], None, ALU.mult).then_inc(sg(x + "probs"), 1)

        subln_norms = plan_stats([
            ([(merged(t), P)], ones, 1.0 / P, 16, [(merged(t), merged(t), small[:, SUB8:SUB8 + 1], P)]) for t in range(4)])

        def up0_pe(pe):
            for hd in range(4):
                if hd >= 2:
                    pe.wait_ge(sg("u0_copied"), hd - 1)
                for a, b in SEG:
                    mm(pe, pair_ap(hd % 2, a, b, 0, QK), wuq[:, QK * hd:QK * hd + QK], tile(qd_b, 0, a, b), True, False)
                    ins = mm(pe, pair_ap(hd % 2, a, b, 0, QK), wuq[0:64, 384 + QK * hd:384 + QK * hd + QK],
                             qd_b[0:64, NT + a:NT + b], False, True)
                ins.then_inc(sg("u0_prod"), 1)
            for hd in range(4):
                pe.wait_ge(sg("u0_copied"), hd + 3)
                for a, b in ((0, 512), (512, NK)):
                    ins = mm(pe, pair_ap(hd % 2, a, b, 0, 64), wukv[:, 192 * hd:192 * hd + 64], ckv_b[:, a:b])
                ins.then_inc(sg("u0_prod"), 1)
            for tt in range(6):
                pe.wait_ge(sg("u0_copied"), tt + 7)
                vcols = wukv[:, :].rearrange("p (h c) -> p h c", h=4)[:, :, 64:192]
                mm(pe, bank(2 * (tt % 2)), ckv_b[:, P * tt:P * tt + P], vcols).then_inc(sg("u0_prod"), 1)
            for hd in range(4):
                pe.wait_ge(sg("u0_copied"), 14)
                if hd >= 2:
                    pe.wait_ge(sg("u0_roped"), hd - 1)
                mm(pe, bank(4 + hd % 2, 512, 0, QK), rotB[0:QK, 0:QK], q_b[0:QK, NT * hd:NT * hd + NL]).then_inc(sg("u0_rot"), 1)

        def up0_act(act):
            for hd in range(4):
                act.wait_ge(sg("u0_prod"), hd + 1)
                act.activation(q_b[0:QK, NT * hd:NT * hd + NT], pair_ap(hd % 2, 0, NT, 0, QK), ACT.Copy,
                               scale=QK ** -0.5).then_inc(sg("u0_copied"), 1)
            for hd in range(4):
                act.wait_ge(sg("u0_prod"), hd + 5)
                act.activation(k_b[0:64, NK * hd:NK * hd + NK], pair_ap(hd % 2, 0, NK, 0, 64), ACT.Copy)\
                    .then_inc(sg("u0_copied"), 1)
            for tt in range(6):
                act.wait_ge(sg("u0_prod"), tt + 9)
                act.activation(v_b[:, 512 * tt:512 * tt + 512], bank(2 * (tt % 2)), ACT.Copy).then_inc(sg("u0_copied"), 1)

        def up0_pool(pool):
            for hd in range(4):
                ins = pool.tensor_copy(k_b[64:QK, NK * hd:NK * hd + NK], kpe_b[64:QK, 0:NK])

        def up0_dve(dve, ch):
            for hd in range(4):
                dve.wait_ge(sg("u0_rot"), hd + 1)
                x = q_b[64:QK, NT * hd:NT * hd + NL]
                rope(dve, x, x, bank(4 + hd % 2, 512, 64, QK), cosB, sinB, ch, 64, QK, done=sg("u0_roped"))
                dve.wait_ge(sg("u0_roped"), hd + 1)

        CB = WN - 15 * NT - 3 * 512
        tk = area(CB)
        rkv_b, low_b = tk(12 * NT), tk(3 * NT)
        w2s, a2s, g2s = tk(512), tk(512), tk(512)
        r_ = lambda j, a=0, b=NT: tile(rkv_b, j, a, b)
        k_ = lambda j, a=0, b=NT: tile(rkv_b, 4 + j, a, b)
        v_ = lambda j, a=0, b=NT: tile(rkv_b, 8 + j, a, b)
        low = lambda i, a=0, b=NT: tile(low_b, i, a, b)
        tk = area(W0)
        zg_b, xs_b, bc_b, dq_b = tk(4 * NT), tk(4 * NT), tk(2 * NT), tk(NT)
        SSD0 = W0 + 11 * NT
        MUH, MU1, DSUM, KA1, EXPA = 64, 79, 94, 98, 102

        def mix1_pe(pe):
            n = 0
            for cols in (4, 4, 2, 4, 4, 4, 3):
                w = next_block(pe)
                for m in range(cols):
                    if n >= 3:
                        pe.wait_ge(sg("p1_done"), n - 2)
                    project(pe, n % 3, lambda k: w[:, k, P * m:P * m + P], hn, KT).then_inc(sg("p1_prod"), 1)
                    n += 1
                if cols == 2:
                    pe.wait_ge(sg("p1_done"), n - 2)
                    for i in range(4):
                        ins = project(pe, n % 3, lambda k: w[:, k, 256:264], hn, KT, p1=32 * i + 8, p0=32 * i)
                    ins.then_inc(sg("p1_prod"), 1)
                    n += 1
                released.append((sg("p1_prod"), n))

        def p1_dst(n):
            if n < 4:
                return zg_b, n, None
            if n < 8:
                return xs_b, n - 4, n - 4
            if n < 10:
                return bc_b, n - 8, n - 4
            if n < 23:
                return rkv_b, n - 11, n - 11
            return low_b, n - 23, n - 11

        def p1_taps(n):
            _, _, i = p1_dst(n)
            if n < 10:
                return pc("conv_w", i), pc("conv_w", 6 + i), pc("conv_w", 12 + i), pc("conv_b", i)
            return (small[:, MUH + i:MUH + i + 1], small[:, MU1 + i:MU1 + i + 1], small[:, MUH + i:MUH + i + 1], 0.0)

        CONV_N = [n for n in range(4, 26) if n != 10]

        def mix1_act(act):
            act.activation(small[0:40, EXPA:EXPA + 1], pc("A_log", 0, 1, 0, 40), ACT.Exp).then_inc(sg("exp_A"), 1)
            act.wait_ge(sg("mu_ready"), 1)
            for n in CONV_N:
                act.wait_ge(sg("p1_prod"), n + 1)
                buf, t, _ = p1_dst(n)
                _, w1, _, b = p1_taps(n)
                act.activation(tile(buf, t), pair_ap(n % 3), ACT.Identity, bias=b, scale=w1).then_inc(sg("p1_centre"), 1)
            act.wait_ge(sg("p1_done"), 26)
            for n in range(4, 10):
                buf, t, _ = p1_dst(n)
                act.activation(tile(buf, t), tile(buf, t), ACT.Silu)
            for t in range(4):
                act.activation(tile(zg_b, t), tile(zg_b, t), ACT.Silu).then_inc(sg("p1_silu"), 1)
            act.activation(low(0), low(0), ACT.Tanh)
            act.activation(low(2), low(2), ACT.Sigmoid).then_inc(sg("low_ready"), 1)

        def mix1_dve(dve, ch):
            ch(dve.tensor_scalar(small[:, MUH:MUH + 15], pc("mu", 0, 15), 0.5, None, ALU.mult))
            ch(dve.tensor_scalar(small[:, KA1:KA1 + 4], pc("k_a", 0, 4), -1.0, 1.0, ALU.mult, ALU.add))
            ch(dve.tensor_tensor(small[:, DSUM:DSUM + 4], pc("Dskip", 0, 4), pc("Dskip", 4, 4), ALU.add))
            dve.tensor_scalar(small[:, MU1:MU1 + 15], pc("mu", 0, 15), -1.0, 1.0, ALU.mult, ALU.add).then_inc(sg("mu_ready"), 1)
            ch(dve.memset(dq_b[:, :], 0.0))
            c = 0
            for n in range(26):
                if n < 4:
                    dve.wait_ge(sg("p1_prod"), n + 1)
                    dve.tensor_copy(tile(zg_b, n), pair_ap(n % 3)).then_inc(sg("p1_done"), 1)
                elif n == 10:
                    dve.wait_ge(sg("p1_prod"), n + 1)
                    for i in range(4):
                        ins = dve.tensor_scalar(dq_b[32 * i:32 * i + 8, :], pair_ap(n % 3, 0, NT, 32 * i, 32 * i + 8),
                                                pc("dt_bias", 0, 1, 32 * i, 32 * i + 8), None, ALU.add)
                        if i < 3:
                            ch(ins)
                    ins.then_inc(sg("p1_done"), 1)
                else:
                    c += 1
                    dve.wait_ge(sg("p1_centre"), c)
                    buf, t, _ = p1_dst(n)
                    w0, _, w2, _ = p1_taps(n)
                    conv3_dve(dve, lambda a, b: tile(buf, t, a, b), lambda a, b: pair_ap(n % 3, a, b), w0, w2, ch,
                              sg("p1_done"))
            dve.wait_ge(sg("p1_done"), 26)

        tk = area(SSD0)
        spa, dA, cumA = tk(NT), tk(NT), tk(NT)
        c_reset, c_selh, c_selr, c_gm = tk(NT), tk(8 * P), tk(4 * P), tk(2 * P)
        sst = tk(2 * 256)
        gm_b, btok, tokD, de_b = tk(2 * 256), tk(5 * P), tk(5 * 104), tk(16)
        assert SSD0 + 4 * NT + 14 * P + 512 + 512 + 640 + 520 + 16 <= CB
        tk = area(0)
        M_b, xdt_b, er_b, ct_b = tk(2 * 1024), tk(2 * 512), tk(2 * 512), tk(2 * 512)
        xde_b = work[:, SSD0:SSD0 + 2 * 512]
        xtok = merged_b[:, 0:5 * 512]
        UNITS = [(d, c) for s in range(4) for d, c in ((0, s), (1, 3 - s))] + [(0, 4), (1, 4)]

        def ssd_prep_dve(dve, ch):
            dve.wait_ge(sg("ssd_loaded"), 16 * 5)
            dve.scalar_tensor_tensor(spa[0:104, :], dq_b[0:104, :], -1.0, dq_b[0:104, :], ALU.mult, ALU.max).then_inc(sg("sp_abs"), 1)
            dve.wait_ge(sg("sp_ln"), 1)
            ch(dve.tensor_scalar(dq_b[0:104, :], dq_b[0:104, :], 0.0, None, ALU.max))
            ch(dve.tensor_tensor(dq_b[0:104, :], dq_b[0:104, :], spa[0:104, :], ALU.add))
            dve.wait_ge(sg("exp_A"), 1)
            ch(dve.tensor_scalar(dA[0:40, :], dq_b[0:40, :], small[0:40, EXPA:EXPA + 1], -1.0, ALU.mult, ALU.mult))
            ch(dve.tensor_tensor_scan(cumA[0:40, :], c_reset[0:40, :], dA[0:40, :], 0.0, ALU.mult, ALU.add))
            ch(dve.tensor_copy(dq_b[0:8, :], cumA[0:8, :]))
            ch(dve.tensor_tensor(dq_b[32:40, :], dA[32:40, :], cumA[32:40, :], ALU.subtract))
            c3 = lambda b, p0, p1: b[p0:p1, :].rearrange("p (c t) -> p c t", t=P)
            dve.tensor_tensor(c3(dq_b, 32, 40), c3(dq_b, 32, 40), c3(cumA, 32, 40)[:, :, P - 1:P].to_broadcast([8, 5, P]),
                              ALU.add).then_inc(sg("dq_ready"), 1)
            for t in range(4):
                ch(dve.tensor_scalar(merged(4 + t), tile(xs_b, t), small[:, DSUM + t:DSUM + t + 1], None, ALU.mult))

        def ssd_prep_act(act):
            act.wait_ge(sg("sp_abs"), 1)
            act.activation(spa[0:104, :], spa[0:104, :], ACT.Exp, scale=-1.0).then_inc(sg("sp_exp"), 1)
            act.wait_ge(sg("sp_exp"), 1)
            act.activation(spa[0:104, :], spa[0:104, :], ACT.Ln, bias=1.0).then_inc(sg("sp_ln"), 1)
            for c in range(5):
                act.wait_ge(sg("ssd_tok"), c + 1)
                b0 = 2 * (c % 2)
                act.activation(xtok[:, 512 * c:512 * c + 512], bank(b0), ACT.Copy)
                act.activation(btok[:, P * c:P * c + P], bank(b0 + 1)[:, 0:P], ACT.Copy)
                act.activation(tokD[:, 104 * c:104 * c + 104], bank(b0 + 1)[:, P:P + 104], ACT.Copy)\
                    .then_inc(sg("ssd_tokcp"), 1)

        def ssd_prep_pe(pe):
            pe.wait_ge(sg("dq_ready"), 1)
            pe.wait_ge(sg("p1_silu"), 4)
            for c in range(5):
                if c >= 2:
                    pe.wait_ge(sg("ssd_tokcp"), c - 1)
                b0 = 2 * (c % 2)
                for t in range(4):
                    pe.transpose(bank(b0)[:, P * t:P * t + P], tile(xs_b, t, P * c, P * c + P), ident[:, :])
                pe.transpose(bank(b0 + 1)[:, 0:P], bc_b[:, P * c:P * c + P], ident[:, :])
                pe.transpose(bank(b0 + 1)[:, P:P + 104], dq_b[0:104, P * c:P * c + P], ident[0:104, 0:104])\
                    .then_inc(sg("ssd_tok"), 1)
            pe.wait_ge(sg("ssd_tokcp"), 5)

        def ssd_pe(pe):
            def front(u):
                d, c = UNITS[u]
                if u >= 1:
                    pe.wait_ge(sg("ssd_seg"), u)
                    pe.wait_ge(sg("ssd_gm"), u)
                    pe.wait_ge(sg("ssd_er"), u)
                for g in range(2):
                    p0 = 64 * g
                    mm(pe, bank(3 + g, P), bc_b[p0:p0 + 64, P * c:P * c + P], bc_b[p0:p0 + 64, NT + P * c:NT + P * c + P])
                p0 = 32 * d
                rhs = dq_b[p0:p0 + 8, P * c:P * c + P]
                for hd in range(8):
                    mm(pe, ps_all[:, P * hd:P * hd + P], c_selh[p0:p0 + 8, P * hd:P * hd + P], rhs)
                for r in range(4):
                    ins = mm(pe, bank(2)[:, P * r:P * r + P], c_selr[p0:p0 + 8, P * r:P * r + P], rhs)
                ins.then_inc(sg("ssd_bc"), 1)

            def back(u):
                d, c = UNITS[u]
                x = u % 2
                pe.wait_ge(sg("ssd_m"), u + 1)
                if u >= 1:
                    pe.wait_ge(sg("ssd_state"), u)
                for g in range(2):
                    for r in range(4):
                        hd = 4 * g + r
                        out = bank(5 + g)[64 * (r % 2):64 * (r % 2) + 64, P * (r // 2):P * (r // 2) + P]
                        mm(pe, out, xdt_b[:, 512 * x + 64 * hd:512 * x + 64 * hd + 64],
                           M_b[:, 1024 * x + P * hd:1024 * x + P * hd + P], True, False)
                        ins = mm(pe, out, sst[64 * g:64 * g + 64, 256 * d + 64 * r:256 * d + 64 * r + 64],
                                 ct_b[64 * g:64 * g + 64, 512 * x + P * r:512 * x + P * r + P], False, True)
                ins.then_inc(sg("ssd_y"), 1)
                for g in range(2):
                    ins = mm(pe, bank(7)[64 * g:64 * g + 64, 0:256], btok[:, P * c + 64 * g:P * c + 64 * g + 64],
                             xde_b[:, 512 * x + 256 * g:512 * x + 256 * g + 256])
                ins.then_inc(sg("ssd_s"), 1)

            front(0)
            for u in range(10):
                if u + 1 < 10:
                    front(u + 1)
                back(u)

        def ssd_act(act):
            for u in range(10):
                x = u % 2
                act.wait_ge(sg("ssd_bc"), u + 1)
                if u >= 2:
                    act.wait_ge(sg("ssd_state"), u - 1)
                act.activation(er_b[:, 512 * x:512 * x + 512], bank(2), ACT.Exp).then_inc(sg("ssd_er"), 1)
                act.wait_ge(sg("ssd_seg"), u + 1)
                M = M_b[:, 1024 * x:1024 * x + 1024]
                act.activation(M, M, ACT.Exp)
                act.activation(de_b[:, 8 * x:8 * x + 8], de_b[:, 8 * x:8 * x + 8], ACT.Exp).then_inc(sg("ssd_exp"), 1)

        def ssd_dve(dve, ch):
            def front(u):
                d, c = UNITS[u]
                x = u % 2
                end = P - 1 if d == 0 else 0
                M3 = M_b[:, 1024 * x:1024 * x + 1024].rearrange("p (h t) -> p h t", t=P)
                bc3 = ps_all[:, 0:1024].rearrange("p (h t) -> p h t", t=P)
                Qt = tokD[:, 104 * c + 32 * d:104 * c + 32 * d + 8]
                dt = tokD[:, 104 * c + 64 + 32 * d:104 * c + 64 + 32 * d + 8]
                dve.wait_ge(sg("ssd_bc"), u + 1)
                if u >= 2:
                    dve.wait_ge(sg("ssd_s"), u - 1)
                ch(dve.tensor_tensor(M3, bc3, Qt.unsqueeze(2).to_broadcast([P, 8, P]), ALU.subtract))
                de = de_b[:, 8 * x:8 * x + 8]
                ch(dve.tensor_tensor(de, bc3[:, :, end], Qt, ALU.subtract))
                M = M_b[:, 1024 * x:1024 * x + 1024]
                dve.tensor_scalar(M, M, 0.0, None, ALU.min).then_inc(sg("ssd_seg"), 1)
                gp = ps_all[:, 1536:2560].rearrange("p (g t) -> p g t", t=512)[:, :, 0:P]
                gm = gm_b[:, 256 * x:256 * x + 256].rearrange("p (g t) -> p g t", t=P)
                dve.tensor_tensor(gm, gp, c_gm[:, P * d:P * d + P].unsqueeze(1).to_broadcast([P, 2, P]), ALU.mult)\
                    .then_inc(sg("ssd_gm"), 1)
                xt3 = lambda b, o: b[:, o:o + 512].rearrange("p (h t) -> p h t", t=64)
                xdt = xt3(xdt_b, 512 * x)
                ch(dve.tensor_tensor(xdt, xt3(xtok, 512 * c), dt.unsqueeze(2).to_broadcast([P, 8, 64]), ALU.mult))
                dve.wait_ge(sg("ssd_er"), u + 1)
                er3 = er_b[:, 512 * x:512 * x + 512].rearrange("p (r t) -> p r t", t=P)
                ct3 = ct_b[:, 512 * x:512 * x + 512].rearrange("p (r t) -> p r t", t=P)
                ch(dve.tensor_tensor(ct3, er3, bc_b[:, NT + P * c:NT + P * c + P].unsqueeze(1).to_broadcast([P, 4, P]), ALU.mult))
                dve.wait_ge(sg("ssd_exp"), u + 1)
                ch(dve.tensor_tensor(xt3(xde_b, 512 * x), xdt, de.unsqueeze(2).to_broadcast([P, 8, 64]), ALU.mult))
                for g in range(2):
                    ins = dve.tensor_tensor(M3[:, 4 * g:4 * g + 4, :], M3[:, 4 * g:4 * g + 4, :],
                                            gm[:, g:g + 1, :].to_broadcast([P, 4, P]), ALU.mult)
                    if g == 0:
                        ch(ins)
                ins.then_inc(sg("ssd_m"), 1)

            def back(u):
                d, c = UNITS[u]
                x = u % 2
                end = P - 1 if d == 0 else 0
                dve.wait_ge(sg("ssd_y"), u + 1)
                for g in range(2):
                    y3 = merged_b[:, (4 + 2 * g) * NT:(6 + 2 * g) * NT].rearrange("p (t n) -> p t n", n=NT)[:, :, P * c:P * c + P]
                    ch(dve.tensor_tensor(y3, y3, bank(5 + g, 256).rearrange("p (t n) -> p t n", n=P), ALU.add))
                dve.wait_ge(sg("ssd_s"), u + 1)
                S3 = sst[:, 256 * d:256 * d + 256].rearrange("p (r t) -> p r t", t=64)
                er3 = er_b[:, 512 * x:512 * x + 512].rearrange("p (r t) -> p r t", t=P)
                ch(dve.tensor_tensor(S3, S3, er3[:, :, end:end + 1].to_broadcast([P, 4, 64]), ALU.mult))
                if u in (6, 7):
                    dve.memset(sst[:, 256 * d:256 * d + 256], 0.0).then_inc(sg("ssd_state"), 1)
                else:
                    dve.tensor_tensor(S3, S3, bank(7, 256).rearrange("p (r t) -> p r t", t=64), ALU.add)\
                        .then_inc(sg("ssd_state"), 1)

            for u in range(11):
                if u < 10:
                    front(u)
                if u >= 1:
                    back(u - 1)
            dve.wait_ge(sg("ssd_state"), 10)
            for t in range(4):
                ins = dve.tensor_tensor(merged(4 + t), merged(4 + t), tile(zg_b, t), ALU.mult)
            ins.then_inc(sg("od_gated"), 1)

        od_norm = plan_stats([([(merged(4 + t), P) for t in range(4)], ones, 1.0 / 512, 16,
                               [(merged(4 + t), merged(4 + t), pc("gnorm", t), P) for t in range(4)])])

        tk = area(0)
        kk_b, sw_b, ag_b, x1_b, x2_b, er1, ea1, eb1 = (tk(NT) for _ in range(8))
        TQ = 3584
        quad_b = work[:, 0:2 * TQ]
        tk = area(2 * TQ)
        AR_b, BK_b = tk(2 * 1280), tk(2 * 1280)
        bkt_b, vt_b, u0_b, u_b = tk(2 * 512), tk(NT), tk(256), tk(256)
        st_b, ssc_b, s0_b, sf_b = tk(P), tk(P), tk(512), tk(512)
        c_ar, c_lev, c_reset2 = tk(4 * P), tk(14 * P), tk(NT)
        wk = tk(32)
        ARv = AR_b[:, :].rearrange("p (d c x t) -> p d c x t", d=2, c=5, x=2)
        BKv = BK_b[:, :].rearrange("p (d c x t) -> p d c x t", d=2, c=5, x=2)
        LBo, LKo, To, Xo, Vo = 0, 1024, 2048, 2560, 3072
        qv = lambda a, o, n=512: quad_b[:, TQ * a + o:TQ * a + o + n]
        GROUPS = ((0, 1), (2, 3), (4,))
        chunk_of = lambda s, d: 4 if s == 4 else (s if d == 0 else 3 - s)

        kk_norms = [plan_stats([([(kk_b[:, :], P)], blk, 1.0, 17, [(kk_b[:, :], kk_b[:, :], small[:, 19:20], P)])])
                    for j in range(4)]

        def wkv_prep_pe(pe, j):
            stats_pe(pe, kk_norms[j])
            for d in range(2):
                n = 2 * j + d
                if d == 1:
                    pe.wait_ge(sg("wkv_sig"), n)
                p0 = 64 * d
                for a, b in SEG:
                    mm(pe, pair_ap(0, a, b), w2s[p0:p0 + 64, P * j:P * j + P], low_b[p0:p0 + 64, a:b])
                    ins = mm(pe, pair_ap(1, a, b), a2s[p0:p0 + 64, P * j:P * j + P], low_b[p0:p0 + 64, NT + a:NT + b])
                ins.then_inc(sg("wkv_lora"), 1)
            for c in range(5):
                ins = pe.transpose(ps_all[:, 2048 + P * c:2048 + P * c + P], v_(j, P * c, P * c + P), ident[:, :])
            ins.then_inc(sg("wkv_vt"), 1)

        def wkv_prep_act(act, j):
            stats_act(act, kk_norms[j])
            for d in range(2):
                n = 2 * j + d
                act.wait_ge(sg("wkv_lora"), n + 1)
                if d == 1:
                    act.wait_ge(sg("wkv_prep"), n)
                act.activation(sw_b[:, :], pair_ap(0), ACT.Sigmoid, bias=pc("w0", 4 * d + j))
                act.activation(ag_b[:, :], pair_ap(1), ACT.Sigmoid, bias=pc("a0", 4 * d + j)).then_inc(sg("wkv_sig"), 1)
                if d == 0:
                    act.wait_ge(sg("wkv_vt"), j + 1)
                    act.activation(vt_b[:, :], ps_all[:, 2048:2048 + NT], ACT.Copy).then_inc(sg("wkv_vtcp"), 1)
                act.wait_ge(sg("wkv_cum"), n + 1)
                ex = lambda out, in_, sign: act.activation(out[:, :], in_[:, :], ACT.Exp, scale=sign * DEC)
                if d == 0:
                    ex(er1, x2_b, -1)
                    ex(ea1, x1_b, -1)
                    ex(eb1, x2_b, 1).then_inc(sg("wkv_exp"), 1)
                else:
                    ex(er1, x1_b, 1)
                    ex(ea1, x2_b, 1)
                    ex(eb1, x1_b, -1).then_inc(sg("wkv_exp"), 1)

        def wkv_prep_dve(dve, j, ch):
            dve.tensor_scalar(kk_b[:, :], k_(j), pc("k_k", j), None, ALU.mult).then_inc(sg("wkv_kx"), 1)
            stats_dve(dve, kk_norms[j], ch)
            c3 = lambda b: b[:, :].rearrange("p (c t) -> p c t", t=P)
            for d in range(2):
                n = 2 * j + d
                dve.wait_ge(sg("wkv_sig"), n + 1)
                ch(dve.tensor_tensor_scan(x1_b[:, :], c_reset2[:, :], sw_b[:, :], 0.0, ALU.mult, ALU.add))
                ch(dve.tensor_tensor(c3(x2_b), c3(x1_b), c3(x1_b)[:, :, 63:64].to_broadcast([P, 5, P]), ALU.subtract))
                dve.tensor_tensor(x1_b[:, :], x2_b[:, :], sw_b[:, :], ALU.subtract).then_inc(sg("wkv_cum"), 1)
                dve.wait_ge(sg("wkv_cum"), n + 1)
                ch(dve.tensor_scalar(sw_b[:, :], ag_b[:, :], pc("k_a", j), small[:, KA1 + j:KA1 + j + 1], ALU.mult, ALU.add))
                ch(dve.tensor_tensor(sw_b[:, :], sw_b[:, :], k_(j), ALU.mult))
                ch(dve.tensor_tensor(ag_b[:, :], ag_b[:, :], kk_b[:, :], ALU.mult))
                dve.wait_ge(sg("wkv_exp"), n + 1)
                ch(dve.tensor_tensor(BKv[:, d, :, 1, :], c3(sw_b), c3(eb1), ALU.mult))
                ch(dve.tensor_tensor(BKv[:, d, :, 0, :], c3(ag_b), c3(eb1), ALU.mult))
                ch(dve.scalar_tensor_tensor(ARv[:, d, :, 0, :], c3(kk_b), -1.0, c3(ea1), ALU.mult, ALU.mult))
                ch(dve.tensor_tensor(ARv[:, d, :, 1, :], r_(j).rearrange("p (c t) -> p c t", t=P), c3(er1), ALU.mult))
                first, last = (0, P - 1) if d == 0 else (P - 1, 0)
                ch(dve.reciprocal(wk[:, 5 * d:5 * d + 5], c3(ea1)[:, :, first]))
                dve.tensor_copy(wk[:, 10 + 5 * d:15 + 5 * d], c3(er1)[:, :, last]).then_inc(sg("wkv_prep"), 1)
            dve.wait_ge(sg("wkv_prep"), 2 * j + 2)

        cnt = {}

        def step(who, name):
            cnt[who, name] = cnt.get((who, name), 0) + 1
            return cnt[who, name]

        def wkv_solve_pe(pe, j, g):
            grp = GROUPS[g]
            for a, s in enumerate(grp):
                if a == 0:
                    pe.wait_ge(sg("wkv_prep"), 2 * j + 2)
                    if s > 0:
                        pe.wait_ge(sg("wkv_state"), 5 * j + s)
                    if g == 0:
                        pe.wait_ge(sg("wkv_vtcp"), j + 1)
                else:
                    pe.wait_ge(sg("wkv_masked"), step("pe", "masked"))
                for e in range(2):
                    p0 = 64 * e
                    for d in range(2):
                        c = chunk_of(s, d)
                        rhs = ARv[p0:p0 + 64, d, c, :, :]
                        mm(pe, bank(e)[:, 256 * d:256 * d + 256], BKv[p0:p0 + 64, d, c, 0, :], rhs)
                        ins = mm(pe, bank(2 + e)[:, 256 * d:256 * d + 256], BKv[p0:p0 + 64, d, c, 1, :], rhs)
                ins.then_inc(sg("wkv_gram"), 1)
                for d in range(2):
                    for x in range(2):
                        i = 2 * d + x
                        ins = pe.transpose(bank(4 + 2 * a)[:, P * i:P * i + P], BKv[:, d, chunk_of(s, d), x, :], ident[:, :])
                ins.then_inc(sg("wkv_bkt"), 1)
            if len(grp) == 1 or True:
                pe.wait_ge(sg("wkv_masked"), step("pe", "masked"))
            for lev in range(7):
                for a, s in enumerate(grp):
                    if lev == 0:
                        pe.wait_ge(sg("wkv_x0"), step("pe", "x0"))
                        pe.wait_ge(sg("wkv_bkcp"), step("pe", "bkcp"))
                        src = qv(a, Xo)
                    else:
                        pe.wait_ge(sg("wkv_tfull"), step("pe", "tfull"))
                        src = qv(a, To)
                    for i in range(4):
                        ins = pe.transpose(bank(4 + 2 * a)[:, P * i:P * i + P], src[:, P * i:P * i + P], ident[:, :])
                    ins.then_inc(sg("wkv_turn"), 1)
                for a, s in enumerate(grp):
                    pe.wait_ge(sg("wkv_turned"), step("pe", "turned"))
                    if lev < 6:
                        for i in range(4):
                            e, d = i // 2, i % 2
                            ins = mm(pe, bank(4 + 2 * a)[:, P * i:P * i + P], qv(a, LBo + 256 * i, P), qv(a, To + P * i, P))
                        ins.then_inc(sg("wkv_lt"), 1)
                if lev < 6:
                    for a, s in enumerate(grp):
                        pe.wait_ge(sg("wkv_vm"), step("pe", "vm"))
                        for i in range(4):
                            ins = mm(pe, bank(5 + 2 * a)[:, P * i:P * i + P], qv(a, Xo + P * i, P), qv(a, Vo + P * i, P))
                        ins.then_inc(sg("wkv_tv"), 1)

        def wkv_solve_act(act, j, g):
            grp = GROUPS[g]
            for a, s in enumerate(grp):
                act.wait_ge(sg("wkv_bkt"), step("act", "bkt"))
                act.activation(bkt_b[:, 512 * a:512 * a + 512], bank(4 + 2 * a), ACT.Copy).then_inc(sg("wkv_bkcp"), 1)
            for lev in range(7):
                for a, s in enumerate(grp):
                    act.wait_ge(sg("wkv_turn"), step("act", "turn"))
                    act.activation(qv(a, To if lev == 0 else Xo), bank(4 + 2 * a), ACT.Copy).then_inc(sg("wkv_turned"), 1)

        def wkv_solve_dve(dve, j, g, ch):
            grp = GROUPS[g]
            v4 = lambda ap: ap.rearrange("p (e d t) -> p e d t", e=2, d=2)
            lev_mask = lambda l: c_lev[:, 256 * l:256 * l + 256].rearrange("p (d t) -> p d t", d=2)\
                .unsqueeze(1).to_broadcast([P, 2, 2, P])
            for a, s in enumerate(grp):
                dve.wait_ge(sg("wkv_gram"), step("dve", "gram"))
                for b in range(4):
                    o = (LBo if b < 2 else LKo) + 512 * (b % 2)
                    ins = dve.tensor_tensor(qv(a, o), bank(b), c_ar[:, :], ALU.mult)
                    if b < 3:
                        ch(ins)
                ins.then_inc(sg("wkv_masked"), 1)
                dve.wait_ge(sg("wkv_masked"), step("dve", "masked"))
                lab = qv(a, LBo, 1024).rearrange("p (e d x t) -> p e d x t", e=2, d=2, x=2)[:, :, :, 0, :]
                for e in range(2):
                    ch(dve.tensor_tensor(v4(qv(a, Vo))[:, e], lab[:, e], lev_mask(0)[:, e], ALU.mult))
                v3 = lambda ap: ap.rearrange("p (i t) -> p i t", i=4)
                dve.tensor_tensor(v3(qv(a, Xo)), v3(qv(a, Vo)), ident[:, :].unsqueeze(1).to_broadcast([P, 4, P]), ALU.add)\
                    .then_inc(sg("wkv_x0"), 1)
            for lev in range(1, 7):
                for a, s in enumerate(grp):
                    dve.wait_ge(sg("wkv_lt"), step("dve", "lt"))
                    for e in range(2):
                        ins = dve.tensor_tensor(v4(qv(a, Vo))[:, e], v4(bank(4 + 2 * a))[:, e], lev_mask(lev)[:, e], ALU.mult)
                        if e == 0:
                            ch(ins)
                    ins.then_inc(sg("wkv_vm"), 1)
                for a, s in enumerate(grp):
                    dve.wait_ge(sg("wkv_tv"), step("dve", "tv"))
                    dve.tensor_tensor(qv(a, To), qv(a, To), bank(5 + 2 * a), ALU.add).then_inc(sg("wkv_tfull"), 1)

        def wkv_apply_pe(pe, j, g):
            for a, s in enumerate(GROUPS[g]):
                pe.wait_ge(sg("wkv_ss"), step("pe", "ss"))
                lk = lambda e, d, x: qv(a, LKo + 512 * e + 256 * d + P * x, P)
                for e in range(2):
                    for d in range(2):
                        c = chunk_of(s, d)
                        out = bank(e)[:, 64 * d:64 * d + 64]
                        mm(pe, out, ARv[64 * e:64 * e + 64, d, c, 0, :], ssc_b[64 * e:64 * e + 64, 64 * d:64 * d + 64], True, False)
                        ins = mm(pe, out, lk(e, d, 0), vt_b[:, P * c + 64 * e:P * c + 64 * e + 64], False, True)
                ins.then_inc(sg("wkv_u0"), 1)
                pe.wait_ge(sg("wkv_u0cp"), step("pe", "u0cp"))
                for i in range(4):
                    ins = mm(pe, bank(2)[:, 64 * i:64 * i + 64], qv(a, Xo + P * i, P), u0_b[:, 64 * i:64 * i + 64])
                ins.then_inc(sg("wkv_u"), 1)
                pe.wait_ge(sg("wkv_ucp"), step("pe", "ucp"))
                for e in range(2):
                    for d in range(2):
                        c, i = chunk_of(s, d), 2 * e + d
                        out = bank(e)[64 * e:64 * e + 64, P * d:P * d + P]
                        vt = vt_b[:, P * c + 64 * e:P * c + 64 * e + 64]
                        mm(pe, out, ssc_b[64 * e:64 * e + 64, 64 * d:64 * d + 64], ARv[64 * e:64 * e + 64, d, c, 1, :], True, False)
                        mm(pe, out, u_b[:, 64 * i:64 * i + 64], qv(a, LBo + 256 * i + P, P), False, False)
                        mm(pe, out, vt, lk(e, d, 1), False, True)
                        so = bank(3)[64 * e:64 * e + 64, 64 * d:64 * d + 64]
                        bk = lambda x: bkt_b[:, 512 * a + 256 * d + P * x + 64 * e:512 * a + 256 * d + P * x + 64 * e + 64]
                        mm(pe, so, bk(0), u_b[:, 64 * i:64 * i + 64], True, False)
                        ins = mm(pe, so, bk(1), vt, False, True)
                ins.then_inc(sg("wkv_y"), 1)

        def wkv_apply_act(act, j, g):
            for a, s in enumerate(GROUPS[g]):
                act.wait_ge(sg("wkv_u0"), step("act", "u0"))
                act.activation(u0_b[:, :].rearrange("p (e x) -> p e x", e=2),
                               ps_all[:, 0:1024].rearrange("p (e x) -> p e x", e=2)[:, :, 0:P], ACT.Copy).then_inc(sg("wkv_u0cp"), 1)
                act.wait_ge(sg("wkv_u"), step("act", "u"))
                act.activation(u_b[:, :], bank(2, 256), ACT.Copy).then_inc(sg("wkv_ucp"), 1)

        def wkv_apply_dve(dve, j, g, ch):
            for a, s in enumerate(GROUPS[g]):
                for d in range(2):
                    c = chunk_of(s, d)
                    dst = ssc_b[:, 64 * d:64 * d + 64]
                    if s == 4:
                        ins = dve.memset(dst, 0.0)
                    else:
                        src = s0_b[:, P * j + 64 * d:P * j + 64 * d + 64] if s == 0 else st_b[:, 64 * d:64 * d + 64]
                        ins = dve.tensor_scalar(dst, src, wk[:, 5 * d + c:5 * d + c + 1], None, ALU.mult)
                    if d == 0:
                        ch(ins)
                ins.then_inc(sg("wkv_ss"), 1)
                dve.wait_ge(sg("wkv_y"), step("dve", "y"))
                for e in range(2):
                    for d in range(2):
                        c = chunk_of(s, d)
                        y = merged(j, P * c, P * c + P)[64 * e:64 * e + 64]
                        ch(dve.tensor_tensor(y, y, bank(e)[64 * e:64 * e + 64, P * d:P * d + P], ALU.add))
                ch(dve.tensor_tensor(ssc_b[:, :], ssc_b[:, :], bank(3, P), ALU.add))
                for d in range(2):
                    c = chunk_of(s, d)
                    dst = sf_b[:, P * j + 64 * d:P * j + 64 * d + 64] if s == 4 else st_b[:, 64 * d:64 * d + 64]
                    ins = dve.tensor_scalar(dst, ssc_b[:, 64 * d:64 * d + 64], wk[:, 10 + 5 * d + c:11 + 5 * d + c], None, ALU.mult)
                    if d == 0:
                        ch(ins)
                ins.then_inc(sg("wkv_state"), 1)
                dve.wait_ge(sg("wkv_state"), 5 * j + s + 1)

        y_norms = plan_stats([([(merged(j), P)], blk, 1.0 / 64, 18, [(merged(j), merged(j), pc("ln_w", j), P)])
                              for j in range(4)])

        def post_pe(pe):
            for j in range(4):
                if j >= 1:
                    pe.wait_ge(sg("y_centred"), j)
                for a, b in SEG:
                    ins = mm(pe, pair_ap(0, a, b), blk[:, :], merged(j, a, b))
                ins.then_inc(sg("y_mean"), 1)
            pe.wait_ge(sg("y_centred"), 4)
            stats_pe(pe, y_norms)
            for j in range(4):
                pe.wait_ge(sg("rk_ready"), j + 1)
                if j >= 1:
                    pe.wait_ge(sg("y_gated"), j)
                for a, b in SEG:
                    mm(pe, pair_ap(0, a, b), blk[:, :], tile(kk_b, 0, a, b))
                    ins = mm(pe, pair_ap(1, a, b), g2s[:, P * j:P * j + P], low(2, a, b))
                ins.then_inc(sg("bonus"), 1)

        def post_dve(dve, ch):
            for j in range(4):
                dve.wait_ge(sg("y_mean"), j + 1)
                dve.scalar_tensor_tensor(merged(j), pair_ap(0), -1.0 / 64, merged(j), ALU.mult, ALU.add)\
                    .then_inc(sg("y_centred"), 1)
            dve.wait_ge(sg("y_centred"), 4)
            stats_dve(dve, y_norms, ch)
            for j in range(4):
                ch(dve.tensor_scalar(merged(j), merged(j), pc("ln_b", j), None, ALU.add))
                dve.scalar_tensor_tensor(kk_b[:, :], r_(j), pc("r_k", j), k_(j), ALU.mult, ALU.mult)\
                    .then_inc(sg("rk_ready"), 1)
                dve.wait_ge(sg("bonus"), j + 1)
                ch(dve.tensor_tensor(kk_b[:, :], pair_ap(0), v_(j), ALU.mult))
                ch(dve.tensor_tensor(merged(j), merged(j), kk_b[:, :], ALU.add))
                dve.tensor_tensor(merged(j), merged(j), pair_ap(1), ALU.mult).then_inc(sg("y_gated"), 1)
            dve.wait_ge(sg("y_gated"), 4)

        block = ctx.enter_context(nc.Block())
        npar_loads = 5

        @block.tensor
        def _(pe):
            ada_pe(pe, 0)
            norm_pe(pe, 0)
            pe.wait_ge(sg("hn_ready"), 8)
            mix0_pe(pe)
            leave_phase(pe, PE_)
            att_pe(pe, 0)
            stats_pe(pe, subln_norms)
            leave_phase(pe, PE_)
            up0_pe(pe)
            leave_phase(pe, PE_)
            att_pe(pe, 1)
            leave_phase(pe, PE_)
            wout_pe(pe, 0)
            norm_pe(pe, 1)
            pe.wait_ge(sg("hn_ready"), 16)
            ffn_pe(pe, 0)
            leave_phase(pe, PE_)
            ada_pe(pe, 1)
            norm_pe(pe, 2)
            pe.wait_ge(sg("hn_ready"), 24)
            mix1_pe(pe)
            leave_phase(pe, PE_)
            ssd_prep_pe(pe)
            ssd_pe(pe)
            pe.wait_ge(sg("od_gated"), 1)
            stats_pe(pe, od_norm)
            leave_phase(pe, PE_)
            for j in range(4):
                wkv_prep_pe(pe, j)
                leave_phase(pe, PE_)
                for g in range(3):
                    wkv_solve_pe(pe, j, g)
                    wkv_apply_pe(pe, j, g)
                leave_phase(pe, PE_)
            post_pe(pe)
            leave_phase(pe, PE_)
            wout_pe(pe, 16)
            norm_pe(pe, 3)
            pe.wait_ge(sg("hn_ready"), 32)
            ffn_pe(pe, 1)
            norm_pe(pe, 4)

        @block.scalar
        def _(act):
            act.wait_ge(sg("par_loaded"), 16 * npar_loads)
            act.activation(small[:, 0:16], pc("cond", 0, 16), ACT.Silu).then_inc(sg("cond_silu"), 1)
            act.wait_ge(sg("eps_ready"), 1)
            norm_act(act, 0, lambda t, c: mod(0, 0, t, c))
            mix0_act(act)
            leave_phase(act, ACT_)
            att_act(act, 0)
            act.wait_ge(sg("att0_out"), 4)
            stats_act(act, subln_norms)
            leave_phase(act, ACT_)
            up0_act(act)
            leave_phase(act, ACT_)
            att_act(act, 1)
            leave_phase(act, ACT_)
            act.wait_ge(sg("res_done"), 8)
            norm_act(act, 1, lambda t, c: mod(0, 3, t, c))
            ffn_act(act, 0)
            leave_phase(act, ACT_)
            norm_act(act, 2, lambda t, c: mod(1, 0, t, c))
            mix1_act(act)
            leave_phase(act, ACT_)
            ssd_prep_act(act)
            ssd_act(act)
            act.wait_ge(sg("od_gated"), 1)
            stats_act(act, od_norm)
            leave_phase(act, ACT_)
            for j in range(4):
                act.wait_ge(sg("wkv_kx"), j + 1)
                wkv_prep_act(act, j)
                leave_phase(act, ACT_)
                for g in range(3):
                    wkv_solve_act(act, j, g)
                    wkv_apply_act(act, j, g)
                leave_phase(act, ACT_)
            act.wait_ge(sg("y_centred"), 4)
            stats_act(act, y_norms)
            leave_phase(act, ACT_)
            act.wait_ge(sg("res_done"), 24)
            norm_act(act, 3, lambda t, c: mod(1, 3, t, c))
            ffn_act(act, 1)
            act.wait_ge(sg("res_done"), 32)
            norm_act(act, 4, None)

        @block.vector
        def _(dve):
            ch = Chain(dve, "vector_chain")
            for col, val in ((16, EPS), (17, 1e-12), (18, 64e-5), (19, 1.0)):
                ch(dve.memset(small[:, col:col + 1], val))
            dve.memset(ones[:, :], 1.0).then_inc(sg("eps_ready"), 1)
            dve.wait_ge(sg("par_loaded"), 16 * npar_loads)
            ada_dve(dve, 0, ch)
            norm_dve(dve, 0, g_eff(0), ch)
            mix0_dve(dve, ch)
            leave_phase(dve, DVE_)
            att_dve(dve, 0, ch)
            stats_dve(dve, subln_norms, ch)
            leave_phase(dve, DVE_)
            up0_dve(dve, ch)
            leave_phase(dve, DVE_)
            att_dve(dve, 1, ch)
            leave_phase(dve, DVE_)
            residual_dve(dve, 0, lambda t, c: mod(0, 2, t, c), ch)
            norm_dve(dve, 1, g_eff(1), ch)
            ffn_dve(dve, 0, ch)
            leave_phase(dve, DVE_)
            ada_dve(dve, 1, ch)
            norm_dve(dve, 2, g_eff(2), ch)
            mix1_dve(dve, ch)
            leave_phase(dve, DVE_)
            ssd_prep_dve(dve, ch)
            ssd_dve(dve, ch)
            stats_dve(dve, od_norm, ch)
            leave_phase(dve, DVE_)
            for j in range(4):
                if j == 0:
                    dve.wait_ge(sg("wkv_loaded"), 16 * 4)
                    ch(dve.memset(merged_b[:, 0:4 * NT], 0.0))
                wkv_prep_dve(dve, j, ch)
                leave_phase(dve, DVE_)
                for g in range(3):
                    wkv_solve_dve(dve, j, g, ch)
                    wkv_apply_dve(dve, j, g, ch)
                leave_phase(dve, DVE_)
            post_dve(dve, ch)
            leave_phase(dve, DVE_)
            residual_dve(dve, 16, lambda t, c: mod(1, 2, t, c), ch)
            norm_dve(dve, 3, g_eff(3), ch)
            ffn_dve(dve, 1, ch)
            norm_dve(dve, 4, lambda t, c: pc("norm_f", t), ch)

        outs = [0]

        @block.gpsimd
        def _(pool):
            con = t_in["const"]
            cs = lambda name, p0=0, p1=P: con[p0:p1, CC[name][0]:CC[name][0] + CC[name][1]]

            def store(dst, src):
                pool.dma_start(dst, src).then_inc(sg("stored"), 16)
                outs[0] += 1
            pool.dma_start(par[:, :], t_in["params"]).then_inc(sg("par_loaded"), 16)
            pool.dma_start(h_b[:, :].rearrange("p (t n) -> p t n", n=NT), t_in["xT"].rearrange("(t p) n -> p t n", p=P))\
                .then_inc(sg("par_loaded"), 16)
            pool.dma_start(ident[:, :], cs("ident")).then_inc(sg("par_loaded"), 16)
            pool.dma_start(blk[:, :], cs("blk")).then_inc(sg("par_loaded"), 16)
            pool.dma_start(cosA, cs("cosA")).then_inc(sg("par_loaded"), 16)
            for dst, src in ((sinA, cs("sinA")), (cosB, cs("cosB")), (sinB, cs("sinB")), (rotA, cs("rotA")), (rotB, cs("rotB")),
                             (wuq[:, 0:384], t_in["l0_w_uq"][0:P, :]), (wuq[0:64, 384:768], t_in["l0_w_uq"][P:QL, :]),
                             (wukv, t_in["l0_w_ukv"]),
                             (v_b[:, 2048:2560].rearrange("p (h d) -> p h d", h=4), t_in["cv"].rearrange("h t d -> t h d")),
                             (ckv_b[:, NL:NT], t_in["cckvT"]), (kpe_b[64:QK, NL:NT], t_in["ckpeT"])):
                pool.dma_start(dst, src).then_inc(sg("m0_loaded"), 16)
            pool.dma_start(k_b[:, :].rearrange("p (h n) -> p h n", h=4)[:, :, NL:NT], t_in["ckT"].rearrange("h d t -> d h t"))\
                .then_inc(sg("m0_loaded"), 16)
            pool.dma_start(rt_b[:, 0:P], cs("ident")).then_inc(sg("m0_loaded"), 16)
            pool.dma_start(rt_b[:, P:2 * P], cs("ident")).then_inc(sg("m0_loaded"), 16)
            leave_phase(pool, POOL_)
            store(t_out["k"].rearrange("h d t -> d h t"), k_b[:, :].rearrange("p (h n) -> p h n", h=4)[:, :, KP0:NK])
            store(t_out["v"], v_b[:, 2560:3072])
            store(t_out["ckv"], ckv_b[:, KP0:NK])
            store(t_out["kpe"], kpe_b[64:QK, KP0:NK])
            pool.wait_ge(sg("stored"), 16 * outs[0])
            leave_phase(pool, POOL_)
            up0_pool(pool)
            leave_phase(pool, POOL_)
            leave_phase(pool, POOL_)
            leave_phase(pool, POOL_)
            for dst, src in ((c_reset, cs("reset")), (c_selh, cs("selh")), (c_selr, cs("selr")), (c_gm, cs("gmask")),
                             (sst, t_in["ssm0"])):
                pool.dma_start(dst, src).then_inc(sg("ssd_loaded"), 16)
            for dst, src in ((w2s, t_in["l1_w2"].rearrange("i r n -> (i r) n")), (a2s, t_in["l1_a2"].rearrange("i r n -> (i r) n")),
                             (g2s, t_in["l1_g2"])):
                pool.dma_start(dst, src).then_inc(sg("lora_loaded"), 16)
            pool.wait_ge(sg("lora_loaded"), 48)
            leave_phase(pool, POOL_)
            leave_phase(pool, POOL_)
            store(t_out["ssm"], sst)
            pool.wait_ge(sg("stored"), 16 * outs[0])
            for dst, src in ((c_ar, cs("armask")), (c_lev, cs("lev")), (c_reset2, cs("reset")), (s0_b, t_in["wkv0"])):
                pool.dma_start(dst, src).then_inc(sg("wkv_loaded"), 16)
            for j in range(4):
                leave_phase(pool, POOL_)
                leave_phase(pool, POOL_)
            store(t_out["wkv"], sf_b)
            pool.wait_ge(sg("stored"), 16 * outs[0])
            leave_phase(pool, POOL_)
            pool.wait_ge(sg("norm_scaled"), 40)
            store(t_out["yT"].rearrange("(t p) n -> p t n", p=P), hn_b.rearrange("p (t n) -> p t n", n=NT))
            pool.wait_ge(sg("stored"), 16 * outs[0])

        @block.sync
        def _(sp):
            for n, (_, parts) in enumerate(blocks):
                if n >= RING:
                    sp.wait_ge(*released[n - RING])
                for src, kt, c0, width, row in parts:
                    dst = ring[:, (n % RING) * SLOT:(n % RING) * SLOT + kt * row].rearrange("p (k c) -> p k c", k=kt)
                    sp.dma_start(dst[:, :, c0:c0 + width], src).then_inc(full[n % RING], 16)


def pack_columns(v):
    return np.ascontiguousarray(np.asarray(v).reshape(-1, P).T)


def shape_constants():
    at, n = const_columns()
    out = np.zeros((P, n), np.float32)

    def put(name, a):
        c, w = at[name]
        a = np.asarray(a, np.float32)
        out[:a.shape[0], c:c + w] = a.reshape(a.shape[0], w)
    i = np.arange(P)
    put("ident", np.eye(P))
    put("blk", (i[:, None] // 64 == i[None, :] // 64))
    pos = np.arange(NL)
    row, col = (pos // 64).astype(np.float32), (pos % 64).astype(np.float32)

    def tables(dim, reps, offset):
        quarter = dim // 4
        inv = (np.float32(10000.0) ** (-np.arange(quarter, dtype=np.float32) / np.float32(quarter))).astype(np.float32)
        cos, sin = np.zeros((P, NL), np.float32), np.zeros((P, NL), np.float32)
        rot = np.zeros((P, P), np.float32)
        for r in range(reps):
            for part, ps in enumerate((row, col)):
                for m in range(quarter):
                    ang = (ps * inv[m]).astype(np.float32)
                    a = offset + r * dim + part * 2 * quarter + m
                    b = a + quarter
                    cos[a] = cos[b] = np.cos(ang)
                    sin[a], sin[b] = -np.sin(ang), np.sin(ang)
                    rot[b, a] = rot[a, b] = 1.0
        return cos, sin, rot
    for x, args in (("A", (DA, 2, 0)), ("B", (ROPE, 1, NOPE))):
        cos, sin, rot = tables(*args)
        put("cos" + x, cos), put("sin" + x, sin), put("rot" + x, rot)
    s, t = i[:, None], i[None, :]
    put("gmask", np.stack([t >= s, t <= s], 1))
    put("armask", np.stack([np.stack([t > s, t >= s], 1), np.stack([t < s, t <= s], 1)], 1))
    lev = []
    for b in range(7):
        w = 1 << b
        same = (s // (2 * w)) == (t // (2 * w))
        up = same & (s % (2 * w) >= w) & (t % (2 * w) < w)
        fwd, bwd = up, up.T
        lev += [fwd.T, bwd.T] if b == 0 else [fwd, bwd]
    put("lev", np.stack(lev, 1))
    put("reset", np.tile((np.arange(NT) % P != 0)[None], (P, 1)))
    selh, selr = np.zeros((P, 8, P)), np.zeros((P, 4, P))
    for base in (0, 32):
        for hd in range(8):
            selh[base + hd, hd] = 1
            selr[base + hd, hd % 4, 64 * (hd // 4):64 * (hd // 4) + 64] = 1
    put("selh", selh), put("selr", selr)
    return out


def lay_out(inp):
    f = {k: np.asarray(v) for k, v in inp.items()}
    at, n = param_columns()
    par = np.zeros((P, n), np.float32)

    def put(name, cols):
        par[:, at[name]:at[name] + cols.shape[1]] = cols
    put("cond", np.stack([pack_columns(f["c"][0]), pack_columns(f["c_ctx"])], 2).reshape(P, 16))
    for i in range(2):
        for k in ("ada_b", "norm1", "norm2"):
            put(f"{k}{i}", pack_columns(f[f"{k}_{i}"]))
        put(f"ffn_b{i}", pack_columns(f[f"ffn_conv_b_{i}"]))
        put(f"ffn_w{i}", pack_columns(f[f"ffn_conv_w_{i}"]))
    put("norm_f", pack_columns(f["norm_f"]))
    lam = np.zeros((P, 4), np.float32)
    for i, k in enumerate(("lambda_q1", "lambda_k1", "lambda_q2", "lambda_k2")):
        lam[:64, i] = f["l0_" + k]
    put("lam", lam)
    qn = np.zeros((2 * P,), np.float32)
    qn[:QL] = f["l0_q_norm"]
    put("q_norm", pack_columns(qn))
    put("subln", pack_columns(f["l0_subln"]))
    put("kv_norm", pack_columns(f["l0_kv_norm"]))
    for k in ("mu", "w0", "a0", "k_k", "k_a", "r_k", "ln_w", "ln_b", "conv_w", "conv_b", "gnorm"):
        put(k, pack_columns(f["l1_" + k]))
    put("Dskip", pack_columns(np.repeat(f["l1_D"], 64, axis=1)))
    small = np.zeros((P, 2), np.float32)
    for base, d in ((0, 0), (32, 1), (64, 0), (96, 1)):
        small[base:base + 8, 0] = f["l1_dt_bias"][d]
    for base, d in ((0, 0), (32, 1)):
        small[base:base + 8, 1] = f["l1_A_log"][d]
    put("dt_bias", small)
    ssm = np.stack([f["state_l1_ssm_fwd"][0], f["state_l1_ssm_bwd"][0]])
    ssm = ssm.reshape(2, 2, 4, PD, NS).transpose(1, 4, 0, 2, 3).reshape(P, 512)
    wkv = np.stack([f["state_l1_wkv_fwd"][0], f["state_l1_wkv_bwd"][0]])
    wkv = wkv.reshape(2, 4, 2, 64, 64).transpose(2, 4, 1, 0, 3).reshape(P, 512)
    arrays = {
        "params": par, "const": shape_constants(),
        "xT": np.concatenate([f["x_sample"][0], f["x_prompt"][0]], 0).T,
        "cv": f["cache_l0_v"][0], "ckT": f["cache_l0_k"][0].transpose(0, 2, 1),
        "cckvT": f["cache_l0_ckv"][0].T, "ckpeT": f["cache_l0_kpe"][0].T,
        "ssm0": ssm, "wkv0": wkv,
    }
    for k in ("ada_w_0", "ada_w_1", "l0_w_in", "l1_w_in", "l0_w_out", "l1_w_out", "ffn_up_0", "ffn_up_1", "ffn_down_0",
              "ffn_down_1", "l0_w_uq", "l0_w_ukv", "l1_w2", "l1_a2", "l1_g2"):
        arrays[k] = f[k]
    return {k: np.ascontiguousarray(v) for k, v in arrays.items()}


OUTS = {"yT": (D, NT), "k": (HA, P, P), "v": (P, 512), "ckv": (P, P), "kpe": (ROPE, P), "ssm": (P, 512), "wkv": (P, 512)}


def kernel(**inputs):
    import concourse.bacc as bacc
    from concourse.bass_utils import run_bass_kernel_spmd
    nc = bacc.Bacc("TRN2", target_bir_lowering=False, num_devices=1)
    arrays = lay_out(inputs)
    t_in = {k: nc.dram_tensor("in_" + k, v.shape, mybir.dt.from_np(v.dtype), kind="ExternalInput").ap()
            for k, v in arrays.items()}
    t_out = {k: nc.dram_tensor("out_" + k, s, F32, kind="ExternalOutput").ap() for k, s in OUTS.items()}
    build(nc, t_in, t_out)
    run = run_bass_kernel_spmd(nc, [{"in_" + k: v for k, v in arrays.items()}], core_ids=[0])
    o = {k: np.asarray(run.results[0]["out_" + k]) for k in OUTS}
    y = o["yT"].T
    new_k = o["k"].transpose(0, 2, 1)[None]
    new_v = o["v"].reshape(P, HA, P).transpose(1, 0, 2)[None]
    ssm = o["ssm"].reshape(2, NS, 2, 4, PD).transpose(2, 0, 3, 4, 1).reshape(2, 1, HD, PD, NS)
    wkv = o["wkv"].reshape(2, 64, 4, 2, 64).transpose(3, 2, 0, 4, 1).reshape(2, 1, HC, 64, 64)
    return tuple(np.ascontiguousarray(a) for a in (
        y[None, NL:], y[None, :NL], new_k, new_v, o["ckv"].T[None], o["kpe"].T[None], wkv[0], wkv[1], ssm[0], ssm[1]))
```

```python
import math
from contextlib import ExitStack

import numpy as np
import concourse.bass as bass
from concourse import mybir

F32 = mybir.dt.float32
F32R = mybir.dt.float32r
ALU = mybir.AluOpType
ACT = mybir.ActivationFunctionType
AXX = mybir.AxisListType.X
P = 128

D = 1024
KT = D // P
NL, NP_, NPAST = 512, 128, 128
NT = NL + NP_
NK = NT + NPAST
FF = 2816
FT = FF // P
HA, DA = 4, 64
HB, NOPE, ROPE, VB = 4, 64, 32, 128
QL, KVL = 192, 128
QK = NOPE + ROPE
HC, NC_ = 8, 64
HD, PD, NS = 8, 64, 64
NCH = NT // P
DEC = 0.606531
EPS = 1e-6
ADA_FIRST = 4
RING = 2
SLOT = 4096
SEG = ((0, NL), (NL, NT))
HALF = ((0, NT // 2), (NT // 2, NT))


def param_columns():
    at, n = {}, 0
    for name, w in ([("cond", 2 * KT)] +
                    [(f"{k}{i}", w) for i in range(2) for k, w in
                     (("ada_b", 48), ("norm1", KT), ("norm2", KT), ("ffn_b", 2 * FT), ("ffn_w", 3 * 2 * FT))] +
                    [("norm_f", KT), ("lam", 4), ("subln", 1), ("q_norm", 2), ("kv_norm", 1),
                     ("mu", 15), ("w0", 8), ("a0", 8), ("k_k", 4), ("k_a", 4), ("r_k", 4), ("ln_w", 4),
                     ("ln_b", 4), ("conv_w", 18), ("conv_b", 6), ("gnorm", 4), ("Dskip", 8),
                     ("dt_bias", 1), ("A_log", 1)]):
        at[name] = n
        n += w
    return at, n


def const_columns():
    at, n = {}, 0
    for name, w in (("ident", P), ("blk", P), ("rotA", P), ("rotB", P), ("cosA", NL), ("sinA", NL),
                    ("cosB", NL), ("sinB", NL), ("gmask", 2 * P), ("armask", 4 * P), ("lev", 7 * 2 * P),
                    ("reset", NT), ("selh", 8 * P), ("selr", 4 * P)):
        at[name] = (n, w)
        n += w
    return at, n


def build(nc, t_in, t_out):
    PC, NPAR = param_columns()
    CC, NCON = const_columns()
    ctx = ExitStack()
    with ctx:
        def sb(name, n, dt=F32):
            return ctx.enter_context(nc.sbuf_tensor(name, [P, n], dt))

        def sem(name):
            return ctx.enter_context(nc.semaphore(name))

        ps_all = ctx.enter_context(nc.psum_tensor("ps", [P, 8 * 512], F32))

        def bank(b, n=512, p0=0, p1=P):
            return ps_all[p0:p1, 512 * b:512 * b + n]

        place = {}

        def placed(name, n):
            place[name] = -(-nc.sbuf_base // 32) * 32
            return sb(name, n)

        def rounded(name, over, at, n):
            return nc.alloc_sbuf_tensor_at(name, [P, n], F32R, offset=place[over] + 4 * at)
        ring = placed("ring", RING * SLOT)
        h_b = sb("h", KT * NT)
        merged_b = placed("merged", KT * NT)
        par = sb("par", NPAR)
        mods = sb("mods", 2 * 96)
        geff = sb("geff", 4 * 16)
        ones = sb("ones", P)
        ident = sb("ident", P)
        blk = sb("blk", P)
        stat = placed("stat", 2 * NT)
        sqb = sb("sqb", 2 * NT)
        small = sb("small", 160)
        WN = 30800
        work = placed("work", WN)

        def area(start):
            pos = [start]

            def take(n):
                a = work[:, pos[0]:pos[0] + n]
                pos[0] += n
                assert pos[0] <= WN, (pos[0], WN)
                return a
            return take

        take0 = area(0)
        hn_b = take0(KT * NT)
        W0 = KT * NT

        def tile(buf, t, a=0, b=NT, n=NT):
            return buf[:, t * n + a:t * n + b]

        h = lambda t, a=0, b=NT: tile(h_b, t, a, b)
        hn = lambda t, a=0, b=NT: tile(hn_b, t, a, b)
        merged = lambda t, a=0, b=NT: tile(merged_b, t, a, b)

        def pc(name, i=0, w=1, p0=0, p1=P):
            return par[p0:p1, PC[name] + i:PC[name] + i + w]

        blocks = []
        def kblock(src, c0, c1):
            return [(src[:, c0:c1].rearrange("(k p) c -> p k c", p=P), KT, 0, c1 - c0, c1 - c0)]

        IN_CUTS = [(c, c + 256) for c in range(1920, 2944, 256)] + [(2944, 3208)] + \
            [(c, min(c + 256, 1920)) for c in range(0, 1920, 256)]

        def plan():
            def ada(l, b):
                blocks.append(("ada", kblock(t_in[f"ada_w_{l}"], 512 * b, 512 * b + 512)))
            for l in range(2):
                if l == 0:
                    for b in range(ADA_FIRST):
                        ada(0, b)
                win = t_in[f"l{l}_w_in"]
                cuts = ((0, 512), (512, 1024), (1536, 1888), (1024, 1536)) if l == 0 else \
                    IN_CUTS
                for a, b in cuts:
                    blocks.append(("win", kblock(win, a, b)))
                if l == 0:
                    for n in range(ADA_FIRST, 24):
                        ada(n // 12, n % 12)
                for b in range(2):
                    blocks.append(("wout", kblock(t_in[f"l{l}_w_out"], 512 * b, 512 * b + 512)))
                up, down = t_in[f"ffn_up_{l}"], t_in[f"ffn_down_{l}"]
                for b in range(FT // 2):
                    src = up.rearrange("(k p) c -> p k c", p=P)
                    blocks.append(("up", [(src[:, :, 256 * b:256 * b + 256], KT, 0, 256, 512),
                                          (src[:, :, FF + 256 * b:FF + 256 * b + 256], KT, 256, 256, 512)]))
                for b in range(KT):
                    blocks.append(("down", [(down[:, P * b:P * b + P].rearrange("(k p) c -> p k c", p=P), FT, 0, P, P)]))
        plan()
        full = [sem(f"block_loaded{i}") for i in range(RING)]
        parts_before = [[0] * (len(blocks) + 1) for _ in range(RING)]
        for n, (_, parts) in enumerate(blocks):
            for i in range(RING):
                parts_before[i][n + 1] = parts_before[i][n] + (len(parts) if n % RING == i else 0)
        released = []
        used = [0]

        def next_block(pe):
            n = used[0]
            used[0] += 1
            _, parts = blocks[n]
            pe.wait_ge(full[n % RING], 16 * parts_before[n % RING][n + 1])
            kt, width = parts[0][1], parts[0][4]
            return ring[:, (n % RING) * SLOT:(n % RING) * SLOT + kt * width].rearrange("p (k c) -> p k c", k=kt)

        S = {}

        def sg(name):
            if name not in S:
                S[name] = sem(name)
            return S[name]

        phase = sem("phase_left")
        phase_no = [0, 0, 0, 0]

        def leave_phase(eng, who):
            phase_no[who] += 1
            eng.drain().then_inc(phase, 1)
            eng.wait_ge(phase, 4 * phase_no[who])

        PE_, ACT_, DVE_, POOL_ = range(4)

        class Chain:
            def __init__(self, eng, name):
                self.eng, self.sem, self.n = eng, sg(name), 0

            def __call__(self, ins):
                self.n += 1
                ins.then_inc(self.sem, 1)
                self.eng.wait_ge(self.sem, self.n)

        def mm(pe, out, lhsT, rhs, first=True, last=True):
            return pe.matmul(out, lhsT, rhs, start=first, stop=last)

        def project(pe, pair, lhs, rhs, nk, p1=P, toks=SEG, p0=0, before=None):
            for k in range(nk):
                if before is not None:
                    before(k)
                for a, b in toks:
                    ins = mm(pe, ps_all[p0:p1, 1024 * pair + a:1024 * pair + b], lhs(k), rhs(k, a, b),
                             k == 0, k == nk - 1)
            return ins

        def pair_ap(pair, a=0, b=NT, p0=0, p1=P):
            return ps_all[p0:p1, 1024 * pair + a:1024 * pair + b]

        def spair(pair, a=0, b=NT, p0=0, p1=P):
            o = 1024 * pair + 512 - NT // 2
            return ps_all[p0:p1, o + a:o + b]

        def project_split(pe, pair, wh, wl, xh, xl, nk, before=None, p1=P):
            for k in range(nk):
                if before is not None:
                    before(k)
                for w, x in ((wh, xh), (wh, xl), (wl, xh)):
                    for a, b in HALF:
                        ins = mm(pe, spair(pair, a, b, 0, p1), w(k), x(k, a, b), k == 0 and w is wh and x is xh,
                                 k == nk - 1 and w is wl)
            return ins

        ada_rows_bank = lambda n: 7 if n >= ADA_FIRST else 6 + n % 2
        ada_cols_bank = lambda n: 7 if n >= ADA_FIRST else 5
        ada_row = lambda n: stat[0:2, 512 * (n % 2):512 * (n % 2) + 512]
        ada_w = {}

        def ada_products(pe, n, ks):
            if ks[0] == 0:
                ada_w[n] = next_block(pe)
                if n >= ADA_FIRST:
                    pe.wait_ge(sg("ada_taken"), n)
            for k in ks:
                ins = mm(pe, bank(ada_rows_bank(n), 512, 0, 2), small[:, 2 * k:2 * k + 2], ada_w[n][:, k, :],
                         k == 0, k == KT - 1)
            if ks[-1] == KT - 1:
                ins.then_inc(sg("ada_rows"), 1)
                released.append((sg("ada_rows"), n + 1))

        def ada_turn(pe, n):
            pe.wait_ge(sg("ada_rowed"), n + 1)
            if n >= 1:
                pe.wait_ge(sg("ada_taken"), n)
            for m in range(4):
                ins = mm(pe, bank(ada_cols_bank(n))[:, 2 * m:2 * m + 2], ada_row(n)[:, P * m:P * m + P], ident[0:2, 0:2])
            ins.then_inc(sg("ada_cols"), 1)

        def ada_take_rows(dve, n):
            dve.wait_ge(sg("ada_rows"), n + 1)
            dve.tensor_copy(ada_row(n), bank(ada_rows_bank(n), 512, 0, 2)).then_inc(sg("ada_rowed"), 1)

        def ada_take_cols(dve, n):
            l, b = n // 12, n % 12
            dve.wait_ge(sg("ada_cols"), n + 1)
            dve.tensor_tensor(mods[:, 8 * n:8 * n + 8].rearrange("p (m c) -> p m c", c=2),
                              bank(ada_cols_bank(n), 8).rearrange("p (m c) -> p m c", c=2),
                              pc(f"ada_b{l}", 4 * b, 4).unsqueeze(2).to_broadcast([P, 4, 2]), ALU.add)\
                .then_inc(sg("ada_taken"), 1)

        def ada_gain(dve, l, i, ch):
            md = mods[:, 96 * l:96 * l + 96].rearrange("p (m c) -> p m c", c=2)
            g = geff[:, 16 * (2 * l + i):16 * (2 * l + i) + 16].rearrange("p (m c) -> p m c", c=2)
            ch(dve.tensor_scalar(g, md[:, 24 * i + 8:24 * i + 16, :], 1.0, None, ALU.add))
            ch(dve.tensor_tensor(g, g, pc(f"norm{i + 1}{l}", 0, KT).unsqueeze(2).to_broadcast([P, KT, 2]), ALU.mult))

        def mod(l, part, t, c):
            o = 96 * l + 2 * (8 * part + t) + c
            return mods[:, o:o + 1]

        def norm_square(act, n, t, base=None):
            if base is not None:
                act.wait_ge(sg("res_done"), base + t + 1)
            if t >= 2:
                act.wait_ge(sg("norm_sum"), 8 * n + t - 1)
            act.activation(tile(sqb, t % 2), h(t), ACT.Square).then_inc(sg("norm_sq"), 1)

        def norm_act(act, n, shift, nt=KT, split=False, meanwhile=None):
            act.wait_ge(sg("norm_sum"), 8 * n + 8)
            act.activation(stat[:, 0:NT], pair_ap(3), ACT.Sqrt, bias=small[:, 16:17], scale=1.0 / D)\
                .then_inc(sg("norm_root"), 1)
            if meanwhile is not None:
                meanwhile()
            if shift is not None:
                for t in range(nt):
                    act.wait_ge(sg("norm_scaled"), 8 * n + t + 1)
                    if split:
                        act.activation(xh(t, 0, NL), hn(t, 0, NL), ACT.Identity, bias=shift(t, 0))
                        act.activation(xh(t, NL, NT), hn(t, NL, NT), ACT.Identity, bias=shift(t, 1)).then_inc(sg("x_hi"), 1)
                        continue
                    act.activation(hn(t, 0, NL), hn(t, 0, NL), ACT.Identity, bias=shift(t, 0)).then_inc(sg("hn_half"), 1)
                    act.activation(hn(t, NL, NT), hn(t, NL, NT), ACT.Identity, bias=shift(t, 1)).then_inc(sg("hn_ready"), 1)

        def norm_sum(pe, n, t):
            pe.wait_ge(sg("norm_sq"), 8 * n + t + 1)
            for a, b in SEG:
                ins = mm(pe, pair_ap(3, a, b), ones[:, :], tile(sqb, t % 2, a, b), t == 0, t == KT - 1)
            ins.then_inc(sg("norm_sum"), 1)

        def norm_dve(dve, n, gain, ch, out=hn, shift=None, layer=0, meanwhile=None):
            dve.wait_ge(sg("norm_root"), n + 1)
            ch(dve.reciprocal(stat[:, NT:2 * NT], stat[:, 0:NT]))
            if meanwhile is not None:
                meanwhile()
            for t in range(KT):
                dve.scalar_tensor_tensor(out(t, 0, NL), h(t, 0, NL), gain(t, 0), stat[:, NT:NT + NL], ALU.mult, ALU.mult)
                dve.scalar_tensor_tensor(out(t, NL, NT), h(t, NL, NT), gain(t, 1), stat[:, NT + NL:2 * NT],
                                         ALU.mult, ALU.mult).then_inc(sg("norm_scaled"), 1)
                if shift is not None and t >= 2:
                    norm_lo(dve, t - 2, shift, layer)
            if shift is not None:
                norm_lo(dve, KT - 2, shift, layer)
                norm_lo(dve, KT - 1, shift, layer)

        def norm_lo(dve, t, shift, layer):
            dve.wait_ge(sg("x_hi"), KT * layer + t + 1)
            for c, (a, b) in enumerate(SEG):
                ins = dve.scalar_tensor_tensor(xl(t, a, b), hn(t, a, b), shift(t, c), xh(t, a, b).bitcast(F32),
                                               ALU.add, ALU.subtract)
            ins.then_inc(sg("x_lo"), 1)

        def g_eff(n):
            return lambda t, c: geff[:, 16 * n + 2 * t + c:16 * n + 2 * t + c + 1]

        res_no = [0]

        def residual_dve(dve, base, gate, ch, pair_ap=pair_ap, between=None):
            for m in range(KT):
                if between is not None:
                    between(m)
                dve.wait_ge(sg("res_prod"), base + m + 1)
                dve.scalar_tensor_tensor(h(m, 0, NL), pair_ap(m % 2, 0, NL), gate(m, 0), h(m, 0, NL), ALU.mult, ALU.add)
                dve.scalar_tensor_tensor(h(m, NL, NT), pair_ap(m % 2, NL, NT), gate(m, 1), h(m, NL, NT),
                                         ALU.mult, ALU.add).then_inc(sg("res_done"), 1)
            dve.wait_ge(sg("res_done"), base + KT)

        def wout_pe(pe, base):
            for b in range(2):
                w = next_block(pe)
                for m in range(4):
                    n = 4 * b + m
                    if n >= 2:
                        pe.wait_ge(sg("res_done"), base + n - 1)
                    project(pe, n % 2, lambda k: w[:, k, P * m:P * m + P], merged, KT).then_inc(sg("res_prod"), 1)
                    if n >= 2:
                        norm_sum(pe, base // 8 + 1, n - 2)
                released.append((sg("res_prod"), base + 4 * b + 4))
            for t in (KT - 2, KT - 1):
                norm_sum(pe, base // 8 + 1, t)

        tk = area(W0)
        G_b = tk(FT * NT)
        G = lambda t, a=0, b=NT: tile(G_b, t, a, b)
        cacc = tk(4 * NT)

        def conv3_dve(dve, acc, psrc, w0, w2, ch, final=None):
            for i, (a, b) in enumerate(SEG):
                ch(dve.scalar_tensor_tensor(acc(a + 1, b), psrc(a, b - 1), w0, acc(a + 1, b), ALU.mult, ALU.add))
            for i, (a, b) in enumerate(SEG):
                ins = dve.scalar_tensor_tensor(acc(a, b - 1), psrc(a + 1, b), w2, acc(a, b - 1), ALU.mult, ALU.add)
                if i == 1 and final is not None:
                    ins.then_inc(final, 1)
                else:
                    ch(ins)

        wh_b = rounded("w_hi", "work", W0 + (FT + 4) * NT, 2 * SLOT)
        assert W0 + (FT + 4) * NT + 2 * SLOT <= WN
        wl_b = rounded("w_lo", "ring", 0, RING * SLOT)
        xh_b, xl_b = rounded("x_hi_r", "merged", 0, KT * NT), rounded("x_lo_r", "work", 0, KT * NT)
        xh = lambda t, a=0, b=NT: tile(xh_b, t, a, b)
        xl = lambda t, a=0, b=NT: tile(xl_b, t, a, b)
        gl_b = rounded("g_lo", "work", W0, FT * NT)
        gh_conv, gh_stat = rounded("g_hi_conv", "work", W0 + FT * NT, 4 * NT), rounded("g_hi_stat", "stat", 0, 2 * NT)
        gl = lambda t, a=0, b=NT: tile(gl_b, t, a, b)

        def gh(t, a=0, b=NT):
            for buf, n in ((gh_stat, 2), (xl_b, KT), (xh_b, KT), (gh_conv, 4)):
                if t < n:
                    return tile(buf, t, a, b)
                t -= n
        NF = FT // 2 + KT
        f_first = [[n for n, b in enumerate(blocks) if b[0] == "up"][FT // 2 * l] for l in range(2)]

        def w_hi_act(act, l, f, part, parts):
            n = f_first[l] + f
            if part == 0:
                act.wait_ge(full[n % RING], 16 * parts_before[n % RING][n + 1])
                if f >= 2:
                    act.wait_ge(*released[n - 2])
            w = (SLOT if f < FT // 2 else FT * P) // parts
            act.activation(wh_b[:, SLOT * (f % 2) + w * part:SLOT * (f % 2) + w * part + w],
                           ring[:, SLOT * (n % RING) + w * part:SLOT * (n % RING) + w * part + w], ACT.Copy)\
                .then_inc(sg("w_hi"), 1)
            w_parts["act"] += 1

        def w_lo_dve(dve, l, f, part, parts):
            n = f_first[l] + f
            w_parts["dve"] += 1
            dve.wait_ge(sg("w_hi"), w_parts["dve"])
            w = (SLOT if f < FT // 2 else FT * P) // parts
            at = SLOT * (n % RING) + w * part
            dve.tensor_tensor(wl_b[:, at:at + w], ring[:, at:at + w],
                              wh_b[:, SLOT * (f % 2) + w * part:SLOT * (f % 2) + w * part + w].bitcast(F32), ALU.subtract)\
                .then_inc(sg("w_lo"), 1)
        w_parts = {"act": 0, "dve": 0}
        WP = 4
        PARTS_AT = ((0,), (1, 2), (3,), ())

        def split_block(pe, l, f):
            n = f_first[l] + f
            w = next_block(pe)
            kt, width = blocks[n][1][0][1], blocks[n][1][0][4]
            pe.wait_ge(sg("w_lo"), WP * (NF * l + f + 1))
            v = lambda buf, slot: buf[:, SLOT * slot:SLOT * slot + kt * width].rearrange("p (k c) -> p k c", k=kt)
            return v(wh_b, f % 2), v(wl_b, n % RING)

        def ffn_pe(pe, l):
            for b in range(FT // 2):
                wh, wl = split_block(pe, l, b)
                for i in range(2):
                    for half in range(2):
                        n = 2 * (2 * b + i) + half
                        if n >= 2:
                            pe.wait_ge(sg("conv_done"), 2 * FT * l + n - 1)
                        c = 256 * half + P * i
                        x_ready = (lambda k: pe.wait_ge(sg("x_lo"), 2 * KT * l + k + 1)) if n == 0 else None
                        project_split(pe, n % 2, lambda k: wh[:, k, c:c + P], lambda k: wl[:, k, c:c + P], xh, xl, KT,
                                      x_ready).then_inc(sg("up_prod"), 1)
                released.append((sg("up_prod"), 2 * FT * l + 4 * b + 4))
            base = KT * (2 * l + 1)
            for m in range(KT):
                wh, wl = split_block(pe, l, FT // 2 + m)
                if m >= 2:
                    pe.wait_ge(sg("res_done"), base + m - 1)
                g_ready = (lambda k: pe.wait_ge(sg("g_lo"), FT * l + k + 1)) if m == 0 else None
                project_split(pe, m % 2, lambda k: wh[:, k, :], lambda k: wl[:, k, :], gh, gl, FT, g_ready)\
                    .then_inc(sg("res_prod"), 1)
                released.append((sg("res_prod"), base + m + 1))
                if m >= 2:
                    norm_sum(pe, 2 * l + 2, m - 2)
            for t in (KT - 2, KT - 1):
                norm_sum(pe, 2 * l + 2, t)

        def cw(l, tap, t):
            return pc(f"ffn_w{l}", tap * 2 * FT + t)

        def ffn_act(act, l):
            for m in range(FT):
                for half in range(2):
                    n = 2 * m + half
                    act.wait_ge(sg("up_prod"), 2 * FT * l + n + 1)
                    if m >= 2:
                        act.wait_ge(sg("gated"), FT * l + m - 1)
                    act.activation(tile(cacc, 2 * (m % 2) + half), spair(n % 2), ACT.Identity,
                                   bias=pc(f"ffn_b{l}", half * FT + m), scale=cw(l, 1, half * FT + m))\
                        .then_inc(sg("centre_tap"), 1)
                    for part in PARTS_AT[n % 4]:
                        w_hi_act(act, l, m // 2 + 1, part, WP)
                act.wait_ge(sg("conv_done"), 2 * FT * l + 2 * m + 1)
                a = tile(cacc, 2 * (m % 2))
                act.activation(a, a, ACT.Silu).then_inc(sg("gate_silu"), 1)
                if m in (4, 5):
                    act.activation(gh(m - 4), G(m - 4), ACT.Copy).then_inc(sg("g_hi"), 1)
            act.wait_ge(sg("gated"), FT * (l + 1))
            for t in range(2, FT):
                act.activation(gh(t), G(t), ACT.Copy).then_inc(sg("g_hi"), 1)
            for m in range(1, KT):
                for part in range(WP):
                    w_hi_act(act, l, FT // 2 + m, part, WP)
                if m >= 2:
                    norm_square(act, 2 * l + 2, m - 2, KT * (2 * l + 1))
            for t in (KT - 2, KT - 1):
                norm_square(act, 2 * l + 2, t, KT * (2 * l + 1))

        def ffn_dve(dve, l, ch):
            def g_lo_dve(t):
                dve.wait_ge(sg("g_hi"), FT * l + t + 1)
                dve.tensor_tensor(gl(t), G(t), gh(t).bitcast(F32), ALU.subtract).then_inc(sg("g_lo"), 1)

            for m in range(FT):
                for half in range(2):
                    n = 2 * m + half
                    dve.wait_ge(sg("centre_tap"), 2 * FT * l + n + 1)
                    conv3_dve(dve, lambda a, b: tile(cacc, 2 * (m % 2) + half, a, b),
                              lambda a, b: spair(n % 2, a, b), cw(l, 0, half * FT + m), cw(l, 2, half * FT + m),
                              ch, sg("conv_done"))
                    for part in PARTS_AT[n % 4]:
                        w_lo_dve(dve, l, m // 2 + 1, part, WP)
                dve.wait_ge(sg("gate_silu"), FT * l + m + 1)
                dve.wait_ge(sg("conv_done"), 2 * FT * l + 2 * m + 2)
                dve.tensor_tensor(G(m), tile(cacc, 2 * (m % 2)), tile(cacc, 2 * (m % 2) + 1), ALU.mult)\
                    .then_inc(sg("gated"), 1)
                if m in (6, 7):
                    g_lo_dve(m - 6)
            for t in range(2, FT):
                g_lo_dve(t)

            def next_lo(m):
                if m + 1 < KT:
                    for part in range(WP):
                        w_lo_dve(dve, l, FT // 2 + m + 1, part, WP)
            residual_dve(dve, KT * (2 * l + 1), lambda t, c: mod(l, 5, t, c), ch, spair, next_lo)

        stat_at = [0, 0]

        def plan_stats(items):
            i0, c0 = stat_at
            stat_at[0] += len(items)
            stat_at[1] += sum(len(it[0]) for it in items)
            return i0, c0, items

        def stats_act(act, planned):
            i, c, items = planned
            for srcs, mat, scale, eps, outs in items:
                for src, kk in srcs:
                    if c >= 2:
                        act.wait_ge(sg("st_sum"), c - 1)
                    act.activation(sqb[0:kk, (c % 2) * NT:(c % 2) * NT + NT], src, ACT.Square).then_inc(sg("st_sq"), 1)
                    c += 1
                act.wait_ge(sg("st_sum"), c)
                if i >= 2:
                    act.wait_ge(sg("st_used"), i - 1)
                act.activation(stat[:, (i % 2) * NT:(i % 2) * NT + NT], pair_ap(3), ACT.Sqrt,
                               bias=small[:, eps:eps + 1], scale=scale).then_inc(sg("st_root"), 1)
                i += 1

        def stats_pe(pe, planned):
            i, c, items = planned
            for srcs, mat, scale, eps, outs in items:
                if i >= 1:
                    pe.wait_ge(sg("st_root"), i)
                for j, (src, kk) in enumerate(srcs):
                    pe.wait_ge(sg("st_sq"), c + 1)
                    for a, b in SEG:
                        ins = mm(pe, pair_ap(3, a, b), mat[0:kk, :], sqb[0:kk, (c % 2) * NT + a:(c % 2) * NT + b],
                                 j == 0, j == len(srcs) - 1)
                    ins.then_inc(sg("st_sum"), 1)
                    c += 1
                i += 1

        def stats_dve(dve, planned, ch):
            i, c, items = planned
            for srcs, mat, scale, eps, outs in items:
                dve.wait_ge(sg("st_root"), i + 1)
                st = stat[:, (i % 2) * NT:(i % 2) * NT + NT]
                ch(dve.reciprocal(st, st))
                for j, (out, in_, gain, kk) in enumerate(outs):
                    ins = dve.scalar_tensor_tensor(out, in_, gain, st[0:kk, :], ALU.mult, ALU.mult)
                    if j == len(outs) - 1:
                        ins.then_inc(sg("st_used"), 1)
                    else:
                        ch(ins)
                i += 1
            dve.wait_ge(sg("st_used"), i)

        tk = area(W0)
        q_b, k_b, v_b = tk(4 * NT), tk(4 * NK), tk(6 * 512)
        pr_b, dT_b, dTp_b = tk(2 * 2 * NT), tk(2 * 5 * 512), tk(2 * P)
        qd_b, ckv_b, kpe_b = tk(2 * NT), tk(NK), tk(NK)
        wuq, wukv = tk(2 * 384), tk(768)
        cosA, sinA, cosB, sinB, rotA, rotB = tk(NL), tk(NL), tk(NL), tk(NL), tk(P), tk(P)
        rt_b = tk(NL)
        q = lambda t, a=0, b=NT: tile(q_b, t, a, b)
        kk_ = lambda t, a=0, b=NK: tile(k_b, t, a, b, NK)
        KP0 = NT
        NEGLAM, SUB8 = 24, 25

        def rope(dve, x, x_raw, psum, cos, sin, ch, p0=0, p1=P, done=None):
            ch(dve.tensor_tensor(rt_b[p0:p1, :], psum, sin[p0:p1, :], ALU.mult))
            ch(dve.tensor_tensor(x, x, cos[p0:p1, :], ALU.mult))
            ins = dve.tensor_tensor(x, x, rt_b[p0:p1, :], ALU.add)
            if done is not None:
                ins.then_inc(done, 1)
            else:
                ch(ins)

        V0 = 12

        def mix0_pe(pe):
            n = 0
            for part in range(2):
                w = next_block(pe)
                for m in range(4):
                    if n >= 3:
                        pe.wait_ge(sg("m0_copied"), n - 2)
                    x_ready = (lambda k: pe.wait_ge(sg("hn_ready"), k + 1)) if n == 0 else None
                    project(pe, n % 3, lambda k: w[:, k, P * m:P * m + P], hn, KT, before=x_ready)\
                        .then_inc(sg("m0_prod"), 1)
                    n += 1
                released.append((sg("m0_prod"), n))
            w = next_block(pe)
            for c0, c1 in ((0, 128), (128, 192), (192, 320), (256, 352)):
                pe.wait_ge(sg("m0_copied"), n - 2)
                project(pe, n % 3, lambda k: w[:, k, c0:c1], hn, KT, p1=c1 - c0).then_inc(sg("m0_prod"), 1)
                n += 1
            released.append((sg("m0_prod"), n))
            w = next_block(pe)
            for tt in range(5):
                pe.wait_ge(sg("m0_copied"), n - 2)
                for k in range(KT):
                    ins = mm(pe, bank(2 * (n % 3)), hn(k, P * tt, P * tt + P), w[:, k, :], k == 0, k == KT - 1)
                ins.then_inc(sg("m0_prod"), 1)
                n += 1
                if tt == 0:
                    pe.wait_ge(sg("m0_loaded"), 16 * 14)
                    pe.wait_ge(sg("m0_copied"), V0)
                if tt == 1:
                    stats_pe(pe, low_norms)
                for m in range(2 * tt, min(2 * tt + 2, 9)):
                    if m >= 2:
                        pe.wait_ge(sg("m0_roped"), m - 1)
                    if m < 8:
                        mm(pe, bank(1 + 2 * (m % 2)), rotA[:, :], q(m, 0, NL) if m < 4 else kk_(m - 4, 0, NL))\
                            .then_inc(sg("m0_rot"), 1)
                    else:
                        mm(pe, bank(1, 512, 0, QK), rotB[0:QK, 0:QK], kpe_b[0:QK, 0:NL]).then_inc(sg("m0_rot"), 1)
            released.append((sg("m0_prod"), n))
            pe.wait_ge(sg("lam_prod"), 1)
            mm(pe, bank(6, 2), ones[0:64, :], small[0:64, 26:28]).then_inc(sg("lam_sum"), 1)

        low_norms = plan_stats([
            ([(tile(qd_b, 0), P), (qd_b[0:64, NT:2 * NT], 64)], ones, 1.0 / QL, 16,
             [(tile(qd_b, 0), tile(qd_b, 0), pc("q_norm", 0), P),
              (qd_b[0:64, NT:2 * NT], qd_b[0:64, NT:2 * NT], pc("q_norm", 1, 1, 0, 64), 64)]),
            ([(sqb[:, 0:NT] if False else merged(0), P)], ones, 1.0 / KVL, 16,
             [(merged(0), merged(0), pc("kv_norm"), P)])])

        def mix0_act(act):
            n = 0
            for m in range(8):
                act.wait_ge(sg("m0_prod"), n + 1)
                if m < 4:
                    act.activation(q(m), pair_ap(n % 3), ACT.Copy, scale=DA ** -0.5).then_inc(sg("m0_copied"), 1)
                else:
                    act.activation(kk_(m - 4, 0, NL), pair_ap(n % 3, 0, NL), ACT.Copy)
                    act.activation(kk_(m - 4, KP0, NK), pair_ap(n % 3, NL, NT), ACT.Copy).then_inc(sg("m0_copied"), 1)
                n += 1
            for i in range(4):
                act.wait_ge(sg("m0_prod"), n + 1)
                pp = n % 3
                if i == 0:
                    act.activation(tile(qd_b, 0), pair_ap(pp), ACT.Copy).then_inc(sg("m0_copied"), 1)
                elif i == 1:
                    act.activation(qd_b[0:64, NT:2 * NT], pair_ap(pp, 0, NT, 0, 64), ACT.Copy).then_inc(sg("m0_copied"), 1)
                elif i == 2:
                    act.activation(merged(0), pair_ap(pp), ACT.Copy).then_inc(sg("m0_copied"), 1)
                else:
                    act.activation(kpe_b[0:QK, 0:NL], pair_ap(pp, 0, NL, 0, QK), ACT.Copy)
                    act.activation(kpe_b[64:QK, KP0:NK], pair_ap(pp, NL, NT, 64, QK), ACT.Copy).then_inc(sg("m0_copied"), 1)
                n += 1
            act.wait_ge(sg("m0_copied"), V0)
            stats_act(act, low_norms)
            for tt in range(5):
                act.wait_ge(sg("m0_prod"), n + 1)
                slot = tt if tt < 4 else 5
                act.activation(v_b[:, 512 * slot:512 * slot + 512], bank(2 * (n % 3)), ACT.Copy).then_inc(sg("m0_copied"), 1)
                n += 1
            act.wait_ge(sg("lam_sum"), 1)
            act.activation(small[:, 28:30], bank(6, 2), ACT.Exp).then_inc(sg("lam_exp"), 1)

        def mix0_dve(dve, ch):
            for m in range(9):
                dve.wait_ge(sg("m0_rot"), m + 1)
                if m < 8:
                    src = q(m, 0, NL) if m < 4 else kk_(m - 4, 0, NL)
                    rope(dve, src, src, bank(1 + 2 * (m % 2)), cosA, sinA, ch, done=sg("m0_roped"))
                else:
                    x = kpe_b[64:QK, 0:NL]
                    rope(dve, x, x, bank(1, 512, 64, QK), cosB, sinB, ch, 64, QK, done=sg("m0_roped"))
                dve.wait_ge(sg("m0_roped"), m + 1)
                if m == 3:
                    stats_dve(dve, low_norms, ch)
            ch(dve.tensor_copy(ckv_b[:, 0:NL], merged(0, 0, NL)))
            ch(dve.tensor_copy(ckv_b[:, KP0:NK], merged(0, NL, NT)))
            lp = par[0:64, PC["lam"]:PC["lam"] + 4].rearrange("p (a b) -> p a b", b=2)
            dve.tensor_tensor(small[0:64, 26:28], lp[:, :, 0], lp[:, :, 1], ALU.mult).then_inc(sg("lam_prod"), 1)
            lam_init = 0.8 - 0.6 * math.exp(0.0)
            dve.wait_ge(sg("lam_exp"), 1)
            ch(dve.tensor_tensor(small[:, NEGLAM:NEGLAM + 1], small[:, 29:30], small[:, 28:29], ALU.subtract))
            ch(dve.tensor_scalar(small[:, NEGLAM:NEGLAM + 1], small[:, NEGLAM:NEGLAM + 1], -lam_init, None, ALU.add))
            ch(dve.tensor_scalar(small[:, SUB8:SUB8 + 1], pc("subln"), 1.0 - lam_init, None, ALU.mult))

        def att_units():
            return [(hd, qt) for hd in range(4) for qt in range(5)]

        def att_pe(pe, g):
            maps = 2 - g
            units = att_units()
            x = f"att{g}_"

            def scores(u):
                hd, qt = units[u]
                for s in range(maps):
                    i = maps * u + s
                    if i >= 2:
                        pe.wait_ge(sg(x + "exp"), i - 1)
                    p0, p1 = (64 * s, 64 * s + 64) if g == 0 else (0, QK)
                    lhs = q_b[p0:p1, NT * hd + P * qt:NT * hd + P * qt + P]
                    key = lambda a, b: k_b[p0:p1, NK * hd + a:NK * hd + b]
                    if qt < 4:
                        mm(pe, pair_ap(i % 2, 0, 512), lhs, key(0, 512))
                        ins = mm(pe, pair_ap(i % 2, 512, 640), lhs, key(512, 640))
                    else:
                        ins = mm(pe, pair_ap(i % 2, 0, P), lhs, key(KP0, NK))
                    ins.then_inc(sg(x + "scores"), 1)

            def transposes(u):
                hd, qt = units[u]
                pe.wait_ge(sg(x + "probs"), u + 1)
                if u >= 1:
                    pe.wait_ge(sg(x + "turned_out"), u)
                if u >= 6:
                    pe.wait_ge(sg(x + "out"), (u - 1) // 5)
                pb = pr_b[:, (u % 2) * 2 * NT:(u % 2) * 2 * NT + NT]
                for kt in range(5 if qt < 4 else 1):
                    ins = pe.transpose(bank(4)[:, P * kt:P * kt + P] if kt < 4 else bank(5, P), pb[:, P * kt:P * kt + P],
                                       ident[:, :])
                ins.then_inc(sg(x + "turned"), 1)

            def values(hd):
                pe.wait_ge(sg(x + "turned_out"), 5 * hd + 5)
                if hd >= 1:
                    pe.wait_ge(sg(x + "out"), hd)
                for kt in range(5):
                    mm(pe, bank(6), v_b[:, 512 * kt + P * hd:512 * kt + P * hd + P],
                       dT_b[:, (hd % 2) * 2560 + 512 * kt:(hd % 2) * 2560 + 512 * kt + 512], kt == 0, kt == 4)
                pe.wait_ge(sg(x + "turned_out"), min(5 * hd + 6, 20))
                mm(pe, bank(5)[:, P:2 * P], v_b[:, 512 * 5 + P * hd:512 * 5 + P * hd + P],
                   dTp_b[:, (hd % 2) * P:(hd % 2) * P + P]).then_inc(sg(x + "values"), 1)

            for u in range(len(units) + 2):
                n = ADA_FIRST + 10 * g + u // 2
                if u % 2 == 0 and 2 <= u <= len(units):
                    ada_turn(pe, n - 1)
                if u < len(units):
                    scores(u)
                    ada_products(pe, n, range(4 * (u % 2), 4 * (u % 2) + 4))
                if 1 <= u <= len(units):
                    transposes(u - 1)
                if u >= 2 and units[u - 2][1] == 4:
                    values(units[u - 2][0])

        def att_act(act, g):
            maps = 2 - g
            units = att_units()
            x = f"att{g}_"
            for u in range(len(units) + 2):
                if u < len(units):
                    hd, qt = units[u]
                    w = NT if qt < 4 else P
                    for s in range(maps):
                        i = maps * u + s
                        act.wait_ge(sg(x + "max"), i + 1)
                        if u >= 2:
                            act.wait_ge(sg(x + "turned"), u - 1)
                        pb = pr_b[:, (u % 2) * 2 * NT + s * NT:(u % 2) * 2 * NT + s * NT + w]
                        c = 32 + (i % 4)
                        act.activation(pb, pair_ap(i % 2, 0, w), ACT.Exp, bias=small[:, c:c + 1],
                                       accum_out=small[:, c + 4:c + 5]).then_inc(sg(x + "exp"), 1)
                if 1 <= u <= len(units):
                    hd, qt = units[u - 1]
                    act.wait_ge(sg(x + "turned"), u)
                    if hd >= 2:
                        act.wait_ge(sg(x + "values"), hd - 1)
                    o = (hd % 2) * 2560
                    if qt < 4:
                        dst = dT_b[:, o:o + 2560].rearrange("p (k q) -> p k q", k=5)
                        act.activation(dst[:, 0:4, P * qt:P * qt + P], bank(4).rearrange("p (k q) -> p k q", k=4), ACT.Copy)
                        act.activation(dst[:, 4, P * qt:P * qt + P], bank(5, P), ACT.Copy).then_inc(sg(x + "turned_out"), 1)
                    else:
                        act.activation(dTp_b[:, (hd % 2) * P:(hd % 2) * P + P], bank(4, P), ACT.Copy)\
                            .then_inc(sg(x + "turned_out"), 1)
                if u >= 2 and units[u - 2][1] == 4:
                    hd = units[u - 2][0]
                    act.wait_ge(sg(x + "values"), hd + 1)
                    act.activation(merged(4 * g + hd, 0, NL), bank(6), ACT.Copy)
                    act.activation(merged(4 * g + hd, NL, NT), bank(5)[:, P:2 * P], ACT.Copy).then_inc(sg(x + "out"), 1)

        def att_dve(dve, g, ch):
            maps = 2 - g
            units = att_units()
            x = f"att{g}_"
            for u in range(len(units) + 1):
                n = ADA_FIRST + 10 * g + u // 2
                if u % 2 == 0 and u >= 2:
                    ada_take_rows(dve, n - 1)
                    ada_take_cols(dve, n - 1)
                if u < len(units):
                    w = NT if units[u][1] < 4 else P
                    for s in range(maps):
                        i = maps * u + s
                        dve.wait_ge(sg(x + "scores"), i + 1)
                        c = 32 + (i % 4)
                        dve.tensor_reduce(small[:, c:c + 1], pair_ap(i % 2, 0, w), AXX, ALU.max, negate=True)\
                            .then_inc(sg(x + "max"), 1)
                if u >= 1:
                    v = u - 1
                    w = NT if units[v][1] < 4 else P
                    dve.wait_ge(sg(x + "exp"), maps * v + maps)
                    pb = pr_b[:, (v % 2) * 2 * NT:(v % 2) * 2 * NT + w]
                    c = 36 + (maps * v) % 4
                    ch(dve.reciprocal(small[:, c + 4:c + 4 + maps], small[:, c:c + maps]))
                    if g == 0:
                        pb2 = pr_b[:, (v % 2) * 2 * NT + NT:(v % 2) * 2 * NT + NT + w]
                        ch(dve.tensor_tensor(small[:, c + 5:c + 6], small[:, c + 5:c + 6], small[:, NEGLAM:NEGLAM + 1], ALU.mult))
                        ch(dve.tensor_scalar(pb, pb, small[:, c + 4:c + 5], None, ALU.mult))
                        dve.scalar_tensor_tensor(pb, pb2, small[:, c + 5:c + 6], pb, ALU.mult, ALU.add)\
                            .then_inc(sg(x + "probs"), 1)
                    else:
                        dve.tensor_scalar(pb, pb, small[:, c + 4:c + 5], None, ALU.mult).then_inc(sg(x + "probs"), 1)

        subln_norms = plan_stats([
            ([(merged(t), P)], ones, 1.0 / P, 16, [(merged(t), merged(t), small[:, SUB8:SUB8 + 1], P)]) for t in range(4)])

        def up0_pe(pe):
            for hd in range(4):
                if hd >= 2:
                    pe.wait_ge(sg("u0_copied"), hd - 1)
                for a, b in SEG:
                    mm(pe, pair_ap(hd % 2, a, b, 0, QK), wuq[:, QK * hd:QK * hd + QK], tile(qd_b, 0, a, b), True, False)
                    ins = mm(pe, pair_ap(hd % 2, a, b, 0, QK), wuq[0:64, 384 + QK * hd:384 + QK * hd + QK],
                             qd_b[0:64, NT + a:NT + b], False, True)
                ins.then_inc(sg("u0_prod"), 1)
            for hd in range(4):
                pe.wait_ge(sg("u0_copied"), hd + 3)
                for a, b in ((0, 512), (512, NK)):
                    ins = mm(pe, pair_ap(hd % 2, a, b, 0, 64), wukv[:, 192 * hd:192 * hd + 64], ckv_b[:, a:b])
                ins.then_inc(sg("u0_prod"), 1)
            for tt in range(6):
                pe.wait_ge(sg("u0_copied"), tt + 7)
                vcols = wukv[:, :].rearrange("p (h c) -> p h c", h=4)[:, :, 64:192]
                mm(pe, bank(2 * (tt % 2)), ckv_b[:, P * tt:P * tt + P], vcols).then_inc(sg("u0_prod"), 1)
            for hd in range(4):
                pe.wait_ge(sg("u0_copied"), 14)
                if hd >= 2:
                    pe.wait_ge(sg("u0_roped"), hd - 1)
                mm(pe, bank(4 + hd % 2, 512, 0, QK), rotB[0:QK, 0:QK], q_b[0:QK, NT * hd:NT * hd + NL]).then_inc(sg("u0_rot"), 1)

        def up0_act(act):
            for hd in range(4):
                act.wait_ge(sg("u0_prod"), hd + 1)
                act.activation(q_b[0:QK, NT * hd:NT * hd + NT], pair_ap(hd % 2, 0, NT, 0, QK), ACT.Copy,
                               scale=QK ** -0.5).then_inc(sg("u0_copied"), 1)
            for hd in range(4):
                act.wait_ge(sg("u0_prod"), hd + 5)
                act.activation(k_b[0:64, NK * hd:NK * hd + NK], pair_ap(hd % 2, 0, NK, 0, 64), ACT.Copy)\
                    .then_inc(sg("u0_copied"), 1)
            for tt in range(6):
                act.wait_ge(sg("u0_prod"), tt + 9)
                act.activation(v_b[:, 512 * tt:512 * tt + 512], bank(2 * (tt % 2)), ACT.Copy).then_inc(sg("u0_copied"), 1)

        def up0_pool(pool):
            for hd in range(4):
                ins = pool.tensor_copy(k_b[64:QK, NK * hd:NK * hd + NK], kpe_b[64:QK, 0:NK])

        def up0_dve(dve, ch):
            for hd in range(4):
                dve.wait_ge(sg("u0_rot"), hd + 1)
                x = q_b[64:QK, NT * hd:NT * hd + NL]
                rope(dve, x, x, bank(4 + hd % 2, 512, 64, QK), cosB, sinB, ch, 64, QK, done=sg("u0_roped"))
                dve.wait_ge(sg("u0_roped"), hd + 1)

        CB = WN - 15 * NT - 3 * 512
        tk = area(CB)
        rkv_b, low_b = tk(12 * NT), tk(3 * NT)
        w2s, a2s, g2s = tk(512), tk(512), tk(512)
        r_ = lambda j, a=0, b=NT: tile(rkv_b, j, a, b)
        k_ = lambda j, a=0, b=NT: tile(rkv_b, 4 + j, a, b)
        v_ = lambda j, a=0, b=NT: tile(rkv_b, 8 + j, a, b)
        low = lambda i, a=0, b=NT: tile(low_b, i, a, b)
        tk = area(W0)
        zg_b, xs_b, bc_b, dq_b = tk(4 * NT), tk(4 * NT), tk(2 * NT), tk(NT)
        SSD0 = W0 + 11 * NT
        MUH, MU1, DSUM, KA1, EXPA = 64, 79, 94, 98, 102

        IN_W = KT * 264
        wi_b = rounded("w_in_hi", "work", SSD0, 2 * IN_W)
        IN_COLS = (2, 2, 2, 2, 3, 2, 2, 2, 2, 2, 2, 2, 1)
        in_block = [n for n, b in enumerate(blocks) if b[0] == "win"][-len(IN_COLS):]
        in_start = {sum(IN_COLS[:q]): q for q in range(len(IN_COLS))}
        in_w = lambda q: KT * (IN_CUTS[q][1] - IN_CUTS[q][0])

        def in_hi(act, q):
            i, w = in_block[q], in_w(q)
            act.wait_ge(full[i % RING], 16 * parts_before[i % RING][i + 1])
            if q >= 2:
                act.wait_ge(*released[i - 2])
            act.activation(wi_b[:, IN_W * (q % 2):IN_W * (q % 2) + w], ring[:, SLOT * (i % RING):SLOT * (i % RING) + w],
                           ACT.Copy).then_inc(sg("in_hi"), 1)

        def in_lo(dve, q):
            i, w = in_block[q], in_w(q)
            dve.wait_ge(sg("in_hi"), q + 1)
            at = SLOT * (i % RING)
            dve.tensor_tensor(wl_b[:, at:at + w], ring[:, at:at + w], wi_b[:, IN_W * (q % 2):IN_W * (q % 2) + w].bitcast(F32),
                              ALU.subtract).then_inc(sg("in_lo"), 1)

        dt_raw, dt_sel = stat[0:8, 0:NT], stat[0:8, NT:NT + 104]

        def mix1_pe(pe):
            n = 0
            for q, cols in enumerate(IN_COLS):
                next_block(pe)
                pe.wait_ge(sg("in_lo"), q + 1)
                k3 = lambda ap: ap.rearrange("p (k c) -> p k c", k=KT)
                wh = k3(wi_b[:, IN_W * (q % 2):IN_W * (q % 2) + in_w(q)])
                wl = k3(wl_b[:, SLOT * (in_block[q] % RING):SLOT * (in_block[q] % RING) + in_w(q)])
                for m in range(cols):
                    if n >= 3:
                        pe.wait_ge(sg("p1_done"), n - 2)
                    c, p1 = P * m, 8 if n == 10 else P
                    x_ready = (lambda k: pe.wait_ge(sg("x_lo"), KT + k + 1)) if n == 0 else None
                    project_split(pe, n % 3, lambda k: wh[:, k, c:c + p1], lambda k: wl[:, k, c:c + p1], xh, xl, KT,
                                  x_ready, p1).then_inc(sg("p1_prod"), 1)
                    n += 1
                    if n == 12:
                        pe.wait_ge(sg("dt_raw"), 1)
                        for a, b in HALF:
                            ins = mm(pe, spair(10 % 3, a, b, 0, 104), dt_sel, dt_raw[:, a:b])
                        ins.then_inc(sg("dt_rows"), 1)
                released.append((sg("p1_prod"), n))

        def p1_dst(n):
            if n < 4:
                return zg_b, n, None
            if n < 8:
                return xs_b, n - 4, n - 4
            if n < 10:
                return bc_b, n - 8, n - 4
            if n < 23:
                return rkv_b, n - 11, n - 11
            return low_b, n - 23, n - 11

        def p1_taps(n):
            _, _, i = p1_dst(n)
            if n < 10:
                return pc("conv_w", i), pc("conv_w", 6 + i), pc("conv_w", 12 + i), pc("conv_b", i)
            return (small[:, MUH + i:MUH + i + 1], small[:, MU1 + i:MU1 + i + 1], small[:, MUH + i:MUH + i + 1], 0.0)

        CONV_N = [n for n in range(4, 26) if n != 10]

        def softplus_act(act):
            act.wait_ge(sg("sp_abs"), 1)
            act.activation(spa[0:104, :], spa[0:104, :], ACT.Exp, scale=-1.0).then_inc(sg("sp_exp"), 1)
            act.wait_ge(sg("sp_exp"), 1)
            act.activation(spa[0:104, :], spa[0:104, :], ACT.Ln, bias=1.0).then_inc(sg("sp_ln"), 1)

        SILU_N = (4, 5, 6, 7, 8, 9, 0, 1, 2, 3)

        def mix1_act(act):
            act.activation(small[0:40, EXPA:EXPA + 1], pc("A_log", 0, 1, 0, 40), ACT.Exp).then_inc(sg("exp_A"), 1)
            act.wait_ge(sg("mu_ready"), 1)
            for n in range(26):
                act.wait_ge(sg("p1_prod"), n + 1)
                if n in in_start and in_start[n] + 1 < len(IN_COLS):
                    in_hi(act, in_start[n] + 1)
                if n not in CONV_N:
                    continue
                buf, t, _ = p1_dst(n)
                _, w1, _, b = p1_taps(n)
                act.activation(tile(buf, t), spair(n % 3), ACT.Identity, bias=b, scale=w1).then_inc(sg("p1_centre"), 1)
                if n == 12:
                    softplus_act(act)
                if 13 <= n < 13 + len(SILU_N):
                    act.wait_ge(sg("p1_done"), 10)
                    buf, t, _ = p1_dst(SILU_N[n - 13])
                    act.activation(tile(buf, t), tile(buf, t), ACT.Silu).then_inc(sg("p1_silu"), 1)
            act.wait_ge(sg("p1_done"), 26)
            act.activation(low(0), low(0), ACT.Tanh)
            act.activation(low(2), low(2), ACT.Sigmoid).then_inc(sg("low_ready"), 1)

        spa, dA, cumA = sqb[:, 0:NT], sqb[:, NT:2 * NT], stat[:, 0:NT]

        def softplus_start_dve(dve):
            dve.scalar_tensor_tensor(spa[0:104, :], dq_b[0:104, :], -1.0, dq_b[0:104, :], ALU.mult, ALU.max).then_inc(sg("sp_abs"), 1)

        def decay_dve(dve, ch):
            dve.wait_ge(sg("ssd_loaded"), 16 * 5)
            dve.wait_ge(sg("sp_ln"), 1)
            ch(dve.tensor_scalar(dq_b[0:104, :], dq_b[0:104, :], 0.0, None, ALU.max))
            ch(dve.tensor_tensor(dq_b[0:104, :], dq_b[0:104, :], spa[0:104, :], ALU.add))
            dve.wait_ge(sg("exp_A"), 1)
            ch(dve.tensor_scalar(dA[0:40, :], dq_b[0:40, :], small[0:40, EXPA:EXPA + 1], -1.0, ALU.mult, ALU.mult))
            ch(dve.tensor_tensor_scan(cumA[0:40, :], c_reset[0:40, :], dA[0:40, :], 0.0, ALU.mult, ALU.add))
            ch(dve.tensor_copy(dq_b[0:8, :], cumA[0:8, :]))
            ch(dve.tensor_tensor(dq_b[32:40, :], dA[32:40, :], cumA[32:40, :], ALU.subtract))
            c3 = lambda b, p0, p1: b[p0:p1, :].rearrange("p (c t) -> p c t", t=P)
            dve.tensor_tensor(c3(dq_b, 32, 40), c3(dq_b, 32, 40), c3(cumA, 32, 40)[:, :, P - 1:P].to_broadcast([8, 5, P]),
                              ALU.add).then_inc(sg("dq_ready"), 1)

        def mix1_dve(dve, ch):
            ch(dve.tensor_scalar(small[:, MUH:MUH + 15], pc("mu", 0, 15), 0.5, None, ALU.mult))
            ch(dve.tensor_scalar(small[:, KA1:KA1 + 4], pc("k_a", 0, 4), -1.0, 1.0, ALU.mult, ALU.add))
            ch(dve.tensor_tensor(small[:, DSUM:DSUM + 4], pc("Dskip", 0, 4), pc("Dskip", 4, 4), ALU.add))
            dve.tensor_scalar(small[:, MU1:MU1 + 15], pc("mu", 0, 15), -1.0, 1.0, ALU.mult, ALU.add).then_inc(sg("mu_ready"), 1)
            ch(dve.memset(dq_b[:, :], 0.0))
            ch(dve.memset(dt_sel, 0.0))
            for i in range(4):
                ch(dve.tensor_copy(dt_sel[:, 32 * i:32 * i + 8], ident[0:8, 0:8]))
            c = 0
            for n in range(26):
                if n in in_start and in_start[n] + 1 < len(IN_COLS):
                    in_lo(dve, in_start[n] + 1)
                if n < 4:
                    dve.wait_ge(sg("p1_prod"), n + 1)
                    dve.tensor_copy(tile(zg_b, n), spair(n % 3)).then_inc(sg("p1_done"), 1)
                elif n == 10:
                    dve.wait_ge(sg("p1_prod"), n + 1)
                    dve.tensor_copy(dt_raw, spair(n % 3, 0, NT, 0, 8)).then_inc(sg("dt_raw"), 1)
                    dve.wait_ge(sg("dt_rows"), 1)
                    for i in range(4):
                        ins = dve.tensor_scalar(dq_b[32 * i:32 * i + 8, :], spair(n % 3, 0, NT, 32 * i, 32 * i + 8),
                                                pc("dt_bias", 0, 1, 32 * i, 32 * i + 8), None, ALU.add)
                        if i < 3:
                            ch(ins)
                    ins.then_inc(sg("p1_done"), 1)
                    dve.wait_ge(sg("p1_done"), n + 1)
                    softplus_start_dve(dve)
                else:
                    c += 1
                    dve.wait_ge(sg("p1_centre"), c)
                    buf, t, _ = p1_dst(n)
                    w0, _, w2, _ = p1_taps(n)
                    conv3_dve(dve, lambda a, b: tile(buf, t, a, b), lambda a, b: spair(n % 3, a, b), w0, w2, ch,
                              sg("p1_done"))
                    if n == 14:
                        decay_dve(dve, ch)
            dve.wait_ge(sg("p1_done"), 26)

        tk = area(SSD0)
        tk(3 * NT)
        gm_b, btok, tokD, de_b = tk(2 * 256), tk(5 * P), tk(5 * 104), tk(16)
        tk = area(SSD0 + 2 * IN_W)
        c_reset, c_selh, c_selr, c_gm = tk(NT), tk(8 * P), tk(4 * P), tk(2 * P)
        sst = tk(2 * 256)
        assert SSD0 + 2 * IN_W + NT + 14 * P + 512 <= CB and 3 * NT + 512 + 640 + 520 + 16 <= 2 * IN_W
        tk = area(0)
        M_b, xdt_b, er_b, ct_b = tk(2 * 1024), tk(2 * 512), tk(2 * 512), tk(2 * 512)
        xde_b = work[:, SSD0:SSD0 + 2 * 512]
        xtok = merged_b[:, 0:5 * 512]
        UNITS = [(d, c) for s in range(4) for d, c in ((0, s), (1, 3 - s))] + [(0, 4), (1, 4)]

        def ssd_prep_dve(dve, ch):
            for t in range(4):
                ch(dve.tensor_scalar(merged(4 + t), tile(xs_b, t), small[:, DSUM + t:DSUM + t + 1], None, ALU.mult))

        def ssd_prep_act(act):
            for c in range(5):
                act.wait_ge(sg("ssd_tok"), c + 1)
                b0 = 2 * (c % 2)
                act.activation(xtok[:, 512 * c:512 * c + 512], bank(b0), ACT.Copy)
                act.activation(btok[:, P * c:P * c + P], bank(b0 + 1)[:, 0:P], ACT.Copy)
                act.activation(tokD[:, 104 * c:104 * c + 104], bank(b0 + 1)[:, P:P + 104], ACT.Copy)\
                    .then_inc(sg("ssd_tokcp"), 1)

        def ssd_prep_pe(pe):
            pe.wait_ge(sg("dq_ready"), 1)
            pe.wait_ge(sg("p1_silu"), 10)
            for c in range(5):
                if c >= 2:
                    pe.wait_ge(sg("ssd_tokcp"), c - 1)
                b0 = 2 * (c % 2)
                for t in range(4):
                    pe.transpose(bank(b0)[:, P * t:P * t + P], tile(xs_b, t, P * c, P * c + P), ident[:, :])
                pe.transpose(bank(b0 + 1)[:, 0:P], bc_b[:, P * c:P * c + P], ident[:, :])
                pe.transpose(bank(b0 + 1)[:, P:P + 104], dq_b[0:104, P * c:P * c + P], ident[0:104, 0:104])\
                    .then_inc(sg("ssd_tok"), 1)
            pe.wait_ge(sg("ssd_tokcp"), 5)

        def ssd_pe(pe):
            def front(u):
                d, c = UNITS[u]
                if u >= 1:
                    pe.wait_ge(sg("ssd_seg"), u)
                    pe.wait_ge(sg("ssd_gm"), u)
                    pe.wait_ge(sg("ssd_er"), u)
                for g in range(2):
                    p0 = 64 * g
                    mm(pe, bank(3 + g, P), bc_b[p0:p0 + 64, P * c:P * c + P], bc_b[p0:p0 + 64, NT + P * c:NT + P * c + P])
                p0 = 32 * d
                rhs = dq_b[p0:p0 + 8, P * c:P * c + P]
                for hd in range(8):
                    mm(pe, ps_all[:, P * hd:P * hd + P], c_selh[p0:p0 + 8, P * hd:P * hd + P], rhs)
                for r in range(4):
                    ins = mm(pe, bank(2)[:, P * r:P * r + P], c_selr[p0:p0 + 8, P * r:P * r + P], rhs)
                ins.then_inc(sg("ssd_bc"), 1)

            def back(u):
                d, c = UNITS[u]
                x = u % 2
                pe.wait_ge(sg("ssd_m"), u + 1)
                if u >= 1:
                    pe.wait_ge(sg("ssd_state"), u)
                for g in range(2):
                    for r in range(4):
                        hd = 4 * g + r
                        out = bank(5 + g)[64 * (r % 2):64 * (r % 2) + 64, P * (r // 2):P * (r // 2) + P]
                        mm(pe, out, xdt_b[:, 512 * x + 64 * hd:512 * x + 64 * hd + 64],
                           M_b[:, 1024 * x + P * hd:1024 * x + P * hd + P], True, False)
                        ins = mm(pe, out, sst[64 * g:64 * g + 64, 256 * d + 64 * r:256 * d + 64 * r + 64],
                                 ct_b[64 * g:64 * g + 64, 512 * x + P * r:512 * x + P * r + P], False, True)
                ins.then_inc(sg("ssd_y"), 1)
                for g in range(2):
                    ins = mm(pe, bank(7)[64 * g:64 * g + 64, 0:256], btok[:, P * c + 64 * g:P * c + 64 * g + 64],
                             xde_b[:, 512 * x + 256 * g:512 * x + 256 * g + 256])
                ins.then_inc(sg("ssd_s"), 1)

            front(0)
            for u in range(10):
                if u + 1 < 10:
                    front(u + 1)
                back(u)

        def ssd_act(act):
            for u in range(10):
                x = u % 2
                act.wait_ge(sg("ssd_bc"), u + 1)
                if u >= 2:
                    act.wait_ge(sg("ssd_state"), u - 1)
                act.activation(er_b[:, 512 * x:512 * x + 512], bank(2), ACT.Exp).then_inc(sg("ssd_er"), 1)
                act.wait_ge(sg("ssd_seg"), u + 1)
                M = M_b[:, 1024 * x:1024 * x + 1024]
                act.activation(M, M, ACT.Exp)
                act.activation(de_b[:, 8 * x:8 * x + 8], de_b[:, 8 * x:8 * x + 8], ACT.Exp).then_inc(sg("ssd_exp"), 1)

        def ssd_dve(dve, ch):
            def front(u):
                d, c = UNITS[u]
                x = u % 2
                end = P - 1 if d == 0 else 0
                M3 = M_b[:, 1024 * x:1024 * x + 1024].rearrange("p (h t) -> p h t", t=P)
                bc3 = ps_all[:, 0:1024].rearrange("p (h t) -> p h t", t=P)
                Qt = tokD[:, 104 * c + 32 * d:104 * c + 32 * d + 8]
                dt = tokD[:, 104 * c + 64 + 32 * d:104 * c + 64 + 32 * d + 8]
                dve.wait_ge(sg("ssd_bc"), u + 1)
                if u >= 2:
                    dve.wait_ge(sg("ssd_s"), u - 1)
                ch(dve.tensor_tensor(M3, bc3, Qt.unsqueeze(2).to_broadcast([P, 8, P]), ALU.subtract))
                de = de_b[:, 8 * x:8 * x + 8]
                ch(dve.tensor_tensor(de, bc3[:, :, end], Qt, ALU.subtract))
                M = M_b[:, 1024 * x:1024 * x + 1024]
                dve.tensor_scalar(M, M, 0.0, None, ALU.min).then_inc(sg("ssd_seg"), 1)
                gp = ps_all[:, 1536:2560].rearrange("p (g t) -> p g t", t=512)[:, :, 0:P]
                gm = gm_b[:, 256 * x:256 * x + 256].rearrange("p (g t) -> p g t", t=P)
                dve.tensor_tensor(gm, gp, c_gm[:, P * d:P * d + P].unsqueeze(1).to_broadcast([P, 2, P]), ALU.mult)\
                    .then_inc(sg("ssd_gm"), 1)
                xt3 = lambda b, o: b[:, o:o + 512].rearrange("p (h t) -> p h t", t=64)
                xdt = xt3(xdt_b, 512 * x)
                ch(dve.tensor_tensor(xdt, xt3(xtok, 512 * c), dt.unsqueeze(2).to_broadcast([P, 8, 64]), ALU.mult))
                dve.wait_ge(sg("ssd_er"), u + 1)
                er3 = er_b[:, 512 * x:512 * x + 512].rearrange("p (r t) -> p r t", t=P)
                ct3 = ct_b[:, 512 * x:512 * x + 512].rearrange("p (r t) -> p r t", t=P)
                ch(dve.tensor_tensor(ct3, er3, bc_b[:, NT + P * c:NT + P * c + P].unsqueeze(1).to_broadcast([P, 4, P]), ALU.mult))
                dve.wait_ge(sg("ssd_exp"), u + 1)
                ch(dve.tensor_tensor(xt3(xde_b, 512 * x), xdt, de.unsqueeze(2).to_broadcast([P, 8, 64]), ALU.mult))
                for g in range(2):
                    ins = dve.tensor_tensor(M3[:, 4 * g:4 * g + 4, :], M3[:, 4 * g:4 * g + 4, :],
                                            gm[:, g:g + 1, :].to_broadcast([P, 4, P]), ALU.mult)
                    if g == 0:
                        ch(ins)
                ins.then_inc(sg("ssd_m"), 1)

            def back(u):
                d, c = UNITS[u]
                x = u % 2
                end = P - 1 if d == 0 else 0
                dve.wait_ge(sg("ssd_y"), u + 1)
                for g in range(2):
                    y3 = merged_b[:, (4 + 2 * g) * NT:(6 + 2 * g) * NT].rearrange("p (t n) -> p t n", n=NT)[:, :, P * c:P * c + P]
                    ch(dve.tensor_tensor(y3, y3, bank(5 + g, 256).rearrange("p (t n) -> p t n", n=P), ALU.add))
                dve.wait_ge(sg("ssd_s"), u + 1)
                S3 = sst[:, 256 * d:256 * d + 256].rearrange("p (r t) -> p r t", t=64)
                er3 = er_b[:, 512 * x:512 * x + 512].rearrange("p (r t) -> p r t", t=P)
                ch(dve.tensor_tensor(S3, S3, er3[:, :, end:end + 1].to_broadcast([P, 4, 64]), ALU.mult))
                if u in (6, 7):
                    dve.memset(sst[:, 256 * d:256 * d + 256], 0.0).then_inc(sg("ssd_state"), 1)
                else:
                    dve.tensor_tensor(S3, S3, bank(7, 256).rearrange("p (r t) -> p r t", t=64), ALU.add)\
                        .then_inc(sg("ssd_state"), 1)

            for u in range(11):
                if u < 10:
                    front(u)
                if u >= 1:
                    back(u - 1)
            dve.wait_ge(sg("ssd_state"), 10)
            for t in range(4):
                ins = dve.tensor_tensor(merged(4 + t), merged(4 + t), tile(zg_b, t), ALU.mult)
            ins.then_inc(sg("od_gated"), 1)

        od_norm = plan_stats([([(merged(4 + t), P) for t in range(4)], ones, 1.0 / 512, 16,
                               [(merged(4 + t), merged(4 + t), pc("gnorm", t), P) for t in range(4)])])

        tk = area(0)
        kk_b, sw_b, ag_b, x1_b, x2_b, er1, ea1, eb1 = (tk(NT) for _ in range(8))
        TQ = 3584
        tk = area(2 * TQ)
        AR_b, BK_b = tk(2 * 1280), tk(2 * 1280)
        bkt_b, vt_b, u0_b, u_b = tk(4 * 512), tk(NT), tk(256), tk(256)
        st_b, ssc_b, s0_b = tk(P), tk(P), tk(512)
        sf_b = s0_b
        c_ar, c_lev, c_reset2 = tk(4 * P), tk(14 * P), tk(NT)
        wk = tk(32)
        assert 2 * TQ + 2 * 2560 + 2048 + NT + 512 + 2 * P + 512 + 18 * P + NT + 32 <= CB

        ARv = AR_b[:, :].rearrange("p (d c x t) -> p d c x t", d=2, c=5, x=2)
        BKv = BK_b[:, :].rearrange("p (d c x t) -> p d c x t", d=2, c=5, x=2)
        LBo, LKo, XFo = 0, 1024, 2048

        def kept(slot, o, n=512):
            base = ring[:, 2560 * slot + o:2560 * slot + o + n] if slot < 3 else work[:, 4096 + o:4096 + o + n]
            return base
        kslot = lambda j, g, a: 2 * ((3 * j + g) % 2) + a
        GROUPS = ((0, 1), (2, 3), (4,))
        chunk_of = lambda s, d: 4 if s == 4 else (s if d == 0 else 3 - s)

        kk_norms = [plan_stats([([(kk_b[:, :], P)], blk, 1.0, 17, [(kk_b[:, :], kk_b[:, :], small[:, 19:20], P)])])
                    for j in range(4)]

        def wkv_prep_pe(pe, j):
            stats_pe(pe, kk_norms[j])
            for d in range(2):
                n = 2 * j + d
                if d == 1:
                    pe.wait_ge(sg("wkv_sig"), n)
                p0 = 64 * d
                for a, b in SEG:
                    mm(pe, pair_ap(0, a, b), w2s[p0:p0 + 64, P * j:P * j + P], low_b[p0:p0 + 64, a:b])
                    ins = mm(pe, pair_ap(1, a, b), a2s[p0:p0 + 64, P * j:P * j + P], low_b[p0:p0 + 64, NT + a:NT + b])
                ins.then_inc(sg("wkv_lora"), 1)
            for c in range(5):
                ins = pe.transpose(ps_all[:, 2048 + P * c:2048 + P * c + P], v_(j, P * c, P * c + P), ident[:, :])
            ins.then_inc(sg("wkv_vt"), 1)

        def wkv_prep_act(act, j):
            stats_act(act, kk_norms[j])
            for d in range(2):
                n = 2 * j + d
                act.wait_ge(sg("wkv_lora"), n + 1)
                if d == 1:
                    act.wait_ge(sg("wkv_prep"), n)
                act.activation(sw_b[:, :], pair_ap(0), ACT.Sigmoid, bias=pc("w0", 4 * d + j))
                act.activation(ag_b[:, :], pair_ap(1), ACT.Sigmoid, bias=pc("a0", 4 * d + j)).then_inc(sg("wkv_sig"), 1)
                if d == 0:
                    act.wait_ge(sg("wkv_vt"), j + 1)
                    act.activation(vt_b[:, :], ps_all[:, 2048:2048 + NT], ACT.Copy).then_inc(sg("wkv_vtcp"), 1)
                act.wait_ge(sg("wkv_cum"), n + 1)
                ex = lambda out, in_, sign: act.activation(out[:, :], in_[:, :], ACT.Exp, scale=sign * DEC)
                if d == 0:
                    ex(er1, x2_b, -1)
                    ex(ea1, x1_b, -1)
                    ex(eb1, x2_b, 1).then_inc(sg("wkv_exp"), 1)
                else:
                    ex(er1, x1_b, 1)
                    ex(ea1, x2_b, 1)
                    ex(eb1, x1_b, -1).then_inc(sg("wkv_exp"), 1)

        def wkv_prep_dve(dve, j, ch):
            dve.tensor_scalar(kk_b[:, :], k_(j), pc("k_k", j), None, ALU.mult).then_inc(sg("wkv_kx"), 1)
            stats_dve(dve, kk_norms[j], ch)
            c3 = lambda b: b[:, :].rearrange("p (c t) -> p c t", t=P)
            for d in range(2):
                n = 2 * j + d
                dve.wait_ge(sg("wkv_sig"), n + 1)
                if n == 0:
                    dve.wait_ge(sg("wkv_loaded"), 16 * 4)
                ch(dve.tensor_tensor_scan(x1_b[:, :], c_reset2[:, :], sw_b[:, :], 0.0, ALU.mult, ALU.add))
                ch(dve.tensor_tensor(c3(x2_b), c3(x1_b), c3(x1_b)[:, :, 63:64].to_broadcast([P, 5, P]), ALU.subtract))
                dve.tensor_tensor(x1_b[:, :], x2_b[:, :], sw_b[:, :], ALU.subtract).then_inc(sg("wkv_cum"), 1)
                dve.wait_ge(sg("wkv_cum"), n + 1)
                ch(dve.tensor_scalar(sw_b[:, :], ag_b[:, :], pc("k_a", j), small[:, KA1 + j:KA1 + j + 1], ALU.mult, ALU.add))
                ch(dve.tensor_tensor(sw_b[:, :], sw_b[:, :], k_(j), ALU.mult))
                ch(dve.tensor_tensor(ag_b[:, :], ag_b[:, :], kk_b[:, :], ALU.mult))
                dve.wait_ge(sg("wkv_exp"), n + 1)
                ch(dve.tensor_tensor(BKv[:, d, :, 1, :], c3(sw_b), c3(eb1), ALU.mult))
                ch(dve.tensor_tensor(BKv[:, d, :, 0, :], c3(ag_b), c3(eb1), ALU.mult))
                ch(dve.scalar_tensor_tensor(ARv[:, d, :, 0, :], c3(kk_b), -1.0, c3(ea1), ALU.mult, ALU.mult))
                ch(dve.tensor_tensor(ARv[:, d, :, 1, :], r_(j).rearrange("p (c t) -> p c t", t=P), c3(er1), ALU.mult))
                first, last = (0, P - 1) if d == 0 else (P - 1, 0)
                ch(dve.reciprocal(wk[:, 5 * d:5 * d + 5], c3(ea1)[:, :, first]))
                dve.tensor_copy(wk[:, 10 + 5 * d:15 + 5 * d], c3(er1)[:, :, last]).then_inc(sg("wkv_prep"), 1)
            dve.wait_ge(sg("wkv_prep"), 2 * j + 2)

        cnt = {}

        def step(who, name):
            cnt[who, name] = cnt.get((who, name), 0) + 1
            return cnt[who, name]

        sq4 = range(4)
        ts = lambda a, i=0, n=P: work[:, 1024 * a + P * i:1024 * a + P * i + n]
        vs = lambda a, i=0, n=P: work[:, 1024 * a + 512 + P * i:1024 * a + 512 + P * i + n]

        def wkv_solve_pe(pe, j, g, between):
            grp = GROUPS[g]
            vb = lambda a, i: bank(a)[:, P * i:P * i + P]
            tb = lambda a, i: bank(4 + 2 * a)[:, P * i:P * i + P]
            xb = lambda a, i: bank(5 + 2 * a)[:, P * i:P * i + P]
            xs = lambda a, i: kept(kslot(j, g, a), XFo + P * i, P)
            first = wkv_quads(j, g)
            if g == 0:
                pe.wait_ge(sg("wkv_prep"), 2 * j + 2)
                pe.wait_ge(sg("wkv_vtcp"), j + 1)
            for a, s in enumerate(grp):
                if a > 0:
                    pe.wait_ge(sg("wkv_bkcp"), first + a)
                for e in range(2):
                    p0 = 64 * e
                    if e == 1 and a == 0 and first > 0:
                        pe.wait_ge(sg("wkv_xf"), first)
                    for d in range(2):
                        rhs = ARv[p0:p0 + 64, d, chunk_of(s, d), :, :]
                        for x in range(2):
                            to = bank(x if e == 0 else 4 + 2 * a + x)[:, 256 * d:256 * d + 256]
                            ins = mm(pe, to, BKv[p0:p0 + 64, d, chunk_of(s, d), x, :], rhs)
                    ins.then_inc(sg("wkv_gram"), 1)
                if between:
                    between.pop(0)()
                pe.wait_ge(sg("wkv_masked"), 2 * (first + a) + 1)
                for d in range(2):
                    for x in range(2):
                        i = 2 * d + x
                        ins = pe.transpose(bank(0)[:, P * i:P * i + P], BKv[:, d, chunk_of(s, d), x, :], ident[:, :])
                ins.then_inc(sg("wkv_bkt"), 1)
                if between:
                    between.pop(0)()
            pe.wait_ge(sg("wkv_masked"), 2 * (first + len(grp)))
            for a, s in enumerate(grp):
                pe.wait_ge(sg("wkv_x0"), first + a + 1)
                for i in sq4:
                    ins = mm(pe, tb(a, i), xs(a, i), ident[:, :])
                ins.then_inc(sg("wkv_tv"), 1)
            pe.wait_ge(sg("wkv_bkcp"), first + len(grp))
            for lev in range(1, 7):
                for a, s in enumerate(grp):
                    if lev == 1:
                        pe.wait_ge(sg("wkv_t0"), first + a + 1)
                    else:
                        pe.wait_ge(sg("wkv_tcp"), step("pe", "tcp"))
                    for i in sq4:
                        ins = mm(pe, vb(a, i), kept(kslot(j, g, a), LBo + 256 * i, P), ts(a, i))
                    ins.then_inc(sg("wkv_lt"), 1)
                if len(grp) == 1 and between:
                    between.pop(0)()
                for a, s in enumerate(grp):
                    pe.wait_ge(sg("wkv_vm"), step("pe", "vm"))
                    if lev > 1:
                        pe.wait_ge(sg("wkv_xcp"), step("pe", "xcp"))
                    if lev < 6:
                        for i in sq4:
                            ins = mm(pe, tb(a, i), xs(a, i), vs(a, i))
                        ins.then_inc(sg("wkv_tfull"), 1)
                    for i in sq4:
                        ins = mm(pe, xb(a, i), vs(a, i), xs(a, i))
                    ins.then_inc(sg("wkv_vx"), 1)
                if len(grp) == 2 and between:
                    between.pop(0)()
            while between:
                between.pop(0)()

        def wkv_quads(j, g):
            return 5 * j + sum(len(x) for x in GROUPS[:g])

        def wkv_solve_act(act, j, g, between):
            grp = GROUPS[g]
            for a, s in enumerate(grp):
                k = kslot(j, g, a)
                if between:
                    between.pop(0)()
                act.wait_ge(sg("wkv_bkt"), step("act", "bkt"))
                act.activation(bkt_b[:, 512 * k:512 * k + 512], bank(0), ACT.Copy).then_inc(sg("wkv_bkcp"), 1)
                if between:
                    between.pop(0)()
            for a, s in enumerate(grp):
                act.wait_ge(sg("wkv_tv"), step("act", "tv"))
                act.activation(ts(a, 0, 512), bank(4 + 2 * a), ACT.Copy).then_inc(sg("wkv_t0"), 1)
            for piece in between:
                piece()
            between.clear()

        def wkv_solve_dve(dve, j, g, ch, between):
            grp = GROUPS[g]
            e2 = lambda ap: ap.rearrange("p (e x) -> p e x", e=2)
            i4 = lambda ap: ap.rearrange("p (i t) -> p i t", i=4)
            for a, s in enumerate(grp):
                k = kslot(j, g, a)
                if a == 0 and between:
                    between.pop(0)()
                for e in range(2):
                    dve.wait_ge(sg("wkv_gram"), step("dve", "gram"))
                    for x in range(2):
                        ins = dve.tensor_tensor(kept(k, (LBo, LKo)[x] + 512 * e), bank(x if e == 0 else 4 + 2 * a + x),
                                                c_ar[:, :], ALU.mult)
                    ins.then_inc(sg("wkv_masked"), 1)
                    dve.wait_ge(sg("wkv_masked"), step("dve", "masked"))
                    dve.tensor_tensor(vs(a, 2 * e, 256).rearrange("p (d t) -> p d t", d=2),
                                      kept(k, LBo + 512 * e).rearrange("p (d x t) -> p d x t", d=2, x=2)[:, :, 0, :],
                                      c_lev[:, 0:256].rearrange("p (d t) -> p d t", d=2), ALU.mult)\
                        .then_inc(sg("wkv_first"), 1)
                dve.wait_ge(sg("wkv_first"), 2 * step("dve", "first"))
                dve.tensor_tensor(i4(kept(k, XFo)), i4(vs(a, 0, 512)), ident[:, :].unsqueeze(1).to_broadcast([P, 4, P]),
                                  ALU.add).then_inc(sg("wkv_x0"), 1)
                for _ in range(1 if a == 0 else 2):
                    if between:
                        between.pop(0)()
            dve.wait_ge(sg("wkv_t0"), wkv_quads(j, g) + len(grp))
            for lev in range(1, 7):
                for a, s in enumerate(grp):
                    dve.wait_ge(sg("wkv_lt"), step("dve", "lt"))
                    dve.tensor_tensor(e2(vs(a, 0, 512)), e2(bank(a)),
                                      c_lev[:, 256 * lev:256 * lev + 256].unsqueeze(1).to_broadcast([P, 2, 256]), ALU.mult)\
                        .then_inc(sg("wkv_vm"), 1)
                if len(grp) == 1 and between:
                    between.pop(0)()
                for a, s in enumerate(grp):
                    if lev < 6:
                        dve.wait_ge(sg("wkv_tfull"), step("dve", "tv"))
                        dve.tensor_tensor(ts(a, 0, 512), ts(a, 0, 512), bank(4 + 2 * a), ALU.add).then_inc(sg("wkv_tcp"), 1)
                    dve.wait_ge(sg("wkv_vx"), step("dve", "vx"))
                    x = kept(kslot(j, g, a), XFo)
                    dve.tensor_tensor(x, x, bank(5 + 2 * a), ALU.add).then_inc(sg("wkv_xf" if lev == 6 else "wkv_xcp"), 1)
                if len(grp) == 2 and between:
                    between.pop(0)()
            while between:
                between.pop(0)()

        def wkv_apply_pe(pe, j, g):
            def pieces(a, s):
                k = kslot(j, g, a)
                lk = lambda e, d, x: kept(k, LKo + 512 * e + 256 * d + P * x, P)

                def u0():
                    pe.wait_ge(sg("wkv_ss"), step("pe", "ss"))
                    for e in range(2):
                        for d in range(2):
                            c = chunk_of(s, d)
                            out = bank(2 + e)[:, 64 * d:64 * d + 64]
                            mm(pe, out, ARv[64 * e:64 * e + 64, d, c, 0, :], ssc_b[64 * e:64 * e + 64, 64 * d:64 * d + 64], True, False)
                            ins = mm(pe, out, lk(e, d, 0), vt_b[:, P * c + 64 * e:P * c + 64 * e + 64], False, True)
                    ins.then_inc(sg("wkv_u0"), 1)

                def u():
                    pe.wait_ge(sg("wkv_u0cp"), step("pe", "u0cp"))
                    pe.wait_ge(sg("wkv_xf"), wkv_quads(j, g) + a + 1)
                    for i in range(4):
                        ins = mm(pe, bank(2)[:, 64 * i:64 * i + 64], kept(k, XFo + P * i, P), u0_b[:, 64 * i:64 * i + 64])
                    ins.then_inc(sg("wkv_u"), 1)

                def y():
                    pe.wait_ge(sg("wkv_ucp"), step("pe", "ucp"))
                    for e in range(2):
                        for d in range(2):
                            c, i = chunk_of(s, d), 2 * e + d
                            out = bank(2 + e)[64 * e:64 * e + 64, P * d:P * d + P]
                            vt = vt_b[:, P * c + 64 * e:P * c + 64 * e + 64]
                            mm(pe, out, ssc_b[64 * e:64 * e + 64, 64 * d:64 * d + 64], ARv[64 * e:64 * e + 64, d, c, 1, :], True, False)
                            mm(pe, out, u_b[:, 64 * i:64 * i + 64], kept(k, LBo + 256 * i + P, P), False, False)
                            mm(pe, out, vt, lk(e, d, 1), False, True)
                            so = bank(2 + e)[64 * e:64 * e + 64, 256 + 64 * d:256 + 64 * d + 64]
                            bk = lambda x: bkt_b[:, 512 * k + 256 * d + P * x + 64 * e:512 * k + 256 * d + P * x + 64 * e + 64]
                            mm(pe, so, bk(0), u_b[:, 64 * i:64 * i + 64], True, False)
                            ins = mm(pe, so, bk(1), vt, False, True)
                    ins.then_inc(sg("wkv_y"), 1)
                return [u0, u, y]
            return [x for a, s in enumerate(GROUPS[g]) for x in pieces(a, s)]

        def wkv_apply_act(act, j, g):
            def pieces(a, s):
                def u0():
                    act.wait_ge(sg("wkv_u0"), step("act", "u0"))
                    act.activation(u0_b[:, :].rearrange("p (e x) -> p e x", e=2),
                                   ps_all[:, 1024:2048].rearrange("p (e x) -> p e x", e=2)[:, :, 0:P], ACT.Copy)\
                        .then_inc(sg("wkv_u0cp"), 1)

                def u():
                    act.wait_ge(sg("wkv_u"), step("act", "u"))
                    act.activation(u_b[:, :], bank(2, 256), ACT.Copy).then_inc(sg("wkv_ucp"), 1)
                return [u0, u, lambda: None]
            return [x for a, s in enumerate(GROUPS[g]) for x in pieces(a, s)]

        def wkv_apply_dve(dve, j, g, ch):
            def pieces(a, s):
                def scale_state():
                    for d in range(2):
                        c = chunk_of(s, d)
                        dst = ssc_b[:, 64 * d:64 * d + 64]
                        if s == 4:
                            ins = dve.memset(dst, 0.0)
                        else:
                            src = s0_b[:, P * j + 64 * d:P * j + 64 * d + 64] if s == 0 else st_b[:, 64 * d:64 * d + 64]
                            ins = dve.tensor_scalar(dst, src, wk[:, 5 * d + c:5 * d + c + 1], None, ALU.mult)
                        if d == 0:
                            ch(ins)
                    ins.then_inc(sg("wkv_ss"), 1)

                def y():
                    dve.wait_ge(sg("wkv_y"), step("dve", "y"))
                    for e in range(2):
                        for d in range(2):
                            c = chunk_of(s, d)
                            yy = merged(j, P * c, P * c + P)[64 * e:64 * e + 64]
                            ch(dve.tensor_tensor(yy, yy, bank(2 + e)[64 * e:64 * e + 64, P * d:P * d + P], ALU.add))
                        sc = ssc_b[64 * e:64 * e + 64, :]
                        ch(dve.tensor_tensor(sc, sc, bank(2 + e)[64 * e:64 * e + 64, 256:384], ALU.add))
                    for d in range(2):
                        c = chunk_of(s, d)
                        dst = sf_b[:, P * j + 64 * d:P * j + 64 * d + 64] if s == 4 else st_b[:, 64 * d:64 * d + 64]
                        ins = dve.tensor_scalar(dst, ssc_b[:, 64 * d:64 * d + 64], wk[:, 10 + 5 * d + c:11 + 5 * d + c], None, ALU.mult)
                        if d == 0:
                            ch(ins)
                    ins.then_inc(sg("wkv_state"), 1)
                    dve.wait_ge(sg("wkv_state"), 5 * j + s + 1)
                return [scale_state, lambda: None, y]
            return [x for a, s in enumerate(GROUPS[g]) for x in pieces(a, s)]

        y_norms = [plan_stats([([(merged(j), P)], blk, 1.0 / 64, 18, [(merged(j), merged(j), pc("ln_w", j), P)])])
                   for j in range(4)]
        bonus_b, gates_b = (kk_b, sw_b, ag_b, x1_b), (x2_b, er1, ea1, eb1)

        def post_pe(pe):
            for j in range(4):
                if j >= 3:
                    pe.wait_ge(sg("y_centred"), j - 2)
                for a, b in SEG:
                    ins = mm(pe, pair_ap(j % 3, a, b), blk[:, :], merged(j, a, b))
                ins.then_inc(sg("y_mean"), 1)
            pe.wait_ge(sg("y_centred"), 4)
            for j in range(4):
                pe.wait_ge(sg("rk_ready"), j + 1)
                if j >= 1:
                    pe.wait_ge(sg("bonus_read"), j)
                    pe.wait_ge(sg("gate_read"), j)
                for a, b in SEG:
                    mm(pe, pair_ap(0, a, b), blk[:, :], bonus_b[j][:, a:b])
                    ins = mm(pe, pair_ap(1, a, b), g2s[:, P * j:P * j + P], low(2, a, b))
                ins.then_inc(sg("bonus"), 1)
                stats_pe(pe, y_norms[j])

        def post_act(act):
            act.wait_ge(sg("y_centred"), 4)
            for j in range(4):
                act.wait_ge(sg("bonus"), j + 1)
                act.activation(gates_b[j][:, :], pair_ap(1), ACT.Copy).then_inc(sg("gate_read"), 1)
                stats_act(act, y_norms[j])

        def post_dve(dve, ch):
            for j in range(4):
                dve.wait_ge(sg("y_mean"), j + 1)
                dve.scalar_tensor_tensor(merged(j), pair_ap(j % 3), -1.0 / 64, merged(j), ALU.mult, ALU.add)\
                    .then_inc(sg("y_centred"), 1)
            for j in range(4):
                dve.scalar_tensor_tensor(bonus_b[j][:, :], r_(j), pc("r_k", j), k_(j), ALU.mult, ALU.mult)\
                    .then_inc(sg("rk_ready"), 1)
            for j in range(4):
                dve.wait_ge(sg("bonus"), j + 1)
                dve.tensor_tensor(bonus_b[j][:, :], pair_ap(0), v_(j), ALU.mult).then_inc(sg("bonus_read"), 1)
                stats_dve(dve, y_norms[j], ch)
                dve.wait_ge(sg("bonus_read"), j + 1)
                ch(dve.scalar_tensor_tensor(merged(j), merged(j), pc("ln_b", j), bonus_b[j][:, :], ALU.add, ALU.add))
                dve.wait_ge(sg("gate_read"), j + 1)
                dve.tensor_tensor(merged(j), merged(j), gates_b[j][:, :], ALU.mult).then_inc(sg("y_gated"), 1)
            dve.wait_ge(sg("y_gated"), 4)

        block = ctx.enter_context(nc.Block())

        @block.tensor
        def _(pe):
            pe.wait_ge(sg("cond_silu"), 1)
            ada_products(pe, 0, range(KT))
            for n in range(1, ADA_FIRST):
                ada_products(pe, n, range(KT))
                ada_turn(pe, n - 1)
            ada_turn(pe, ADA_FIRST - 1)
            for t in range(KT):
                norm_sum(pe, 0, t)
            mix0_pe(pe)
            leave_phase(pe, PE_)
            att_pe(pe, 0)
            stats_pe(pe, subln_norms)
            leave_phase(pe, PE_)
            up0_pe(pe)
            leave_phase(pe, PE_)
            att_pe(pe, 1)
            leave_phase(pe, PE_)
            wout_pe(pe, 0)
            ffn_pe(pe, 0)
            leave_phase(pe, PE_)
            mix1_pe(pe)
            leave_phase(pe, PE_)
            ssd_prep_pe(pe)
            ssd_pe(pe)
            pe.wait_ge(sg("od_gated"), 1)
            stats_pe(pe, od_norm)
            leave_phase(pe, PE_)
            for j in range(4):
                wkv_prep_pe(pe, j)
                leave_phase(pe, PE_)
                pending = []
                for g in range(3):
                    wkv_solve_pe(pe, j, g, pending)
                    pending = wkv_apply_pe(pe, j, g)
                for piece in pending:
                    piece()
                leave_phase(pe, PE_)
            post_pe(pe)
            leave_phase(pe, PE_)
            wout_pe(pe, 16)
            ffn_pe(pe, 1)

        @block.scalar
        def _(act):
            act.wait_ge(sg("par_loaded"), 16)
            act.activation(small[:, 0:16], pc("cond", 0, 16), ACT.Silu).then_inc(sg("cond_silu"), 1)
            act.wait_ge(sg("eps_ready"), 1)
            act.wait_ge(sg("x_loaded"), 16 * 4)
            for t in range(KT):
                norm_square(act, 0, t)
            norm_act(act, 0, lambda t, c: mod(0, 0, t, c))
            mix0_act(act)
            leave_phase(act, ACT_)
            att_act(act, 0)
            act.wait_ge(sg("att0_out"), 4)
            stats_act(act, subln_norms)
            leave_phase(act, ACT_)
            up0_act(act)
            leave_phase(act, ACT_)
            att_act(act, 1)
            leave_phase(act, ACT_)
            for t in range(KT):
                norm_square(act, 1, t, 0)
                if t == 3:
                    for part in range(WP):
                        w_hi_act(act, 0, 0, part, WP)
            norm_act(act, 1, lambda t, c: mod(0, 3, t, c), split=True)
            ffn_act(act, 0)
            leave_phase(act, ACT_)
            norm_act(act, 2, lambda t, c: mod(1, 0, t, c), split=True, meanwhile=lambda: in_hi(act, 0))
            mix1_act(act)
            leave_phase(act, ACT_)
            ssd_prep_act(act)
            ssd_act(act)
            act.wait_ge(sg("od_gated"), 1)
            stats_act(act, od_norm)
            leave_phase(act, ACT_)
            for j in range(4):
                act.wait_ge(sg("wkv_kx"), j + 1)
                wkv_prep_act(act, j)
                leave_phase(act, ACT_)
                pending = []
                for g in range(3):
                    wkv_solve_act(act, j, g, pending)
                    pending = wkv_apply_act(act, j, g)
                for piece in pending:
                    piece()
                leave_phase(act, ACT_)
            post_act(act)
            leave_phase(act, ACT_)
            for t in range(KT):
                norm_square(act, 3, t, 16)
                if t == 3:
                    for part in range(WP):
                        w_hi_act(act, 1, 0, part, WP)
            norm_act(act, 3, lambda t, c: mod(1, 3, t, c), split=True)
            ffn_act(act, 1)
            norm_act(act, 4, None)

        @block.vector
        def _(dve):
            ch = Chain(dve, "vector_chain")
            for col, val in ((16, EPS), (17, 1e-12), (18, 64e-5), (19, 1.0)):
                ch(dve.memset(small[:, col:col + 1], val))
            dve.memset(ones[:, :], 1.0).then_inc(sg("eps_ready"), 1)
            dve.wait_ge(sg("par_loaded"), 16)
            dve.wait_ge(sg("x_loaded"), 16 * 4)
            ada_take_rows(dve, 0)
            for n in range(1, ADA_FIRST):
                ada_take_rows(dve, n)
                ada_take_cols(dve, n - 1)
            ada_take_cols(dve, ADA_FIRST - 1)
            dve.wait_ge(sg("ada_taken"), ADA_FIRST)
            ada_gain(dve, 0, 0, ch)
            norm_dve(dve, 0, g_eff(0), ch)
            mix0_dve(dve, ch)
            leave_phase(dve, DVE_)
            att_dve(dve, 0, ch)
            stats_dve(dve, subln_norms, ch)
            leave_phase(dve, DVE_)
            up0_dve(dve, ch)
            leave_phase(dve, DVE_)
            att_dve(dve, 1, ch)
            dve.wait_ge(sg("ada_taken"), 24)
            for l, i in ((0, 1), (1, 0), (1, 1)):
                ada_gain(dve, l, i, ch)
            leave_phase(dve, DVE_)
            residual_dve(dve, 0, lambda t, c: mod(0, 2, t, c), ch,
                         between=lambda m: w_lo_dve(dve, 0, 0, m - 4, WP) if m >= 4 else None)
            norm_dve(dve, 1, g_eff(1), ch, shift=lambda t, c: mod(0, 3, t, c), layer=0)
            ffn_dve(dve, 0, ch)
            leave_phase(dve, DVE_)
            norm_dve(dve, 2, g_eff(2), ch, shift=lambda t, c: mod(1, 0, t, c), layer=1, meanwhile=lambda: in_lo(dve, 0))
            mix1_dve(dve, ch)
            leave_phase(dve, DVE_)
            ssd_prep_dve(dve, ch)
            ssd_dve(dve, ch)
            stats_dve(dve, od_norm, ch)
            leave_phase(dve, DVE_)
            for j in range(4):
                if j == 0:
                    ch(dve.memset(merged_b[:, 0:4 * NT], 0.0))
                wkv_prep_dve(dve, j, ch)
                leave_phase(dve, DVE_)
                pending = []
                for g in range(3):
                    wkv_solve_dve(dve, j, g, ch, pending)
                    pending = wkv_apply_dve(dve, j, g, ch)
                for piece in pending:
                    piece()
                leave_phase(dve, DVE_)
            post_dve(dve, ch)
            leave_phase(dve, DVE_)
            residual_dve(dve, 16, lambda t, c: mod(1, 2, t, c), ch,
                         between=lambda m: w_lo_dve(dve, 1, 0, m - 4, WP) if m >= 4 else None)
            norm_dve(dve, 3, g_eff(3), ch, shift=lambda t, c: mod(1, 3, t, c), layer=2)
            ffn_dve(dve, 1, ch)
            norm_dve(dve, 4, lambda t, c: pc("norm_f", t), ch)

        outs = [0]

        @block.gpsimd
        def _(pool):
            con = t_in["const"]
            cs = lambda name, p0=0, p1=P: con[p0:p1, CC[name][0]:CC[name][0] + CC[name][1]]

            def store(dst, src):
                pool.dma_start(dst, src).then_inc(sg("stored"), 16)
                outs[0] += 1
            pool.dma_start(par[:, :], t_in["params"]).then_inc(sg("par_loaded"), 16)
            pool.dma_start(ident[:, :], cs("ident")).then_inc(sg("x_loaded"), 16)
            pool.dma_start(h_b[:, :].rearrange("p (t n) -> p t n", n=NT), t_in["xT"].rearrange("(t p) n -> p t n", p=P))\
                .then_inc(sg("x_loaded"), 16)
            pool.dma_start(blk[:, :], cs("blk")).then_inc(sg("x_loaded"), 16)
            pool.dma_start(cosA, cs("cosA")).then_inc(sg("x_loaded"), 16)
            for dst, src in ((sinA, cs("sinA")), (cosB, cs("cosB")), (sinB, cs("sinB")), (rotA, cs("rotA")), (rotB, cs("rotB")),
                             (wuq[:, 0:384], t_in["l0_w_uq"][0:P, :]), (wuq[0:64, 384:768], t_in["l0_w_uq"][P:QL, :]),
                             (wukv, t_in["l0_w_ukv"]),
                             (v_b[:, 2048:2560].rearrange("p (h d) -> p h d", h=4), t_in["cv"].rearrange("h t d -> t h d")),
                             (ckv_b[:, NL:NT], t_in["cckvT"]), (kpe_b[64:QK, NL:NT], t_in["ckpeT"])):
                pool.dma_start(dst, src).then_inc(sg("m0_loaded"), 16)
            pool.dma_start(k_b[:, :].rearrange("p (h n) -> p h n", h=4)[:, :, NL:NT], t_in["ckT"].rearrange("h d t -> d h t"))\
                .then_inc(sg("m0_loaded"), 16)
            pool.dma_start(rt_b[:, 0:P], cs("ident")).then_inc(sg("m0_loaded"), 16)
            pool.dma_start(rt_b[:, P:2 * P], cs("ident")).then_inc(sg("m0_loaded"), 16)
            leave_phase(pool, POOL_)
            store(t_out["k"].rearrange("h d t -> d h t"), k_b[:, :].rearrange("p (h n) -> p h n", h=4)[:, :, KP0:NK])
            store(t_out["v"], v_b[:, 2560:3072])
            store(t_out["ckv"], ckv_b[:, KP0:NK])
            store(t_out["kpe"], kpe_b[64:QK, KP0:NK])
            pool.wait_ge(sg("stored"), 16 * outs[0])
            leave_phase(pool, POOL_)
            up0_pool(pool)
            leave_phase(pool, POOL_)
            leave_phase(pool, POOL_)
            leave_phase(pool, POOL_)
            for dst, src in ((c_reset, cs("reset")), (c_selh, cs("selh")), (c_selr, cs("selr")), (c_gm, cs("gmask")),
                             (sst, t_in["ssm0"])):
                pool.dma_start(dst, src).then_inc(sg("ssd_loaded"), 16)
            for dst, src in ((w2s, t_in["l1_w2"].rearrange("i r n -> (i r) n")), (a2s, t_in["l1_a2"].rearrange("i r n -> (i r) n")),
                             (g2s, t_in["l1_g2"])):
                pool.dma_start(dst, src).then_inc(sg("lora_loaded"), 16)
            pool.wait_ge(sg("lora_loaded"), 48)
            leave_phase(pool, POOL_)
            leave_phase(pool, POOL_)
            store(t_out["ssm"], sst)
            for dst, src in ((c_ar, cs("armask")), (c_lev, cs("lev")), (s0_b, t_in["wkv0"])):
                pool.dma_start(dst, src).then_inc(sg("wkv_loaded"), 16)
            pool.wait_ge(sg("stored"), 16 * outs[0])
            pool.dma_start(c_reset2, cs("reset")).then_inc(sg("wkv_loaded"), 16)
            for j in range(4):
                leave_phase(pool, POOL_)
                leave_phase(pool, POOL_)
            store(t_out["wkv"], sf_b)
            pool.wait_ge(sg("stored"), 16 * outs[0])
            leave_phase(pool, POOL_)
            for t in range(0, KT, 2):
                pool.wait_ge(sg("norm_scaled"), 4 * KT + t + 2)
                store(t_out["yT"][P * t:P * t + 2 * P, :].rearrange("(t p) n -> p t n", p=P),
                      hn_b[:, NT * t:NT * t + 2 * NT].rearrange("p (t n) -> p t n", n=NT))
            pool.wait_ge(sg("stored"), 16 * outs[0])

        WKV_LEFT = 15
        first_after_wkv = max(n for n, b in enumerate(blocks) if b[0] == "win") + 1

        @block.sync
        def _(sp):
            for n, (_, parts) in enumerate(blocks):
                if n == first_after_wkv:
                    sp.wait_ge(phase, 4 * WKV_LEFT)
                if n >= RING:
                    sp.wait_ge(*released[n - RING])
                for src, kt, c0, width, row in parts:
                    dst = ring[:, (n % RING) * SLOT:(n % RING) * SLOT + kt * row].rearrange("p (k c) -> p k c", k=kt)
                    sp.dma_start(dst[:, :, c0:c0 + width], src).then_inc(full[n % RING], 16)


def pack_columns(v):
    return np.ascontiguousarray(np.asarray(v).reshape(-1, P).T)


def shape_constants():
    at, n = const_columns()
    out = np.zeros((P, n), np.float32)

    def put(name, a):
        c, w = at[name]
        a = np.asarray(a, np.float32)
        out[:a.shape[0], c:c + w] = a.reshape(a.shape[0], w)
    i = np.arange(P)
    put("ident", np.eye(P))
    put("blk", (i[:, None] // 64 == i[None, :] // 64))
    pos = np.arange(NL)
    row, col = (pos // 64).astype(np.float32), (pos % 64).astype(np.float32)

    def tables(dim, reps, offset):
        quarter = dim // 4
        inv = (np.float32(10000.0) ** (-np.arange(quarter, dtype=np.float32) / np.float32(quarter))).astype(np.float32)
        cos, sin = np.zeros((P, NL), np.float32), np.zeros((P, NL), np.float32)
        rot = np.zeros((P, P), np.float32)
        for r in range(reps):
            for part, ps in enumerate((row, col)):
                for m in range(quarter):
                    ang = (ps * inv[m]).astype(np.float32)
                    a = offset + r * dim + part * 2 * quarter + m
                    b = a + quarter
                    cos[a] = cos[b] = np.cos(ang)
                    sin[a], sin[b] = -np.sin(ang), np.sin(ang)
                    rot[b, a] = rot[a, b] = 1.0
        return cos, sin, rot
    for x, args in (("A", (DA, 2, 0)), ("B", (ROPE, 1, NOPE))):
        cos, sin, rot = tables(*args)
        put("cos" + x, cos), put("sin" + x, sin), put("rot" + x, rot)
    s, t = i[:, None], i[None, :]
    put("gmask", np.stack([t >= s, t <= s], 1))
    put("armask", np.stack([np.stack([t > s, t >= s], 1), np.stack([t < s, t <= s], 1)], 1))
    lev = []
    for b in range(7):
        w = 1 << b
        same = (s // (2 * w)) == (t // (2 * w))
        up = same & (s % (2 * w) >= w) & (t % (2 * w) < w)
        fwd, bwd = up, up.T
        lev += [fwd.T, bwd.T] if b == 0 else [fwd, bwd]
    put("lev", np.stack(lev, 1))
    put("reset", np.tile((np.arange(NT) % P != 0)[None], (P, 1)))
    selh, selr = np.zeros((P, 8, P)), np.zeros((P, 4, P))
    for base in (0, 32):
        for hd in range(8):
            selh[base + hd, hd] = 1
            selr[base + hd, hd % 4, 64 * (hd // 4):64 * (hd // 4) + 64] = 1
    put("selh", selh), put("selr", selr)
    return out


def lay_out(inp):
    f = {k: np.asarray(v) for k, v in inp.items()}
    at, n = param_columns()
    par = np.zeros((P, n), np.float32)

    def put(name, cols):
        par[:, at[name]:at[name] + cols.shape[1]] = cols
    put("cond", np.stack([pack_columns(f["c"][0]), pack_columns(f["c_ctx"])], 2).reshape(P, 16))
    for i in range(2):
        for k in ("ada_b", "norm1", "norm2"):
            put(f"{k}{i}", pack_columns(f[f"{k}_{i}"]))
        put(f"ffn_b{i}", pack_columns(f[f"ffn_conv_b_{i}"]))
        put(f"ffn_w{i}", pack_columns(f[f"ffn_conv_w_{i}"]))
    put("norm_f", pack_columns(f["norm_f"]))
    lam = np.zeros((P, 4), np.float32)
    for i, k in enumerate(("lambda_q1", "lambda_k1", "lambda_q2", "lambda_k2")):
        lam[:64, i] = f["l0_" + k]
    put("lam", lam)
    qn = np.zeros((2 * P,), np.float32)
    qn[:QL] = f["l0_q_norm"]
    put("q_norm", pack_columns(qn))
    put("subln", pack_columns(f["l0_subln"]))
    put("kv_norm", pack_columns(f["l0_kv_norm"]))
    for k in ("mu", "w0", "a0", "k_k", "k_a", "r_k", "ln_w", "ln_b", "conv_w", "conv_b", "gnorm"):
        put(k, pack_columns(f["l1_" + k]))
    put("Dskip", pack_columns(np.repeat(f["l1_D"], 64, axis=1)))
    small = np.zeros((P, 2), np.float32)
    for base, d in ((0, 0), (32, 1), (64, 0), (96, 1)):
        small[base:base + 8, 0] = f["l1_dt_bias"][d]
    for base, d in ((0, 0), (32, 1)):
        small[base:base + 8, 1] = f["l1_A_log"][d]
    put("dt_bias", small)
    ssm = np.stack([f["state_l1_ssm_fwd"][0], f["state_l1_ssm_bwd"][0]])
    ssm = ssm.reshape(2, 2, 4, PD, NS).transpose(1, 4, 0, 2, 3).reshape(P, 512)
    wkv = np.stack([f["state_l1_wkv_fwd"][0], f["state_l1_wkv_bwd"][0]])
    wkv = wkv.reshape(2, 4, 2, 64, 64).transpose(2, 4, 1, 0, 3).reshape(P, 512)
    arrays = {
        "params": par, "const": shape_constants(),
        "xT": np.concatenate([f["x_sample"][0], f["x_prompt"][0]], 0).T,
        "cv": f["cache_l0_v"][0], "ckT": f["cache_l0_k"][0].transpose(0, 2, 1),
        "cckvT": f["cache_l0_ckv"][0].T, "ckpeT": f["cache_l0_kpe"][0].T,
        "ssm0": ssm, "wkv0": wkv,
    }
    for k in ("ada_w_0", "ada_w_1", "l0_w_in", "l1_w_in", "l0_w_out", "l1_w_out", "ffn_up_0", "ffn_up_1", "ffn_down_0",
              "ffn_down_1", "l0_w_uq", "l0_w_ukv", "l1_w2", "l1_a2", "l1_g2"):
        arrays[k] = f[k]
    return {k: np.ascontiguousarray(v) for k, v in arrays.items()}


OUTS = {"yT": (D, NT), "k": (HA, P, P), "v": (P, 512), "ckv": (P, P), "kpe": (ROPE, P), "ssm": (P, 512), "wkv": (P, 512)}


def kernel(**inputs):
    import concourse.bacc as bacc
    from concourse.bass_utils import run_bass_kernel_spmd
    nc = bacc.Bacc("TRN2", target_bir_lowering=False, num_devices=1)
    arrays = lay_out(inputs)
    t_in = {k: nc.dram_tensor("in_" + k, v.shape, mybir.dt.from_np(v.dtype), kind="ExternalInput").ap()
            for k, v in arrays.items()}
    t_out = {k: nc.dram_tensor("out_" + k, s, F32, kind="ExternalOutput").ap() for k, s in OUTS.items()}
    build(nc, t_in, t_out)
    run = run_bass_kernel_spmd(nc, [{"in_" + k: v for k, v in arrays.items()}], core_ids=[0])
    o = {k: np.asarray(run.results[0]["out_" + k]) for k in OUTS}
    y = o["yT"].T
    new_k = o["k"].transpose(0, 2, 1)[None]
    new_v = o["v"].reshape(P, HA, P).transpose(1, 0, 2)[None]
    ssm = o["ssm"].reshape(2, NS, 2, 4, PD).transpose(2, 0, 3, 4, 1).reshape(2, 1, HD, PD, NS)
    wkv = o["wkv"].reshape(2, 64, 4, 2, 64).transpose(3, 2, 0, 4, 1).reshape(2, 1, HC, 64, 64)
    return tuple(np.ascontiguousarray(a) for a in (
        y[None, NL:], y[None, :NL], new_k, new_v, o["ckv"].T[None], o["kpe"].T[None], wkv[0], wkv[1], ssm[0], ssm[1]))
```
